# Optimizing a Trainium2 kernel written in Bass

```python
import math
import jax
import jax.numpy as jnp
from jax import lax
import numpy as np
import jax, jax.numpy as jnp

D_MODEL = 1024
BATCH = 1
SEQ = 512
DEPTH = 2

CHUNK = 64
GDN_HEADS = 8
GDN_DK = 128
GDN_DV = 128
GDN_CONV = 4
GDN_QK = GDN_HEADS * GDN_DK
GDN_V = GDN_HEADS * GDN_DV
GDN_IN = 2 * GDN_QK + 2 * GDN_V + 2 * GDN_HEADS
GDN_DT_MIN = 1e-3
GDN_DT_MAX = 1e-1
S5_GROUP = 16
S5_GROUPS = D_MODEL // S5_GROUP
S5_STATE = 64
S5_DT_MIN = 1e-3
S5_DT_MAX = 1e-1
D_FF = 11 * D_MODEL // 4
N_EXPERTS = 8
TOP_K = 2
D_FF_EXPERT = D_FF // 2
N_EVEN = (DEPTH + 1) // 2
N_ODD = DEPTH // 2
ALPHA = (2 * DEPTH) ** 0.25
BETA_INIT = (8 * DEPTH) ** -0.25
LN_EPS = 1e-5
NORM_EPS = 1e-6


def layer_norm(x, g, b):
    xf = x.astype(jnp.float32)
    mu = jnp.mean(xf, -1, keepdims=True)
    var = jnp.mean(jnp.square(xf - mu), -1, keepdims=True)
    y = (xf - mu) * lax.rsqrt(var + LN_EPS) * g.astype(jnp.float32) + b.astype(jnp.float32)
    return y.astype(x.dtype)

def l2norm(t):
    return t * lax.rsqrt(jnp.sum(t * t, -1, keepdims=True) + NORM_EPS)

def causal_dwconv(x, w):
    k = w.shape[0]
    return lax.conv_general_dilated(x, w[:, None, :].astype(x.dtype), window_strides=(1,),
                                    padding=[(k - 1, 0)], dimension_numbers=('NWC', 'WIO', 'NWC'),
                                    feature_group_count=x.shape[-1])

def gated_delta_rule_chunked(q, k, v, g, beta):
    bsz, seq, nh, dk = q.shape
    dv = v.shape[-1]
    n = seq // CHUNK

    def to_chunks(t):
        t = t.reshape((bsz, n, CHUNK) + t.shape[2:])
        return jnp.moveaxis(t, 3, 1)

    q, k, v, g, beta = (to_chunks(t) for t in (q, k, v, g, beta))
    g = jnp.cumsum(g, axis=-1)
    idx = jnp.arange(CHUNK)
    causal = idx[:, None] >= idx[None, :]
    strict = idx[:, None] > idx[None, :]
    decay = jnp.exp(jnp.where(causal, g[..., :, None] - g[..., None, :], -jnp.inf))
    k_beta = k * beta[..., None]
    v_beta = v * beta[..., None]
    lmat = jnp.where(strict, jnp.einsum('bhncd,bhnsd->bhncs', k_beta, k) * decay, 0.0)
    eye = jnp.eye(CHUNK, dtype=jnp.float32)
    t_inv = lax.linalg.triangular_solve(eye + lmat, jnp.broadcast_to(eye, lmat.shape),
                                        left_side=True, lower=True, unit_diagonal=True)
    u = jnp.einsum('bhncs,bhnsd->bhncd', t_inv, v_beta)
    w = jnp.einsum('bhncs,bhnsd->bhncd', t_inv, k_beta * jnp.exp(g)[..., None])
    a_intra = jnp.einsum('bhncd,bhnsd->bhncs', q, k) * decay

    def step(state, inp):
        q_c, k_c, u_c, w_c, g_c, a_c = inp
        v_new = u_c - jnp.einsum('bhcd,bhde->bhce', w_c, state)
        o = (jnp.einsum('bhcd,bhde->bhce', q_c * jnp.exp(g_c)[..., None], state)
             + jnp.einsum('bhcs,bhse->bhce', a_c, v_new))
        g_last = g_c[..., -1]
        state = (state * jnp.exp(g_last)[..., None, None]
                 + jnp.einsum('bhcd,bhce->bhde', k_c * jnp.exp(g_last[..., None] - g_c)[..., None], v_new))
        return state, o

    xs = tuple(jnp.moveaxis(t, 2, 0) for t in (q, k, u, w, g, a_intra))
    s0 = jnp.zeros((bsz, nh, dk, dv), jnp.float32)
    _, o = lax.scan(step, s0, xs)
    o = jnp.moveaxis(jnp.moveaxis(o, 0, 2), 1, 3)
    return o.reshape(bsz, seq, nh, dv)

def gdn_mixer(x, w_in, conv_w, a_log, dt_bias, norm_g, w_out):
    bsz, seq, _ = x.shape
    f32 = jnp.float32
    proj = x @ w_in
    qkv, z, b, a = jnp.split(proj, [2 * GDN_QK + GDN_V, 2 * GDN_QK + 2 * GDN_V,
                                    2 * GDN_QK + 2 * GDN_V + GDN_HEADS], axis=-1)
    qkv = jax.nn.silu(causal_dwconv(qkv, conv_w)).astype(f32)
    q, k, v = jnp.split(qkv, [GDN_QK, 2 * GDN_QK], axis=-1)
    q = l2norm(q.reshape(bsz, seq, GDN_HEADS, GDN_DK)) * (GDN_DK ** -0.5)
    k = l2norm(k.reshape(bsz, seq, GDN_HEADS, GDN_DK))
    v = v.reshape(bsz, seq, GDN_HEADS, GDN_DV)
    beta = jax.nn.sigmoid(b.astype(f32))
    g = -jnp.exp(a_log.astype(f32)) * jax.nn.softplus(a.astype(f32) + dt_bias.astype(f32))
    o = gated_delta_rule_chunked(q, k, v, g, beta)
    o = o * lax.rsqrt(jnp.mean(o * o, -1, keepdims=True) + NORM_EPS) * norm_g.astype(f32)
    o = o * jax.nn.silu(z.reshape(bsz, seq, GDN_HEADS, GDN_DV).astype(f32))
    return o.reshape(bsz, seq, GDN_V).astype(x.dtype) @ w_out

def s5_mixer(x, w_in, lam_re, lam_im, log_dt, b_re, b_im, c_re, c_im, d_skip, w_glu):
    bsz, seq, _ = x.shape
    f32 = jnp.float32
    n = seq // CHUNK
    u = (x @ w_in).astype(f32)
    lam = lax.complex(lam_re.astype(f32), lam_im.astype(f32))
    dt = jnp.exp(log_dt.astype(f32))[:, None]
    a_bar = jnp.exp(lam * dt)
    b_bar = ((a_bar - 1.0) / lam)[..., None] * lax.complex(b_re.astype(f32), b_im.astype(f32))
    c = lax.complex(c_re.astype(f32), c_im.astype(f32))
    steps = jnp.arange(1, CHUNK + 1, dtype=f32)[:, None, None]
    a_pow = jnp.exp((lam * dt)[None] * steps)

    def binop(e1, e2):
        a1, b1 = e1
        a2, b2 = e2
        return a2 * a1, a2 * b1 + b2

    def step(h, u_c):
        bu = jnp.einsum('gpc,btgc->btgp', b_bar, u_c.astype(jnp.complex64))
        _, hs = lax.associative_scan(binop, (jnp.broadcast_to(a_bar, bu.shape), bu), axis=1)
        hs = hs + a_pow[None] * h[:, None]
        y = jnp.einsum('gcp,btgp->btgc', c, hs).real
        return hs[:, -1], y

    uc = jnp.moveaxis(u.reshape(bsz, n, CHUNK, S5_GROUPS, S5_GROUP), 1, 0)
    h0 = jnp.zeros((bsz, S5_GROUPS, S5_STATE), jnp.complex64)
    _, ys = lax.scan(step, h0, uc)
    y = jnp.moveaxis(ys, 0, 1).reshape(bsz, seq, D_MODEL) + d_skip.astype(f32) * u
    hid = jax.nn.gelu(y.astype(x.dtype), approximate=False)
    val, gate = jnp.split(hid @ w_glu, 2, axis=-1)
    return val * jax.nn.sigmoid(gate)

def swiglu(x, w1, w3, w2):
    return (jax.nn.silu(x @ w1) * (x @ w3)) @ w2

def moe_swiglu(x, w_router, b_router, w1, w3, w2):
    bsz, seq, d = x.shape
    xt = x.reshape(-1, d)
    logits = (xt @ w_router).astype(jnp.float32) + b_router.astype(jnp.float32)
    top_v, top_i = lax.top_k(logits, TOP_K)
    gates = jax.nn.softmax(top_v, axis=-1)
    dense_gate = jnp.sum(jax.nn.one_hot(top_i, N_EXPERTS, dtype=jnp.float32) * gates[..., None], axis=1)
    y = jnp.zeros_like(xt)
    for e in range(N_EXPERTS):
        y = y + dense_gate[:, e:e + 1].astype(x.dtype) * swiglu(xt, w1[e], w3[e], w2[e])
    return y.reshape(bsz, seq, d)

def first_inputs(seed: int = 0) -> dict:
    key = jax.random.key(seed)
    ks = jax.random.split(key, 27)
    f32 = jnp.float32

    def nrm(i, shape, scale):
        return jax.random.normal(ks[i], shape, f32) * scale

    x = nrm(0, (BATCH, SEQ, D_MODEL), 1.0)
    gdn_w_in = nrm(1, (N_EVEN, D_MODEL, GDN_IN), D_MODEL ** -0.5)
    gdn_conv_w = nrm(2, (N_EVEN, GDN_CONV, 2 * GDN_QK + GDN_V), GDN_CONV ** -0.5)
    gdn_a_log = jnp.log(jax.random.uniform(ks[3], (N_EVEN, GDN_HEADS), f32, 1.0, 16.0))
    dt = jnp.exp(jax.random.uniform(ks[4], (N_EVEN, GDN_HEADS), f32, math.log(GDN_DT_MIN), math.log(GDN_DT_MAX)))
    gdn_dt_bias = dt + jnp.log(-jnp.expm1(-dt))
    gdn_norm_g = 1.0 + nrm(5, (N_EVEN, GDN_DV), 0.02)
    gdn_w_out = nrm(6, (N_EVEN, GDN_V, D_MODEL), GDN_V ** -0.5 * BETA_INIT)
    ffn_w1 = nrm(7, (N_EVEN, D_MODEL, D_FF), D_MODEL ** -0.5)
    ffn_w3 = nrm(8, (N_EVEN, D_MODEL, D_FF), D_MODEL ** -0.5)
    ffn_w2 = nrm(9, (N_EVEN, D_FF, D_MODEL), D_FF ** -0.5 * BETA_INIT)
    s5_w_in = nrm(10, (N_ODD, D_MODEL, D_MODEL), D_MODEL ** -0.5)
    s5_lam_re = -0.5 + nrm(11, (N_ODD, S5_GROUPS, S5_STATE), 0.01)
    s5_lam_im = math.pi * jnp.arange(S5_STATE, dtype=f32) + nrm(12, (N_ODD, S5_GROUPS, S5_STATE), 0.01)
    s5_log_dt = jax.random.uniform(ks[13], (N_ODD, S5_GROUPS), f32, math.log(S5_DT_MIN), math.log(S5_DT_MAX))
    s5_b_re = nrm(14, (N_ODD, S5_GROUPS, S5_STATE, S5_GROUP), (2 * S5_GROUP) ** -0.5)
    s5_b_im = nrm(15, (N_ODD, S5_GROUPS, S5_STATE, S5_GROUP), (2 * S5_GROUP) ** -0.5)
    s5_c_re = nrm(16, (N_ODD, S5_GROUPS, S5_GROUP, S5_STATE), S5_STATE ** -0.5)
    s5_c_im = nrm(17, (N_ODD, S5_GROUPS, S5_GROUP, S5_STATE), S5_STATE ** -0.5)
    s5_d = nrm(18, (N_ODD, D_MODEL), 1.0)
    s5_w_glu = nrm(19, (N_ODD, D_MODEL, 2 * D_MODEL), D_MODEL ** -0.5 * BETA_INIT)
    moe_w_router = nrm(20, (N_ODD, D_MODEL, N_EXPERTS), D_MODEL ** -0.5)
    moe_b_router = nrm(21, (N_ODD, N_EXPERTS), 0.01)
    moe_w1 = nrm(22, (N_ODD, N_EXPERTS, D_MODEL, D_FF_EXPERT), D_MODEL ** -0.5)
    moe_w3 = nrm(23, (N_ODD, N_EXPERTS, D_MODEL, D_FF_EXPERT), D_MODEL ** -0.5)
    moe_w2 = nrm(24, (N_ODD, N_EXPERTS, D_FF_EXPERT, D_MODEL), D_FF_EXPERT ** -0.5 * BETA_INIT)
    ln_g = 1.0 + nrm(25, (DEPTH, 2, D_MODEL), 0.02)
    ln_b = nrm(26, (DEPTH, 2, D_MODEL), 0.02)
    return {'x': x, 'gdn_w_in': gdn_w_in, 'gdn_conv_w': gdn_conv_w, 'gdn_a_log': gdn_a_log,
            'gdn_dt_bias': gdn_dt_bias, 'gdn_norm_g': gdn_norm_g, 'gdn_w_out': gdn_w_out,
            'ffn_w1': ffn_w1, 'ffn_w3': ffn_w3, 'ffn_w2': ffn_w2,
            's5_w_in': s5_w_in, 's5_lam_re': s5_lam_re, 's5_lam_im': s5_lam_im, 's5_log_dt': s5_log_dt,
            's5_b_re': s5_b_re, 's5_b_im': s5_b_im, 's5_c_re': s5_c_re, 's5_c_im': s5_c_im,
            's5_d': s5_d, 's5_w_glu': s5_w_glu,
            'moe_w_router': moe_w_router, 'moe_b_router': moe_b_router,
            'moe_w1': moe_w1, 'moe_w3': moe_w3, 'moe_w2': moe_w2,
            'ln_g': ln_g, 'ln_b': ln_b}

def first_block(x, gdn_w_in, gdn_conv_w, gdn_a_log, gdn_dt_bias, gdn_norm_g, gdn_w_out,
              ffn_w1, ffn_w3, ffn_w2,
              s5_w_in, s5_lam_re, s5_lam_im, s5_log_dt, s5_b_re, s5_b_im, s5_c_re, s5_c_im,
              s5_d, s5_w_glu,
              moe_w_router, moe_b_router, moe_w1, moe_w3, moe_w2,
              ln_g, ln_b):
    for i in range(DEPTH):
        j = i // 2
        if i % 2 == 0:
            h = gdn_mixer(x, gdn_w_in[j], gdn_conv_w[j], gdn_a_log[j], gdn_dt_bias[j],
                          gdn_norm_g[j], gdn_w_out[j])
        else:
            h = s5_mixer(x, s5_w_in[j], s5_lam_re[j], s5_lam_im[j], s5_log_dt[j], s5_b_re[j],
                         s5_b_im[j], s5_c_re[j], s5_c_im[j], s5_d[j], s5_w_glu[j])
        x = layer_norm(ALPHA * x + h, ln_g[i, 0], ln_b[i, 0])
        if i % 2 == 0:
            f = swiglu(x, ffn_w1[j], ffn_w3[j], ffn_w2[j])
        else:
            f = moe_swiglu(x, moe_w_router[j], moe_b_router[j], moe_w1[j], moe_w3[j], moe_w2[j])
        x = layer_norm(ALPHA * x + f, ln_g[i, 1], ln_b[i, 1])
    return x


HEAD_DIM = 64
A_HEADS = 6
A_NOPE = 64
A_ROPE = 32
A_V = 64
Q_LORA = 768
KV_LORA = 256
ROPE_THETA = 10000.0
B_HEADS = 6
DILATED_PATTERNS = ((128, 1), (512, 4), (2048, 16))
C_HEADS = 4
IDX_HEADS = 8
IDX_DIM = 64
TOPK_MAX = 256
Q_BLOCK = 128

A_WIDTH = A_HEADS * A_V
B_WIDTH = B_HEADS * HEAD_DIM
C_WIDTH = C_HEADS * HEAD_DIM
MIX_WIDTH = A_WIDTH + B_WIDTH + C_WIDTH
N_ALIBI = B_HEADS + C_HEADS

SPLIT_SIZES = (Q_LORA, KV_LORA, A_ROPE,
               B_WIDTH, B_WIDTH, B_WIDTH,
               C_WIDTH, C_WIDTH, C_WIDTH,
               IDX_HEADS * IDX_DIM, IDX_DIM, IDX_HEADS,
               MIX_WIDTH)
IN_WIDTH = sum(SPLIT_SIZES)
SPLIT_POINTS = [int(v) for v in np.cumsum(SPLIT_SIZES)[:-1]]

ALPHA_2 = (2 * DEPTH) ** 0.25
BETA = (8 * DEPTH) ** -0.25


F32 = jnp.float32

def layer_norm_2(x, g, b, eps=1e-5):
    xf = x.astype(F32)
    mu = jnp.mean(xf, axis=-1, keepdims=True)
    xc = xf - mu
    var = jnp.mean(xc * xc, axis=-1, keepdims=True)
    return (xc * lax.rsqrt(var + eps) * g.astype(F32) + b.astype(F32)).astype(x.dtype)

def rms_norm(x, g, eps=1e-6):
    xf = x.astype(F32)
    ms = jnp.mean(xf * xf, axis=-1, keepdims=True)
    return (xf * lax.rsqrt(ms + eps) * g.astype(F32)).astype(x.dtype)

def apply_rope(x, cos, sin):
    half = x.shape[-1] // 2
    x1, x2 = x[..., :half].astype(F32), x[..., half:].astype(F32)
    return jnp.concatenate([x1 * cos - x2 * sin, x1 * sin + x2 * cos], axis=-1).astype(x.dtype)

def alibi_slopes():
    return 2.0 ** (-8.0 * jnp.arange(1, N_ALIBI + 1, dtype=F32) / N_ALIBI)

def to_blocks(a):
    b, s = a.shape[0], a.shape[1]
    return a.reshape((b, s // Q_BLOCK, Q_BLOCK) + a.shape[2:]).swapaxes(0, 1)

def from_blocks(a):
    a = a.swapaxes(0, 1)
    return a.reshape((a.shape[0], a.shape[1] * a.shape[2]) + a.shape[3:])

def mla_attention(q_nope, q_rope, k_nope, k_rope, v):
    s_len = q_nope.shape[1]
    nb = s_len // Q_BLOCK
    scale = (A_NOPE + A_ROPE) ** -0.5
    key_pos = jnp.arange(s_len)

    def block(args):
        qn, qr, start = args
        qpos = start + jnp.arange(Q_BLOCK)
        s = (jnp.einsum('bqhd,bshd->bhqs', qn, k_nope, preferred_element_type=F32)
             + jnp.einsum('bqhr,bsr->bhqs', qr, k_rope, preferred_element_type=F32)) * scale
        s = jnp.where(key_pos[None, :] <= qpos[:, None], s, -jnp.inf)
        p = jax.nn.softmax(s, axis=-1)
        return jnp.einsum('bhqs,bshd->bqhd', p.astype(v.dtype), v)

    out = lax.map(block, (to_blocks(q_nope), to_blocks(q_rope), jnp.arange(nb) * Q_BLOCK))
    return from_blocks(out)

def dilated_attention(q, k, v, slopes):
    bsz, s_len, nh, dh = q.shape
    outs, lses = [], []
    for window, dil in DILATED_PATTERNS:
        n = window // dil
        L = s_len // dil
        nb = -(-L // n)
        Lp = nb * n

        def gather(a):
            a = a.reshape(bsz, L, dil, nh, dh).swapaxes(1, 2)
            a = jnp.pad(a, ((0, 0), (0, 0), (0, Lp - L), (0, 0), (0, 0)))
            return a.reshape(bsz, dil, nb, n, nh, dh)

        def band(a):
            prev = jnp.pad(a, ((0, 0), (0, 0), (1, 0), (0, 0), (0, 0), (0, 0)))[:, :, :-1]
            return jnp.concatenate([prev, a], axis=3)

        qb = gather(q)
        kb = band(gather(k))
        vb = band(gather(v))
        s = jnp.einsum('brnqhd,brnkhd->brnhqk', qb, kb, preferred_element_type=F32) * dh ** -0.5
        kj = jnp.arange(2 * n)
        step = jnp.arange(n)[:, None] + n - kj[None, :]
        valid = ((step >= 0) & (step <= n))[None] & ((jnp.arange(nb)[:, None, None] > 0) | (kj >= n)[None, None, :])
        s = s - slopes[:, None, None] * (step * dil).astype(F32)
        s = jnp.where(valid[:, None], s, -jnp.inf)
        m = jnp.max(s, axis=-1, keepdims=True)
        p = jnp.exp(s - m)
        den = jnp.sum(p, axis=-1, keepdims=True)
        o = jnp.einsum('brnhqk,brnkhd->brnqhd', (p / den).astype(v.dtype), vb)
        lse = (m + jnp.log(den))[..., 0].swapaxes(-1, -2)

        def ungather(a):
            tr = a.shape[4:]
            a = a.reshape((bsz, dil, Lp) + tr)[:, :, :L]
            return a.swapaxes(1, 2).reshape((bsz, s_len) + tr)

        outs.append(ungather(o))
        lses.append(ungather(lse))
    w = jax.nn.softmax(jnp.stack(lses, axis=0), axis=0)
    out = jnp.sum(w[..., None] * jnp.stack(outs, axis=0).astype(F32), axis=0)
    return out.astype(q.dtype)

def sparse_attention(q, k, v, q_idx, k_idx, w_idx, slopes):
    s_len, dh = q.shape[1], q.shape[3]
    topk = min(TOPK_MAX, s_len // 4)
    nb = s_len // Q_BLOCK
    key_pos = jnp.arange(s_len)
    take = jax.vmap(lambda a, i: a[i])

    def block(args):
        qb, qib, wb, start = args
        qpos = start + jnp.arange(Q_BLOCK)
        logits = jnp.einsum('bqhd,bsd->bqhs', qib, k_idx, preferred_element_type=F32) * IDX_DIM ** -0.5
        score = jnp.einsum('bqh,bqhs->bqs', wb.astype(F32) * IDX_HEADS ** -0.5, jax.nn.relu(logits))
        score = jnp.where(key_pos[None, None, :] <= qpos[None, :, None], score, -jnp.inf)
        _, idx = lax.top_k(score, topk)
        valid = idx <= qpos[None, :, None]
        kg = take(k, idx)
        vg = take(v, idx)
        s = jnp.einsum('bqhd,bqkhd->bhqk', qb, kg, preferred_element_type=F32) * dh ** -0.5
        dist = (qpos[None, :, None] - idx).astype(F32)
        s = s - slopes[None, :, None, None] * dist[:, None]
        s = jnp.where(valid[:, None], s, -jnp.inf)
        p = jax.nn.softmax(s, axis=-1)
        return jnp.einsum('bhqk,bqkhd->bqhd', p.astype(v.dtype), vg)

    out = lax.map(block, (to_blocks(q), to_blocks(q_idx), to_blocks(w_idx), jnp.arange(nb) * Q_BLOCK))
    return from_blocks(out)

def second_inputs(seed: int = 0) -> dict:
    key = jax.random.key(seed)
    ks = jax.random.split(key, 14)
    nrm = jax.random.normal
    return {
        "x": nrm(ks[0], (BATCH, SEQ, D_MODEL), F32),
        "c": nrm(ks[1], (BATCH, D_MODEL), F32),
        "w_ada": nrm(ks[2], (DEPTH, D_MODEL, 3 * D_MODEL), F32) * (0.1 * D_MODEL ** -0.5),
        "b_ada": nrm(ks[3], (DEPTH, 3 * D_MODEL), F32) * 0.02,
        "w_in": nrm(ks[4], (DEPTH, D_MODEL, IN_WIDTH), F32) * D_MODEL ** -0.5,
        "q_norm_g": 1.0 + 0.02 * nrm(ks[5], (DEPTH, Q_LORA), F32),
        "kv_norm_g": 1.0 + 0.02 * nrm(ks[6], (DEPTH, KV_LORA), F32),
        "w_uq": nrm(ks[7], (DEPTH, Q_LORA, A_HEADS * (A_NOPE + A_ROPE)), F32) * Q_LORA ** -0.5,
        "w_uk": nrm(ks[8], (DEPTH, KV_LORA, A_HEADS * A_NOPE), F32) * KV_LORA ** -0.5,
        "w_uv": nrm(ks[9], (DEPTH, KV_LORA, A_HEADS * A_V), F32) * KV_LORA ** -0.5,
        "w_out": nrm(ks[10], (DEPTH, MIX_WIDTH, D_MODEL), F32) * (BETA * MIX_WIDTH ** -0.5),
        "ln_g": 1.0 + 0.02 * nrm(ks[11], (DEPTH, D_MODEL), F32),
        "ln_b": 0.02 * nrm(ks[12], (DEPTH, D_MODEL), F32),
    }

def second_block(x, c, w_ada, b_ada, w_in, q_norm_g, kv_norm_g, w_uq, w_uk, w_uv, w_out, ln_g, ln_b):
    bsz, s_len, _ = x.shape
    slopes = alibi_slopes()
    slopes_b, slopes_c = slopes[:B_HEADS], slopes[B_HEADS:]
    pos = jnp.arange(s_len, dtype=F32)
    freqs = ROPE_THETA ** (-jnp.arange(0, A_ROPE, 2, dtype=F32) / A_ROPE)
    ang = pos[:, None] * freqs[None, :]
    cos, sin = jnp.cos(ang), jnp.sin(ang)

    def heads(a, n):
        return a.reshape(bsz, s_len, n, -1)

    for l in range(DEPTH):
        mod = jax.nn.silu(c) @ w_ada[l] + b_ada[l]
        shift, scale, gate = jnp.split(mod, 3, axis=-1)
        h = x * (1.0 + scale[:, None, :]) + shift[:, None, :]
        (p_cq, p_ckv, p_kr, p_qb, p_kb, p_vb, p_qc, p_kc, p_vc,
         p_qi, p_ki, p_wi, p_gate) = jnp.split(h @ w_in[l], SPLIT_POINTS, axis=-1)

        cq = rms_norm(p_cq, q_norm_g[l])
        ckv = rms_norm(p_ckv, kv_norm_g[l])
        qa = heads(cq @ w_uq[l], A_HEADS)
        qa_nope = qa[..., :A_NOPE]
        qa_rope = apply_rope(qa[..., A_NOPE:], cos[:, None, :], sin[:, None, :])
        ka_nope = heads(ckv @ w_uk[l], A_HEADS)
        va = heads(ckv @ w_uv[l], A_HEADS)
        ka_rope = apply_rope(p_kr, cos, sin)
        o_a = mla_attention(qa_nope, qa_rope, ka_nope, ka_rope, va)

        o_b = dilated_attention(heads(p_qb, B_HEADS), heads(p_kb, B_HEADS), heads(p_vb, B_HEADS), slopes_b)

        o_c = sparse_attention(heads(p_qc, C_HEADS), heads(p_kc, C_HEADS), heads(p_vc, C_HEADS),
                               heads(p_qi, IDX_HEADS), p_ki, p_wi, slopes_c)

        y = jnp.concatenate([o_a.reshape(bsz, s_len, A_WIDTH),
                             o_b.reshape(bsz, s_len, B_WIDTH),
                             o_c.reshape(bsz, s_len, C_WIDTH)], axis=-1) * jax.nn.silu(p_gate)
        sub = y @ w_out[l]
        x = layer_norm_2(ALPHA_2 * x + (1.0 + gate[:, None, :]) * sub, ln_g[l], ln_b[l])
    return x


def setup_inputs(seed=0):
    out = dict(first_inputs(seed))
    for name, value in second_inputs(seed + 1).items():
        if name != "x":
            out[name + "_2"] = value
    return out


def reference(
    x, gdn_w_in, gdn_conv_w, gdn_a_log, gdn_dt_bias, gdn_norm_g, gdn_w_out, ffn_w1, ffn_w3,
    ffn_w2, s5_w_in, s5_lam_re, s5_lam_im, s5_log_dt, s5_b_re, s5_b_im, s5_c_re, s5_c_im, s5_d,
    s5_w_glu, moe_w_router, moe_b_router, moe_w1, moe_w3, moe_w2, ln_g, ln_b, c_2, w_ada_2,
    b_ada_2, w_in_2, q_norm_g_2, kv_norm_g_2, w_uq_2, w_uk_2, w_uv_2, w_out_2, ln_g_2, ln_b_2,
):
    x = first_block(
        x, gdn_w_in, gdn_conv_w, gdn_a_log, gdn_dt_bias, gdn_norm_g, gdn_w_out, ffn_w1, ffn_w3,
        ffn_w2, s5_w_in, s5_lam_re, s5_lam_im, s5_log_dt, s5_b_re, s5_b_im, s5_c_re, s5_c_im,
        s5_d, s5_w_glu, moe_w_router, moe_b_router, moe_w1, moe_w3, moe_w2, ln_g, ln_b,
    )
    return second_block(
        x, c_2, w_ada_2, b_ada_2, w_in_2, q_norm_g_2, kv_norm_g_2, w_uq_2, w_uk_2, w_uv_2,
        w_out_2, ln_g_2, ln_b_2,
    )


_drawn_inputs = setup_inputs


def setup_inputs(seed=0):
    import zlib

    import numpy as np

    out = dict(_drawn_inputs(seed))
    spreads = {}
    factors = {'gdn_norm_g': 6.693,
     's5_lam_re': 8.0,
     's5_lam_im': 3.652,
     's5_log_dt': 3.563,
     's5_b_re': 4.418,
     's5_b_im': 4.339,
     's5_c_re': 4.316,
     's5_c_im': 4.614,
     'moe_b_router': 8.0,
     'b_ada_2': 6.07,
     'q_norm_g_2': 8.0,
     'kv_norm_g_2': 8.0,
     'w_uk_2': 2.756}
    for name, (base, spread) in spreads.items():
        noise = np.random.default_rng([zlib.crc32(name.encode()), seed]).standard_normal(out[name].shape)
        drawn = base * np.exp(spread * noise) if base else spread * noise
        out[name] = jnp.asarray(drawn.astype(out[name].dtype))
    for name, factor in factors.items():
        out[name] = (out[name] * factor).astype(out[name].dtype)
    return out
```

```python
from contextlib import ExitStack

import numpy as np

import concourse.bass as bass
from concourse import mybir

F32 = mybir.dt.float32
ALU = mybir.AluOpType
ACT = mybir.ActivationFunctionType
AX_X = mybir.AxisListType.X

P = 128
D = 1024
KD = D // P
S = 512
NT = S // P
BANK = 512
DEPTH = 2
ALPHA = (2 * DEPTH) ** 0.25
LN_EPS = 1e-5
NORM_EPS = 1e-6

HEADS = 8
CH = 128
NCH = S // CH
LEVELS = 7
HG = 4

FF_PART = 1408
FT = FF_PART // P
EXPERTS = 8

RING = 4
RING_COLS = 2048
UP_COLS = 256


class Weights:

    def __init__(self, ring, loaded, used):
        self.ring, self.loaded, self.used = ring, loaded, used
        self.tiles, self.first, self.size = [], {}, {}
        self.n_loads = [0] * RING
        self.released, self.n_released, self.issued, self.passed = {}, 0, 0, 0

    def plan(self, stage, sources, align=False):
        while align and len(self.tiles) % RING:
            self.tiles.append(None)
        self.first[stage], self.size[stage] = len(self.tiles), len(sources)
        for src in sources:
            slot = len(self.tiles) % RING
            self.n_loads[slot] += 1
            self.tiles.append((src, slot, 16 * self.n_loads[slot]))

    def view(self, index):
        src, slot, _ = self.tiles[index]
        k, n = src.shape[1], src.shape[2]
        return self.ring[:, slot, 0:k * n].rearrange("p (k n) -> p k n", n=n)

    def take(self, pe, stage, i):
        index = self.first[stage] + i
        _, slot, ready = self.tiles[index]
        pe.wait_ge(self.loaded[slot], ready)
        return self.view(index)

    def leave(self, matmul, stage, i):
        matmul.then_inc(self.used, 1)
        self.n_released += 1
        self.released[self.first[stage] + i] = self.n_released

    def load(self, sp, index):
        src, slot, _ = self.tiles[index]
        sp.dma_start(self.view(index), src).then_inc(self.loaded[slot], 16)

    def fill(self, sp, stage):
        while self.issued < len(self.tiles):
            n, old = self.issued, self.issued - RING
            if self.tiles[n] is not None:
                if old >= self.passed and self.tiles[old] is not None:
                    if old not in self.released:
                        break
                    sp.wait_ge(self.used, self.released[old])
                self.load(sp, n)
            self.issued += 1
        if stage in self.first:
            self.passed = self.first[stage] + self.size[stage]


class Program:

    def __init__(self, nc, ctx):
        self.nc, self.ctx = nc, ctx
        self.sets = [[ctx.enter_context(nc.semaphore(f"{w}_{i}")) for i in range(44)] for w in ("even", "odd")]
        self.turn, self.dirty = 0, []

    def sbuf(self, name, shape, ctx=None):
        return (ctx or self.ctx).enter_context(self.nc.sbuf_tensor(name, shape, F32))


class Stage:

    def __init__(self, prog, name):
        self.prog, self.name = prog, name
        self.loads, self.after = None, None

    def __enter__(self):
        self.block_ctx = self.prog.nc.Block()
        self.block = self.block_ctx.__enter__()
        self.free = list(self.prog.sets[self.prog.turn])
        self.taken = []
        self.tensor, self.vector = self.block.tensor, self.block.vector
        self.scalar, self.gpsimd = self.block.scalar, self.block.gpsimd
        return self

    def counter(self, name):
        self.taken.append(self.free.pop(0))
        return self.taken[-1]

    def sync(self, f):
        self.loads = f
        return f

    def __exit__(self, *exc):
        if exc[0] is not None:
            return False

        @self.block.sync
        def _(sp):
            for s in self.prog.dirty:
                sp.sem_clear(s)
            if self.loads:
                self.loads(sp)
            self.prog.weights.fill(sp, self.name)
        self.block_ctx.__exit__(None, None, None)
        self.prog.dirty, self.prog.turn = self.taken, 1 - self.prog.turn
        return False


def linker(eng, sem):
    count = [0]

    def link(ins):
        count[0] += 1
        ins.then_inc(sem, 1)
        eng.wait_ge(sem, count[0])
    return link


def bc(ap, shape):
    return ap.to_broadcast(shape)


def col_tiles(w, width):
    n = w.shape[1]
    return [w[:, c:min(c + width, n)].rearrange("(k p) n -> p k n", p=P) for c in range(0, n, width)]



def project(prog, name, src, k_tiles, groups):
    nc, W, ps = prog.nc, prog.weights, prog.ps
    NB = 8
    by_act = [g[6] is not None or i % 2 == 0 for i, g in enumerate(groups)]
    order = [sum(by_act[:i + 1]) if a else i + 1 - sum(by_act[:i + 1]) for i, a in enumerate(by_act)]

    def out_of(i):
        _, _, width, tok, part, _, _ = groups[i]
        return ps[part:part + width, i % NB, :] if tok is None else ps[:, i % NB, 0:width]

    with Stage(prog, name) as st:
        product = st.counter("product")
        act_copied = st.counter("act_copied")
        dve_copied = st.counter("dve_copied")

        @st.tensor
        def _(pe):
            held, w = None, None
            for i, (tile, c, width, tok, part, _, _) in enumerate(groups):
                left = held if tile != held else None
                if tile != held:
                    w = W.take(pe, name, tile)
                    held = tile
                if i >= NB:
                    pe.wait_ge(act_copied if by_act[i - NB] else dve_copied, order[i - NB])
                for k in range(k_tiles):
                    if tok is None:
                        m = nc.tensor.matmul(out_of(i), w[:, k, c:c + width], src[:, k, :],
                                             start=(k == 0), stop=(k == k_tiles - 1))
                    else:
                        m = nc.tensor.matmul(out_of(i), src[:, k, tok * P:(tok + 1) * P], w[:, k, c:c + width],
                                             start=(k == 0), stop=(k == k_tiles - 1))
                    if k == 0 and left is not None:
                        W.leave(m, name, left)
                m.then_inc(product, 1)

        @st.scalar
        def _(act):
            for i, g in enumerate(groups):
                if by_act[i]:
                    act.wait_ge(product, i + 1)
                    nc.scalar.activation(g[5], out_of(i), g[6] or ACT.Copy).then_inc(act_copied, 1)

        @st.vector
        def _(dve):
            for i, g in enumerate(groups):
                if not by_act[i]:
                    dve.wait_ge(product, i + 1)
                    nc.vector.tensor_copy(g[5], out_of(i)).then_inc(dve_copied, 1)


def transpose_stage(prog, name, jobs):
    nc, ps, ident = prog.nc, prog.ps, prog.ident
    with Stage(prog, name) as st:
        turned = st.counter("turned")
        act_copied = st.counter("act_copied")
        dve_copied = st.counter("dve_copied")

        @st.tensor
        def _(pe):
            for i, (sources, _) in enumerate(jobs):
                if i >= 8:
                    pe.wait_ge((act_copied, dve_copied)[i % 2], (i - 8) // 2 + 1)
                for j, s in enumerate(sources):
                    m = nc.tensor.transpose(ps[:, i % 8, j * P:(j + 1) * P], s, ident)
                m.then_inc(turned, 1)

        def out(i):
            return ps[:, i % 8, 0:len(jobs[i][0]) * P]

        def fit(dst, src):
            return src.rearrange("p (a b) -> p a b", b=dst.shape[-1]) if len(dst.shape) == 3 else src

        @st.scalar
        def _(act):
            for i in range(0, len(jobs), 2):
                act.wait_ge(turned, i + 1)
                nc.scalar.activation(jobs[i][1], fit(jobs[i][1], out(i)), ACT.Copy).then_inc(act_copied, 1)

        @st.vector
        def _(dve):
            for i in range(1, len(jobs), 2):
                dve.wait_ge(turned, i + 1)
                nc.vector.tensor_copy(jobs[i][1], fit(jobs[i][1], out(i))).then_inc(dve_copied, 1)


def load_stage(prog, name, pairs):
    with Stage(prog, name) as st:
        landed = st.counter("landed")

        @st.sync
        def _(sp):
            for dst, src in pairs:
                sp.dma_start(dst, src).then_inc(landed, 16)
            sp.wait_ge(landed, 16 * len(pairs))


def down_project(prog, name, src_feat, w, gate=None):
    nc, ps = prog.nc, prog.ps
    with ExitStack() as own:
        dw = prog.sbuf(name + "_w", [P, KD, D], own)
        with Stage(prog, name) as st:
            landed = [st.counter(f"landed_{q}") for q in range(4)]
            product, summed = st.counter("product"), st.counter("summed")

            @st.sync
            def _(sp):
                for q in range(4):
                    sp.dma_start(dw[:, 2 * q:2 * q + 2, :],
                                 w[2 * q * P:(2 * q + 2) * P, :].rearrange("(k p) n -> p k n", p=P)
                                 ).then_inc(landed[q], 16)

            @st.tensor
            def _(pe):
                for k in range(KD):
                    if k % 2 == 0:
                        pe.wait_ge(landed[k // 2], 16)
                    for i in range(2 * NT):
                        m = nc.tensor.matmul(ps[:, i, :], src_feat[:, k, (i // 2) * P:(i // 2 + 1) * P],
                                             dw[:, k, (i % 2) * BANK:(i % 2 + 1) * BANK],
                                             start=(k == 0), stop=(k == KD - 1))
                        if k == KD - 1:
                            m.then_inc(product, 1)

            @st.vector
            def _(dve):
                for i in range(2 * NT):
                    t, c = i // 2, slice((i % 2) * BANK, (i % 2 + 1) * BANK)
                    dve.wait_ge(product, i + 1)
                    out = prog.acc[:, t, c]
                    if gate is None:
                        nc.vector.scalar_tensor_tensor(out=out, in0=prog.x_tok[:, t, c], scalar=ALPHA,
                                                       in1=ps[:, i, :], op0=ALU.mult, op1=ALU.add)
                    else:
                        nc.vector.scalar_tensor_tensor(out=out, in0=gate[:, c], scalar=1.0, in1=ps[:, i, :],
                                                       op0=ALU.add, op1=ALU.mult).then_inc(summed, 1)
                if gate is not None:
                    dve.wait_ge(summed, 2 * NT)
                    for t in range(NT):
                        nc.vector.scalar_tensor_tensor(out=prog.acc[:, t, :], in0=prog.x_tok[:, t, :], scalar=ALPHA,
                                                       in1=prog.acc[:, t, :], op0=ALU.mult, op1=ALU.add)


def layer_norm(prog, name, gb_src, last=False):
    nc, ps, acc, x_tok = prog.nc, prog.ps, prog.acc, prog.x_tok
    with ExitStack() as own:
        gb = prog.sbuf(name + "_gb", [P, 2, D], own)
        stats = prog.sbuf(name + "_stats", [P, NT, 12], own)
        mv = prog.sbuf(name + "_mv", [P, NT, 2], own)
        var = prog.sbuf(name + "_var", [P, NT], own)
        sd = prog.sbuf(name + "_sd", [P, NT], own)
        rs = prog.sbuf(name + "_rs", [P, NT], own)
        with Stage(prog, name) as st:
            landed = st.counter("landed")
            dve_link, var_ready = st.counter("dve_link"), st.counter("var_ready")
            sd_ready, normed = st.counter("sd_ready"), st.counter("normed")
            done, stored = st.counter("done"), st.counter("stored")
            turned, act_copied, dve_copied = st.counter("turned"), st.counter("act_copied"), st.counter("dve_copied")

            @st.sync
            def _(sp):
                sp.dma_start(gb[:, :, :], gb_src).then_inc(landed, 16)
                if last:
                    for t in range(NT):
                        sp.wait_ge(done, t + 1)
                        sp.dma_start(prog.out[t * P:(t + 1) * P, :], x_tok[:, t, :]).then_inc(stored, 16)
                    sp.wait_ge(stored, 16 * NT)

            def copy_out(dve, t):
                dve.wait_ge(turned, 2 * t + 2)
                nc.vector.tensor_copy(prog.x_feat[:, 4:8, t * P:(t + 1) * P],
                                      ps[:, 2 * t + 1, :].rearrange("p (k n) -> p k n", n=P)).then_inc(dve_copied, 1)

            @st.vector
            def _(dve):
                link = linker(dve, dve_link)
                for t in range(NT):
                    for h in range(2):
                        m = nc.vector.bn_stats(stats[:, t, 6 * h:6 * h + 6], acc[:, t, h * BANK:(h + 1) * BANK])
                link(m)
                for t in range(NT):
                    m = nc.vector.bn_aggr(mv[:, t, :], stats[:, t, :])
                link(m)
                nc.vector.tensor_scalar(var[:, :], mv[:, :, 1], LN_EPS, None, ALU.add).then_inc(var_ready, 1)
                dve.wait_ge(sd_ready, 1)
                link(nc.vector.reciprocal(rs[:, :], sd[:, :]))
                dve.wait_ge(landed, 16)
                for t in range(NT):
                    link(nc.vector.tensor_scalar(acc[:, t, :], acc[:, t, :], mv[:, t, 0:1], rs[:, t:t + 1],
                                                 ALU.subtract, ALU.mult))
                    nc.vector.tensor_tensor(acc[:, t, :], acc[:, t, :], gb[:, 0, :], ALU.mult).then_inc(normed, 1)
                    if not last and t >= 1:
                        copy_out(dve, t - 1)
                if not last:
                    copy_out(dve, NT - 1)

            @st.gpsimd
            def _(pool):
                pool.wait_ge(landed, 16)
                for t in range(NT):
                    pool.wait_ge(normed, t + 1)
                    nc.gpsimd.tensor_tensor(x_tok[:, t, :], acc[:, t, :], gb[:, 1, :], ALU.add).then_inc(done, 1)

            @st.scalar
            def _(act):
                act.wait_ge(var_ready, 1)
                nc.scalar.activation(sd[:, :], var[:, :], ACT.Sqrt).then_inc(sd_ready, 1)
                if not last:
                    for t in range(NT):
                        act.wait_ge(turned, 2 * t + 1)
                        nc.scalar.activation(prog.x_feat[:, 0:4, t * P:(t + 1) * P],
                                             ps[:, 2 * t, :].rearrange("p (k n) -> p k n", n=P), ACT.Copy
                                             ).then_inc(act_copied, 1)

            @st.tensor
            def _(pe):
                if not last:
                    for t in range(NT):
                        pe.wait_ge(done, t + 1)
                        for k in range(KD):
                            m = nc.tensor.transpose(ps[:, 2 * t + k // 4, (k % 4) * P:(k % 4 + 1) * P],
                                                    x_tok[:, t, k * P:(k + 1) * P], prog.ident)
                            if k % 4 == 3:
                                m.then_inc(turned, 1)


def swiglu_parts(prog, name, parts, w1, w3, w2, gates=None):
    nc, W, ps = prog.nc, prog.weights, prog.ps
    chunks = [(c, min(c + UP_COLS, FF_PART)) for c in range(0, FF_PART, UP_COLS)]
    NTILE = 2 * len(chunks)
    assert NTILE % RING == 0
    first = W.first[name]
    ready = [W.tiles[first + s][2] for s in range(RING)]
    used0 = W.n_released
    per_slot = NTILE // RING * 16

    def source(e, j):
        c0, c1 = chunks[j // 2]
        w = (w1, w3)[j % 2]
        return w[bass.ds(e, 1), :, c0:c1].rearrange("a (k p) n -> p (a k) n", p=P)

    def slot_view(j):
        c0, c1 = chunks[j // 2]
        n = c1 - c0
        return W.ring[:, j % RING, 0:KD * n].rearrange("p (k n) -> p k n", n=n)

    with ExitStack() as own:
        hid = prog.sbuf(name + "_hid", [P, FT, S], own)
        sig = prog.sbuf(name + "_sig", [P, 2, S], own)
        dw = prog.sbuf(name + "_w2", [P, FT, D], own)
        with Stage(prog, name) as st:
            up_ready, silu_done = st.counter("up_ready"), st.counter("silu_done")
            hid_done = st.counter("hid_done")
            down_ready = st.counter("down_ready")
            down_added = st.counter("down_added")
            w2_landed, acc_ready = st.counter("w2_landed"), st.counter("acc_ready")

            @st.sync
            def _(sp):
                while W.issued < first + RING:
                    if W.tiles[W.issued] is not None:
                        W.load(sp, W.issued)
                    W.issued += 1

                def part(e, values, count):
                    here, after = e
                    for j in range(count):
                        sp.wait_ge(W.used, values[j])
                        if j == 0:
                            sp.dma_start(dw[:, :, :], w2[bass.ds(here, 1)].rearrange("a (k p) n -> p (a k) n", p=P)
                                         ).then_inc(w2_landed, 16)
                        ahead = j + RING
                        e_of, j_of = (here, ahead) if ahead < NTILE else (after, ahead - NTILE)
                        sp.dma_start(slot_view(j_of), source(e_of, j_of)).then_inc(W.loaded[j_of % RING], 16)

                with sp.Fori(0, parts - 1) as e:
                    values = [sp.snap(e * NTILE + (used0 + j + 1)) for j in range(NTILE)]
                    part((e, sp.snap(e + 1)), values, NTILE)
                part((parts - 1, None), [(parts - 1) * NTILE + used0 + j + 1 for j in range(NTILE)], NTILE - RING)
                W.n_released += parts * NTILE
                for i in range(parts * NTILE):
                    W.released[first + i] = used0 + i + 1
                W.issued = first + parts * NTILE

            @st.tensor
            def _(pe):
                with pe.Fori(0, parts) as e:
                    for m in range(FT):
                        c, col = m // 2, (m % 2) * P
                        pe.wait_ge(hid_done, e * FT + (m + 1))
                        for which in range(2):
                            j = 2 * c + which
                            if m % 2 == 0:
                                pe.wait_ge(W.loaded[j % RING], e * per_slot + (ready[j % RING] + 16 * (j // RING)))
                            w = slot_view(j)
                            for k in range(KD):
                                mm = nc.tensor.matmul(ps[:, 2 * (m % 2) + which, :], w[:, k, col:col + P],
                                                      prog.x_feat[:, k, :], start=(k == 0), stop=(k == KD - 1))
                                last_of_chunk = m % 2 == 1 or m == FT - 1
                                if k == 0 and (which == 1 and last_of_chunk):
                                    mm.then_inc(W.used, 1)
                                if k == 0 and which == 0 and m % 2 == 0 and m > 0:
                                    mm.then_inc(W.used, 1)
                            mm.then_inc(up_ready, 1)
                    pe.wait_ge(w2_landed, e * 16 + 16)
                    pe.wait_ge(hid_done, e * FT + (FT + 2))
                    for i in range(2 * NT):
                        t, h = i // 2, i % 2
                        pe.wait_ge(down_added, e * (2 * NT) + (i + 1))
                        for m in range(FT):
                            mm = nc.tensor.matmul(ps[:, 4 + i % 4, :], hid[:, m, t * P:(t + 1) * P],
                                                  dw[:, m, h * BANK:(h + 1) * BANK],
                                                  start=(m == 0), stop=(m == FT - 1))
                            if i == 0 and m == 0:
                                mm.then_inc(W.used, 1)
                        mm.then_inc(down_ready, 1)

            @st.scalar
            def _(act):
                with act.Fori(0, parts) as e:
                    for m in range(FT):
                        act.wait_ge(up_ready, e * (2 * FT) + (2 * m + 1))
                        act.wait_ge(hid_done, e * FT + (m + 1))
                        nc.scalar.activation(sig[:, m % 2, :], ps[:, 2 * (m % 2), :], ACT.Silu).then_inc(silu_done, 1)

            @st.vector
            def _(dve):
                dve.sem_inc(hid_done, 2)
                dve.sem_inc(down_added, 4)
                for t in range(NT):
                    nc.vector.tensor_scalar(prog.acc[:, t, :], prog.x_tok[:, t, :], ALPHA, None, ALU.mult
                                            ).then_inc(acc_ready, 1)
                dve.wait_ge(acc_ready, NT)
                with dve.Fori(0, parts) as e:
                    for m in range(FT):
                        dve.wait_ge(up_ready, e * (2 * FT) + (2 * m + 2))
                        dve.wait_ge(silu_done, e * FT + (m + 1))
                        nc.vector.tensor_tensor(hid[:, m, :], sig[:, m % 2, :], ps[:, 2 * (m % 2) + 1, :],
                                                ALU.mult).then_inc(hid_done, 1)
                    dve.wait_ge(down_added, e * (2 * NT) + 4)
                    for i in range(2 * NT):
                        t, c = i // 2, slice((i % 2) * BANK, (i % 2 + 1) * BANK)
                        dve.wait_ge(down_ready, e * (2 * NT) + (i + 1))
                        if gates is None:
                            m_ = nc.vector.tensor_tensor(prog.acc[:, t, c], ps[:, 4 + i % 4, :], prog.acc[:, t, c],
                                                         ALU.add)
                        else:
                            m_ = nc.vector.scalar_tensor_tensor(out=prog.acc[:, t, c], in0=ps[:, 4 + i % 4, :],
                                                                scalar=gates[:, t, bass.ds(e, 1)],
                                                                in1=prog.acc[:, t, c], op0=ALU.mult, op1=ALU.add)
                        m_.then_inc(down_added, 1)



def gdn_conv(prog, name, dests, taps):
    nc, W, ps = prog.nc, prog.weights, prog.ps
    NF, PAD = len(dests), 3
    with ExitStack() as own:
        padded = prog.sbuf(name + "_padded", [P, 2, PAD + S], own)
        conv = prog.sbuf(name + "_conv", [P, 2, S], own)
        with Stage(prog, name) as st:
            product, copied = st.counter("product"), st.counter("copied")
            convolved, activated = st.counter("convolved"), st.counter("activated")
            zeroed, dve_link = st.counter("zeroed"), st.counter("dve_link")

            @st.gpsimd
            def _(pool):
                nc.gpsimd.memset(padded[:, :, 0:PAD], 0.0).then_inc(zeroed, 1)

            @st.tensor
            def _(pe):
                for f in range(NF):
                    if f % 2 == 0:
                        w = W.take(pe, name, f // 2)
                    if f >= 4:
                        pe.wait_ge(copied, f - 3)
                    for k in range(KD):
                        m = nc.tensor.matmul(ps[:, f % 4, :], w[:, k, (f % 2) * P:(f % 2 + 1) * P],
                                             prog.x_feat[:, k, :], start=(k == 0), stop=(k == KD - 1))
                        if k == 0 and f % 2 == 0 and f:
                            W.leave(m, name, f // 2 - 1)
                    m.then_inc(product, 1)

            @st.scalar
            def _(act):
                def silu(f):
                    act.wait_ge(convolved, f + 1)
                    nc.scalar.activation(dests[f], conv[:, f % 2, :], ACT.Silu).then_inc(activated, 1)
                for f in range(NF):
                    act.wait_ge(product, f + 1)
                    if f >= 2:
                        act.wait_ge(convolved, f - 1)
                    nc.scalar.activation(padded[:, f % 2, PAD:PAD + S], ps[:, f % 4, :], ACT.Copy).then_inc(copied, 1)
                    if f:
                        silu(f - 1)
                silu(NF - 1)

            @st.vector
            def _(dve):
                link = linker(dve, dve_link)
                dve.wait_ge(zeroed, 1)
                for f in range(NF):
                    dve.wait_ge(copied, f + 1)
                    if f >= 2:
                        dve.wait_ge(activated, f - 1)
                    out, x = conv[:, f % 2, :], padded[:, f % 2, :]
                    link(nc.vector.tensor_scalar(out, x[:, 0:S], taps[:, 4 * f:4 * f + 1], None, ALU.mult))
                    for j in (1, 2, 3):
                        m = nc.vector.scalar_tensor_tensor(out=out, in0=x[:, j:j + S], scalar=taps[:, 4 * f + j:4 * f + j + 1],
                                                           in1=out, op0=ALU.mult, op1=ALU.add)
                        if j < 3:
                            link(m)
                    m.then_inc(convolved, 1)


def gdn_norms(prog, name, tiles):
    nc, ps = prog.nc, prog.ps
    with ExitStack() as own:
        sq = prog.sbuf(name + "_sq", [P, 2, S], own)
        sd = prog.sbuf(name + "_sd", [P, 2, S], own)
        with Stage(prog, name) as st:
            squared, summed, rooted = st.counter("squared"), st.counter("summed"), st.counter("rooted")
            inverted, done = st.counter("inverted"), st.counter("done")
            n = len(tiles)

            @st.gpsimd
            def _(pool):
                for i, (x, _) in enumerate(tiles):
                    if i >= 2:
                        pool.wait_ge(summed, i - 1)
                    nc.gpsimd.tensor_tensor(sq[:, i % 2, :], x, x, ALU.mult).then_inc(squared, 1)

            @st.tensor
            def _(pe):
                for i in range(n):
                    pe.wait_ge(squared, i + 1)
                    if i >= 4:
                        pe.wait_ge(rooted, i - 3)
                    nc.tensor.matmul(ps[:, i % 4, :], prog.ones, sq[:, i % 2, :], start=True, stop=True).then_inc(summed, 1)

            @st.scalar
            def _(act):
                for i, (_, scale) in enumerate(tiles):
                    act.wait_ge(summed, i + 1)
                    if i >= 2:
                        act.wait_ge(done, i - 1)
                    c = scale ** -2.0
                    nc.scalar.activation(sd[:, i % 2, :], ps[:, i % 4, :], ACT.Sqrt, scale=c,
                                         bias=prog.eps_qk if c != 1.0 else prog.eps_norm).then_inc(rooted, 1)

            @st.vector
            def _(dve):
                for i, (x, _) in enumerate(tiles):
                    dve.wait_ge(rooted, i + 1)
                    nc.vector.reciprocal(sd[:, i % 2, :], sd[:, i % 2, :]).then_inc(inverted, 1)
                    dve.wait_ge(inverted, i + 1)
                    nc.vector.tensor_tensor(x, x, sd[:, i % 2, :], ALU.mult).then_inc(done, 1)


def gdn_gates(prog, name, ba, params, small):
    nc, ps = prog.nc, prog.ps
    g, beta, G, beG, kd, eL, t0, t1, neg_a = small
    b, a = ba[:, :, 0:HEADS], ba[:, :, HEADS:2 * HEADS]
    dt_bias, a_log = params[:, 0:HEADS], params[:, HEADS:2 * HEADS]
    rep = [P, NCH, HEADS]

    def over(x):
        return x.unsqueeze(1).to_broadcast(rep)

    def flat(x):
        return x.rearrange("p c h -> p (c h)")
    with Stage(prog, name) as st:
        acted, link_sem = st.counter("acted"), st.counter("dve_link")
        x_ready, a_ready, e_ready = st.counter("x_ready"), st.counter("a_ready"), st.counter("e_ready")
        g_ready, sums, diff = st.counter("g_ready"), st.counter("sums"), st.counter("diff")

        @st.scalar
        def _(act):
            nc.scalar.activation(beta, b, ACT.Sigmoid).then_inc(acted, 1)
            nc.scalar.activation(neg_a, a_log, ACT.Exp).then_inc(acted, 1)
            act.wait_ge(x_ready, 1)
            nc.scalar.activation(t1, t1, ACT.Exp, scale=-1.0).then_inc(acted, 1)
            act.wait_ge(acted, 3)
            nc.scalar.activation(t1, t1, ACT.Ln, bias=1.0).then_inc(acted, 1)
            act.wait_ge(diff, 1)
            nc.scalar.activation(kd, kd, ACT.Exp).then_inc(acted, 1)
            nc.scalar.activation(eL, ps[:, 1, 0:NCH * HEADS].rearrange("p (c h) -> p c h", h=HEADS), ACT.Exp
                                 ).then_inc(acted, 1)
            nc.scalar.activation(beG, G, ACT.Exp).then_inc(acted, 1)

        @st.vector
        def _(dve):
            link = linker(dve, link_sem)
            link(nc.vector.tensor_tensor(t0, a, over(dt_bias), ALU.add))
            link(nc.vector.tensor_scalar(t1, t0, -1.0, None, ALU.mult))
            nc.vector.tensor_tensor(t1, t0, t1, ALU.max).then_inc(x_ready, 1)
            link(nc.vector.tensor_scalar(t0, t0, 0.0, None, ALU.max))
            dve.wait_ge(acted, 4)
            link(nc.vector.tensor_tensor(t0, t0, t1, ALU.add))
            nc.vector.scalar_tensor_tensor(out=g, in0=t0, scalar=-1.0, in1=over(neg_a),
                                           op0=ALU.mult, op1=ALU.mult).then_inc(g_ready, 1)
            dve.wait_ge(sums, 2)
            link(nc.vector.tensor_copy(flat(G), ps[:, 0, 0:NCH * HEADS]))
            nc.vector.tensor_tensor(flat(kd), ps[:, 1, 0:NCH * HEADS], flat(G), ALU.subtract).then_inc(diff, 1)
            dve.wait_ge(acted, 7)
            link(nc.vector.tensor_tensor(beG, beG, beta, ALU.mult))

        @st.tensor
        def _(pe):
            pe.wait_ge(g_ready, 1)
            nc.tensor.matmul(ps[:, 0, 0:NCH * HEADS], prog.tri, flat(g), start=True, stop=True).then_inc(sums, 1)
            nc.tensor.matmul(ps[:, 1, 0:NCH * HEADS], prog.ones, flat(g), start=True, stop=True).then_inc(sums, 1)


def gdn_decays(prog, name, h0, q, k, g, G, dec, att, am):
    nc, ps = prog.nc, prog.ps
    with ExitStack() as own:
        eg = prog.sbuf(name + "_eg", [P, 2, S], own)
        with Stage(prog, name) as st:
            product = st.counter("product")
            shifted, decayed, masked = st.counter("shifted"), st.counter("decayed"), st.counter("masked")
            grown, scaled, weighted = st.counter("grown"), st.counter("scaled"), st.counter("weighted")

            @st.tensor
            def _(pe):
                for i in range(HG):
                    b0 = 4 * (i % 2)
                    if i >= 2:
                        pe.wait_ge(weighted, 2 * (i - 1))
                        pe.wait_ge(grown, i - 1)
                        pe.wait_ge(shifted, i - 1)
                    for c in range(NCH):
                        m = nc.tensor.matmul(ps[:, b0, c * P:(c + 1) * P], bc(g[:, c, h0 + i:h0 + i + 1], [P, P]), prog.tri,
                                             start=True, stop=True)
                    m.then_inc(product, 1)
                    for j, other in ((1, k), (2, q)):
                        for c in range(NCH):
                            cs = slice(c * P, (c + 1) * P)
                            m = nc.tensor.matmul(ps[:, b0 + j, cs], k[:, h0 + i, cs], other[:, h0 + i, cs],
                                                 start=True, stop=True)
                        m.then_inc(product, 1)

            @st.vector
            def _(dve):
                for i in range(HG):
                    b0 = 4 * (i % 2)
                    dve.wait_ge(product, 3 * i + 1)
                    for c in range(NCH):
                        m = nc.vector.tensor_scalar(dec[:, i, c * P:(c + 1) * P], ps[:, b0, c * P:(c + 1) * P],
                                                    G[:, c, h0 + i:h0 + i + 1], 0.0, ALU.subtract, ALU.min)
                    m.then_inc(shifted, 1)
                    dve.wait_ge(masked, i + 1)
                    dve.wait_ge(product, 3 * i + 3)
                    for out, j in ((am, 1), (att, 2)):
                        nc.vector.tensor_tensor(out[:, i, :], ps[:, b0 + j, :], dec[:, i, :], ALU.mult
                                                ).then_inc(weighted, 1)

            @st.scalar
            def _(act):
                for i in range(HG):
                    act.wait_ge(shifted, i + 1)
                    nc.scalar.activation(dec[:, i, :], dec[:, i, :], ACT.Exp).then_inc(decayed, 1)
                    if i >= 2:
                        act.wait_ge(scaled, i - 1)
                    nc.scalar.activation(eg[:, i % 2, :], ps[:, 4 * (i % 2), :], ACT.Exp).then_inc(grown, 1)

            @st.gpsimd
            def _(pool):
                for i in range(HG):
                    d = dec[:, i, :].rearrange("p (c n) -> p c n", n=P)
                    pool.wait_ge(decayed, i + 1)
                    nc.gpsimd.tensor_tensor(d, d, prog.tri.unsqueeze(1).to_broadcast([P, NCH, P]), ALU.mult
                                            ).then_inc(masked, 1)
                    pool.wait_ge(grown, i + 1)
                    pool.wait_ge(product, 3 * i + 3)
                    nc.gpsimd.tensor_tensor(q[:, h0 + i, :], q[:, h0 + i, :], eg[:, i % 2, :], ALU.mult
                                            ).then_inc(scaled, 1)


def gdn_inverse(prog, name, h0, beta, am, inv, inv_t, prod):
    nc, ps = prog.nc, prog.ps
    N = LEVELS * HG

    def blocks(x):
        return x.rearrange("p (c n) -> p c n", n=P)
    with ExitStack() as own:
        part = prog.sbuf(name + "_part", [P, 2, S], own)
        with Stage(prog, name) as st:
            start, cut = st.counter("start"), st.counter("cut")
            u_ready, u_copied = st.counter("u_ready"), st.counter("u_copied")
            p_ready, updated = st.counter("p_ready"), st.counter("updated")

            @st.gpsimd
            def _(pool):
                for n in range(N):
                    level, i = divmod(n, HG)
                    if n >= 2:
                        pool.wait_ge(u_ready, n - 1)
                    nc.gpsimd.tensor_tensor(blocks(part[:, n % 2, :]), blocks(am[:, i, :]),
                                            prog.level_masks[:, level, :].unsqueeze(1).to_broadcast([P, NCH, P]),
                                            ALU.mult).then_inc(cut, 1)

            @st.tensor
            def _(pe):
                def chunks():
                    return [slice(c * P, (c + 1) * P) for c in range(NCH)]

                def u(n):
                    i = n % HG
                    pe.wait_ge(cut, n + 1)
                    pe.wait_ge(start, HG)
                    if n >= HG:
                        pe.wait_ge(updated, 2 * (n - HG + 1))
                    for cs in chunks():
                        m = nc.tensor.matmul(ps[:, i, cs], part[:, n % 2, cs], inv[:, i, cs], start=True, stop=True)
                    m.then_inc(u_ready, 1)

                def p(n):
                    i, b = n % HG, 4 + 2 * (n % 2)
                    pe.wait_ge(u_copied, n + 1)
                    if n >= 2:
                        pe.wait_ge(updated, 2 * (n - 1))
                    for cs in chunks():
                        m = nc.tensor.matmul(ps[:, b, cs], inv_t[:, i, cs], prod[:, i, cs], start=True, stop=True)
                    m.then_inc(p_ready, 1)
                    for cs in chunks():
                        m = nc.tensor.matmul(ps[:, b + 1, cs], prod[:, i, cs], inv_t[:, i, cs], start=True, stop=True)
                    m.then_inc(p_ready, 1)

                for level in range(LEVELS):
                    for i in range(HG):
                        u(level * HG + i)
                    for i in range(HG):
                        p(level * HG + i)

            @st.vector
            def _(dve):
                for i in range(HG):
                    for x in (inv, inv_t):
                        m = nc.vector.tensor_copy(blocks(x[:, i, :]), prog.ident.unsqueeze(1).to_broadcast([P, NCH, P]))
                    m.then_inc(start, 1)
                for level in range(LEVELS):
                    for i in range(HG):
                        n = level * HG + i
                        dve.wait_ge(u_ready, n + 1)
                        if n >= HG:
                            dve.wait_ge(u_copied, n - HG + 1)
                        scale = beta[:, :, h0 + i:h0 + i + 1].to_broadcast([P, NCH, P])
                        nc.vector.tensor_tensor(blocks(prod[:, i, :]), blocks(ps[:, i, :]), scale, ALU.mult
                                                ).then_inc(u_copied, 1)
                    for i in range(HG):
                        n = level * HG + i
                        b = 4 + 2 * (n % 2)
                        dve.wait_ge(start, HG)
                        if n >= HG:
                            dve.wait_ge(updated, 2 * (n - HG + 1))
                        dve.wait_ge(p_ready, 2 * n + 2)
                        nc.vector.tensor_tensor(inv[:, i, :], inv[:, i, :], ps[:, b, :], ALU.subtract).then_inc(updated, 1)
                        nc.vector.tensor_tensor(inv_t[:, i, :], inv_t[:, i, :], ps[:, b + 1, :], ALU.subtract
                                                ).then_inc(updated, 1)


def gdn_uw(prog, name, h0, k_tok, v_tok, beta, beG, kd, inv_t, vb, kb, u, w_t):
    nc, ps = prog.nc, prog.ps
    hs = slice(h0 * P, (h0 + HG) * P)

    def heads(x):
        return x.rearrange("p (h n) -> p h n", n=P)
    with Stage(prog, name) as st:
        vb_ready, kb_ready = st.counter("vb_ready"), st.counter("kb_ready")
        u_ready, w_ready, u_copied, w_copied = (st.counter(x) for x in ("u_ready", "w_ready", "u_copied", "w_copied"))

        @st.vector
        def _(dve):
            for c in range(NCH):
                nc.vector.tensor_tensor(heads(vb[:, c, :]), heads(v_tok[:, c, hs]),
                                        beta[:, c, h0:h0 + HG].unsqueeze(2).to_broadcast([P, HG, P]),
                                        ALU.mult).then_inc(vb_ready, 1)
            for c in range(NCH):
                dve.wait_ge(u_ready, c + 1)
                nc.vector.tensor_copy(u[:, c, :], ps[:, c, :]).then_inc(u_copied, 1)

        @st.gpsimd
        def _(pool):
            for c in range(NCH):
                nc.gpsimd.tensor_tensor(heads(kb[:, c, :]), heads(k_tok[:, c, hs]),
                                        beG[:, c, h0:h0 + HG].unsqueeze(2).to_broadcast([P, HG, P]),
                                        ALU.mult).then_inc(kb_ready, 1)
            pool.wait_ge(kb_ready, NCH)
            for c in range(NCH):
                nc.gpsimd.tensor_tensor(heads(k_tok[:, c, hs]), heads(k_tok[:, c, hs]),
                                        kd[:, c, h0:h0 + HG].unsqueeze(2).to_broadcast([P, HG, P]), ALU.mult)

        @st.tensor
        def _(pe):
            for c in range(NCH):
                cs = slice(c * P, (c + 1) * P)
                pe.wait_ge(vb_ready, c + 1)
                for i in range(HG):
                    m = nc.tensor.matmul(ps[:, c, i * P:(i + 1) * P], inv_t[:, i, cs], vb[:, c, i * P:(i + 1) * P],
                                         start=True, stop=True)
                m.then_inc(u_ready, 1)
            pe.wait_ge(kb_ready, NCH)
            for i in range(HG):
                for c in range(NCH):
                    cs = slice(c * P, (c + 1) * P)
                    m = nc.tensor.matmul(ps[:, 4 + i, cs], kb[:, c, i * P:(i + 1) * P], inv_t[:, i, cs],
                                         start=True, stop=True)
                m.then_inc(w_ready, 1)

        @st.scalar
        def _(act):
            for i in range(HG):
                act.wait_ge(w_ready, i + 1)
                nc.scalar.activation(w_t[:, i, :], ps[:, 4 + i, :], ACT.Copy).then_inc(w_copied, 1)


def gdn_scan(prog, name, h0, q, att, k_tok, eL, u, w_t, out):
    nc, ps = prog.nc, prog.ps
    with ExitStack() as own:
        state = prog.sbuf(name + "_state", [P, HG * P], own)
        with Stage(prog, name) as st:
            ws, v_new, o_ready = st.counter("ws"), st.counter("v_new"), st.counter("o_ready")
            o_copied, kv, s_new = st.counter("o_copied"), st.counter("kv"), st.counter("s_new")

            @st.tensor
            def _(pe):
                for c in range(NCH):
                    cs = slice(c * P, (c + 1) * P)
                    if c:
                        pe.wait_ge(s_new, c)
                        pe.wait_ge(v_new, c)
                        for i in range(HG):
                            m = nc.tensor.matmul(ps[:, 0, i * P:(i + 1) * P], w_t[:, i, cs], state[:, i * P:(i + 1) * P],
                                                 start=True, stop=True)
                        m.then_inc(ws, 1)
                    if c >= 2:
                        pe.wait_ge(o_copied, c - 1)
                    pe.wait_ge(v_new, c + 1)
                    for i in range(HG):
                        hp = slice(i * P, (i + 1) * P)
                        if c:
                            nc.tensor.matmul(ps[:, 1 + c % 2, hp], q[:, h0 + i, cs], state[:, hp], start=True, stop=False)
                        m = nc.tensor.matmul(ps[:, 1 + c % 2, hp], att[:, i, cs], u[:, c, hp], start=(c == 0), stop=True)
                    m.then_inc(o_ready, 1)
                    if c < NCH - 1:
                        for i in range(HG):
                            hp = slice(i * P, (i + 1) * P)
                            m = nc.tensor.matmul(ps[:, 3, hp], k_tok[:, c, (h0 + i) * P:(h0 + i + 1) * P], u[:, c, hp],
                                                 start=True, stop=True)
                        m.then_inc(kv, 1)

            @st.vector
            def _(dve):
                for c in range(NCH):
                    if c == 0:
                        dve.sem_inc(v_new, 1)
                    else:
                        dve.wait_ge(ws, c)
                        nc.vector.tensor_tensor(u[:, c, :], u[:, c, :], ps[:, 0, :], ALU.subtract).then_inc(v_new, 1)
                    if c < NCH - 1:
                        dve.wait_ge(kv, c + 1)
                        if c == 0:
                            nc.vector.tensor_copy(state[:, :], ps[:, 3, :]).then_inc(s_new, 1)
                        else:
                            dve.wait_ge(s_new, c)
                            dve.wait_ge(o_ready, c + 1)
                            for i in range(HG):
                                hp = slice(i * P, (i + 1) * P)
                                m = nc.vector.scalar_tensor_tensor(out=state[:, hp], in0=state[:, hp],
                                                                   scalar=eL[:, c, h0 + i:h0 + i + 1], in1=ps[:, 3, hp],
                                                                   op0=ALU.mult, op1=ALU.add)
                            m.then_inc(s_new, 1)

            @st.scalar
            def _(act):
                for c in range(NCH):
                    act.wait_ge(o_ready, c + 1)
                    nc.scalar.activation(out[:, c, h0 * P:(h0 + HG) * P], ps[:, 1 + c % 2, :], ACT.Copy
                                         ).then_inc(o_copied, 1)


def gdn_output_gate(prog, name, o, z, norm_g):
    nc = prog.nc
    with ExitStack() as own:
        sq = prog.sbuf(name + "_sq", [P, NT, D], own)
        ms = prog.sbuf(name + "_ms", [P, NT, HEADS], own)
        with Stage(prog, name) as st:
            squared, summed, rooted = st.counter("squared"), st.counter("summed"), st.counter("rooted")
            dve_link, gained, sd = st.counter("dve_link"), st.counter("gained"), None

            def heads(x):
                return x.rearrange("p (h n) -> p h n", n=P)

            @st.scalar
            def _(act):
                for t in range(NT):
                    nc.scalar.activation(sq[:, t, :], o[:, t, :], ACT.Square).then_inc(squared, 1)
                act.wait_ge(summed, NT)
                nc.scalar.activation(ms[:, :, :], ms[:, :, :], ACT.Sqrt, scale=1.0 / P, bias=prog.eps_norm).then_inc(rooted, 1)

            @st.gpsimd
            def _(pool):
                for t in range(NT):
                    nc.gpsimd.tensor_tensor(heads(z[:, t, :]), heads(z[:, t, :]),
                                            norm_g.unsqueeze(1).to_broadcast([P, HEADS, P]), ALU.mult).then_inc(gained, 1)

            @st.vector
            def _(dve):
                link = linker(dve, dve_link)
                for t in range(NT):
                    dve.wait_ge(squared, t + 1)
                    nc.vector.tensor_reduce(ms[:, t, :], heads(sq[:, t, :]), AX_X, ALU.add).then_inc(summed, 1)
                dve.wait_ge(rooted, 1)
                link(nc.vector.reciprocal(ms[:, :, :], ms[:, :, :]))
                for t in range(NT):
                    link(nc.vector.tensor_tensor(heads(o[:, t, :]), heads(o[:, t, :]),
                                                 ms[:, t, :].unsqueeze(2).to_broadcast([P, HEADS, P]), ALU.mult))
                    dve.wait_ge(gained, t + 1)
                    nc.vector.tensor_tensor(o[:, t, :], o[:, t, :], z[:, t, :], ALU.mult)


def gdn_layer(prog, inp):
    w_in = inp["gdn_w_in"][0]
    with ExitStack() as own:
        def new(name, shape, c=own):
            return prog.sbuf(name, shape, c)
        small = new("gdn_small", [P, 9, NCH * HEADS])
        tabs = [small[:, i, :].rearrange("p (c h) -> p c h", h=HEADS) for i in range(8)] + [small[:, 8, 0:HEADS]]
        g, beta, G, beG, kd, eL = tabs[:6]
        par = new("gdn_par", [P, 16 + P])
        with ExitStack() as mid:
            q, k = new("gdn_q", [P, HEADS, S], mid), new("gdn_k", [P, HEADS, S], mid)
            k_tok, v_tok = new("gdn_ktok", [P, NT, D], mid), new("gdn_vtok", [P, NT, D], mid)
            with ExitStack() as early:
                v = new("gdn_v", [P, HEADS, S], early)
                taps = new("gdn_taps", [P, 96], early)
                ba = new("gdn_ba", [P, NT, 2 * HEADS], early)
                load_stage(prog, "gdn_params", [(taps[:, :], inp["gdn_taps"]), (par[:, :], inp["gdn_par"])])
                gdn_conv(prog, "gdn_conv", [x[:, h, :] for x in (q, k, v) for h in range(HEADS)], taps)
                project(prog, "gdn_ba", prog.x_feat, KD,
                        [(0, 0, 2 * HEADS, t, 0, ba[:, t, :], None) for t in range(NT)])
                gdn_norms(prog, "gdn_norms", [(q[:, h, :], P ** -0.5) for h in range(HEADS)]
                          + [(k[:, h, :], 1.0) for h in range(HEADS)])
                gdn_gates(prog, "gdn_gates", ba, par, tabs)
                transpose_stage(prog, "gdn_turn", [([x[:, h, t * P:(t + 1) * P] for h in range(hh, hh + 4)],
                                                    y[:, t, hh * P:(hh + 4) * P])
                                                   for x, y in ((k, k_tok), (v, v_tok)) for t in range(NT) for hh in (0, 4)])
            for h0 in range(0, HEADS, HG):
                with ExitStack() as grp:
                    dec, att, am, inv, inv_t = (new(f"gdn_{n}{h0}", [P, HG, S], grp) for n in ("dec", "att", "am", "inv", "invt"))
                    gdn_decays(prog, f"gdn_decays{h0}", h0, q, k, g, G, dec, att, am)
                    gdn_inverse(prog, f"gdn_inverse{h0}", h0, beta, am, inv, inv_t, dec)
                    kb = new(f"gdn_kb{h0}", [P, HG, S], grp)
                    gdn_uw(prog, f"gdn_uw{h0}", h0, k_tok, v_tok, beta, beG, kd, inv_t, inv, kb, dec, am)
                    gdn_scan(prog, f"gdn_scan{h0}", h0, q, att, k_tok, eL, dec, am, prog.acc)
        z, o_feat = new("gdn_z", [P, NT, D]), new("gdn_ofeat", [P, KD, S])
        project(prog, "gdn_z", prog.x_feat, KD,
                [(c, 0, UP_COLS, t, 0, z[:, t, c * UP_COLS:(c + 1) * UP_COLS], ACT.Silu)
                 for c in range(4) for t in range(NT)])
        gdn_output_gate(prog, "gdn_gate", prog.acc, z, par[:, 16:16 + P])
        transpose_stage(prog, "gdn_turn_o", [([prog.acc[:, t, kk * P:(kk + 1) * P] for t in range(NT)], o_feat[:, kk, :])
                                             for kk in range(KD)])
        down_project(prog, "gdn_out", o_feat, inp["gdn_w_out"][0])



GROUPS, GC, GP = 64, 16, 64
PAIRS = GROUPS // 2
STEP = P // GC
NJ = S // STEP
TWO_PI = 2 * np.pi
MAGIC = 1.5 * 2.0 ** 23
TWO_PI_HI = 6.28125
TWO_PI_LO = TWO_PI - TWO_PI_HI
PI_IN = 3.1415925
GSTEP = 8


def reduce_angle(nc, link, x, tmp, shift=0.0):
    if shift:
        link(nc.vector.tensor_scalar(x, x, shift, None, ALU.add))
    link(nc.vector.tensor_scalar(tmp, x, 1.0 / TWO_PI, MAGIC, ALU.mult, ALU.add))
    link(nc.vector.tensor_scalar(tmp, tmp, MAGIC, None, ALU.subtract))
    link(nc.vector.scalar_tensor_tensor(out=x, in0=tmp, scalar=-TWO_PI_HI, in1=x, op0=ALU.mult, op1=ALU.add))
    link(nc.vector.scalar_tensor_tensor(out=x, in0=tmp, scalar=-TWO_PI_LO, in1=x, op0=ALU.mult, op1=ALU.add))
    link(nc.vector.tensor_scalar(x, x, PI_IN, -PI_IN, ALU.min, ALU.max))


def s5_tables(prog, name, lanes, taus, pow_re, pow_im, bbar, b):
    nc = prog.nc
    NTAU = STEP + 1
    with ExitStack() as own:
        w = prog.sbuf(name + "_w", [P, 12, PAIRS], own)
        ang = prog.sbuf(name + "_ang", [P, 3, NTAU, PAIRS], own)
        tmp_b = prog.sbuf(name + "_tb", [P, 4, PAIRS, GC], own)
        with Stage(prog, name) as st:
            link_sem, acted = st.counter("dve_link"), st.counter("acted")
            to_act = st.counter("to_act")
            lr, li, ldt = (lanes[:, i, :] for i in range(3))
            dt, xr, xi, t, em1, half, m1c, den, fr, fi, s0, s1 = (w[:, i, :] for i in range(12))
            mag, cos, tmp = (ang[:, i, :, :] for i in range(3))

            @st.scalar
            def _(act):
                nc.scalar.activation(dt, ldt, ACT.Exp).then_inc(acted, 1)
                act.wait_ge(to_act, 1)
                nc.scalar.activation(t, xr, ACT.Tanh, scale=0.5).then_inc(acted, 1)
                nc.scalar.activation(mag, mag, ACT.Exp).then_inc(acted, 1)
                act.wait_ge(to_act, 2)
                nc.scalar.activation(half, xi, ACT.Sin, scale=0.5).then_inc(acted, 1)
                nc.scalar.activation(pow_im, pow_im, ACT.Sin).then_inc(acted, 1)
                nc.scalar.activation(cos, cos, ACT.Sin).then_inc(acted, 1)

            @st.vector
            def _(dve):
                link = linker(dve, link_sem)
                tt, ts = nc.vector.tensor_tensor, nc.vector.tensor_scalar
                rep = [P, NTAU, PAIRS]
                dve.wait_ge(acted, 1)
                link(tt(xr, lr, dt, ALU.mult))
                link(tt(xi, li, dt, ALU.mult))
                tau = taus.unsqueeze(2).to_broadcast(rep)
                tt(mag, xr.unsqueeze(1).to_broadcast(rep), tau, ALU.mult).then_inc(to_act, 1)
                reduce_angle(nc, link, xi, s0)
                link(tt(pow_im, xi.unsqueeze(1).to_broadcast(rep), tau, ALU.mult))
                reduce_angle(nc, link, pow_im, tmp)
                link(nc.vector.tensor_copy(cos, pow_im))
                reduce_angle(nc, link, cos, tmp, np.pi / 2)
                nc.vector.memset(s1, 0.0).then_inc(to_act, 1)
                dve.wait_ge(acted, 6)
                link(tt(pow_re, mag, cos, ALU.mult))
                link(tt(pow_im, mag, pow_im, ALU.mult))
                link(ts(s0, t, -1.0, 1.0, ALU.mult, ALU.add))
                link(nc.vector.reciprocal(s0, s0))
                link(nc.vector.scalar_tensor_tensor(out=em1, in0=t, scalar=2.0, in1=s0, op0=ALU.mult, op1=ALU.mult))
                link(tt(m1c, em1, cos[:, 1, :], ALU.mult))
                link(tt(s0, half, half, ALU.mult))
                link(nc.vector.scalar_tensor_tensor(out=m1c, in0=s0, scalar=-2.0, in1=m1c, op0=ALU.mult, op1=ALU.add))
                link(tt(den, lr, lr, ALU.mult))
                link(tt(s0, li, li, ALU.mult))
                link(tt(den, den, s0, ALU.add))
                link(nc.vector.reciprocal(den, den))
                ai = pow_im[:, 1, :]
                link(tt(fr, m1c, lr, ALU.mult))
                link(tt(s0, ai, li, ALU.mult))
                link(tt(fr, fr, s0, ALU.add))
                link(tt(fr, fr, den, ALU.mult))
                link(tt(fi, ai, lr, ALU.mult))
                link(tt(s0, m1c, li, ALU.mult))
                link(tt(fi, fi, s0, ALU.subtract))
                link(tt(fi, fi, den, ALU.mult))
                rep = [P, PAIRS, GC]
                frb, fib = fr.unsqueeze(2).to_broadcast(rep), fi.unsqueeze(2).to_broadcast(rep)
                for i, (f, x) in enumerate(((frb, 0), (fib, 1), (frb, 1), (fib, 0))):
                    m = tt(tmp_b[:, i], b[:, x], f, ALU.mult)
                link(m)
                tt(bbar[:, 0], tmp_b[:, 0], tmp_b[:, 1], ALU.subtract)
                tt(bbar[:, 1], tmp_b[:, 2], tmp_b[:, 3], ALU.add)


def complex_powers(prog, name, x, pow_re, pow_im, out_re, out_im, taus, conj):
    nc = prog.nc
    with ExitStack() as own:
        tmp = prog.acc[:, 0:2, :].rearrange("p a (b q c) -> p a b q c", b=2, c=GC)
        with Stage(prog, name) as st:
            v_link, p_link = st.counter("dve_link"), st.counter("pool_link")

            def rep(p, tau):
                return p[:, tau, :].unsqueeze(2).to_broadcast([P, PAIRS, GC])

            @st.vector
            def _(dve):
                link = linker(dve, v_link)
                for tau, at in taus:
                    nc.vector.tensor_tensor(tmp[:, 0, 0], x[:, 0], rep(pow_re, tau), ALU.mult)
                    link(nc.vector.tensor_tensor(tmp[:, 0, 1], x[:, 1], rep(pow_im, tau), ALU.mult))
                    link(nc.vector.tensor_tensor(out_re[:, at], tmp[:, 0, 0], tmp[:, 0, 1], ALU.subtract))

            @st.gpsimd
            def _(pool):
                link = linker(pool, p_link)
                for tau, at in taus:
                    nc.gpsimd.tensor_tensor(tmp[:, 1, 0], x[:, 0], rep(pow_im, tau), ALU.mult)
                    link(nc.gpsimd.tensor_tensor(tmp[:, 1, 1], x[:, 1], rep(pow_re, tau), ALU.mult))
                    m = nc.gpsimd.tensor_tensor(out_im[:, at], tmp[:, 1, 0], tmp[:, 1, 1], ALU.add)
                    if conj:
                        link(m)
                        m = nc.gpsimd.tensor_scalar(out_im[:, at], out_im[:, at], -1.0, None, ALU.mult)
                    link(m)


def s5_layer(prog, inp):
    nc, ps, W = prog.nc, prog.ps, prog.weights
    u_dram, y_dram = prog.u_dram, prog.y_dram
    with ExitStack() as own:
        def new(name, shape, c=own):
            return prog.sbuf(name, shape, c)
        u_feat = new("s5_ufeat", [P, KD, STEP, NJ])
        par = new("s5_par", [P, KD + 3 * PAIRS + STEP + 1])
        d_skip = par[:, 0:KD]
        lanes = par[:, KD:KD + 3 * PAIRS].rearrange("p (a q) -> p a q", q=PAIRS)
        taus = par[:, KD + 3 * PAIRS:]
        with ExitStack() as core:
            bc_in = new("s5_bc", [P, 4, PAIRS, GC], core)
            bbar = new("s5_bbar", [P, 2, PAIRS, GC], core)
            pw = new("s5_pow", [P, 2, STEP + 1, PAIRS], core)
            a8 = new("s5_a8", [P, 2, 2, PAIRS], core)
            u_blk = new("s5_ublk", [P, GROUPS, NJ], core)
            he = new("s5_he", [P, 2, NJ * 2 * PAIRS], core)
            h_all = he[:, 0, :].rearrange("p (j r q) -> p j r q", r=2, q=PAIRS)
            e_all = he[:, 1, :].rearrange("p (j r q) -> p j r q", r=2, q=PAIRS)
            load_stage(prog, "s5_params", [(par[:, :], inp["s5_par"]), (bc_in[:, :, :, :], inp["s5_bc"])])
            project(prog, "s5_u", prog.x_feat, KD,
                    [(f // 2, (f % 2) * P, P, None, 0, u_feat[:, f].rearrange("p i j -> p j i"), None)
                     for f in range(KD)])
            s5_tables(prog, "s5_tables", lanes, taus, pw[:, 0], pw[:, 1], bbar, bc_in[:, 0:2])

            with Stage(prog, "s5_u_turn") as st:
                stored, landed = st.counter("stored"), st.counter("landed")
                a8_ready = st.counter("a8_ready")

                @st.sync
                def _(sp):
                    sp.dma_start(u_dram.rearrange("f p n -> p f n"), u_feat[:, :].rearrange("p f i j -> p f (i j)")
                                 ).then_inc(stored, 16)
                    sp.wait_ge(stored, 16)
                    src = u_dram.rearrange("f (g c) (i j) -> i c (f g) j", c=GC, j=NJ)
                    for i in range(STEP):
                        sp.dma_start(u_blk[i * GC:(i + 1) * GC, :, :], src[i]).then_inc(landed, 16)
                    sp.wait_ge(landed, 16 * STEP)

                @st.vector
                def _(dve):
                    for r in range(2):
                        nc.vector.tensor_copy(a8[:, 0, r, :], pw[:, 0, STEP, :]).then_inc(a8_ready, 1)
                    nc.vector.tensor_scalar(a8[:, 1, 0, :], pw[:, 1, STEP, :], -1.0, None, ALU.mult)
                    nc.vector.tensor_copy(a8[:, 1, 1, :], pw[:, 1, STEP, :])

            with ExitStack() as phase:
                into = new("s5_into", [P, 2, PAIRS, P], phase)
                p_t = he[:, :, :].rearrange("p r (q i c) -> p r q i c", q=PAIRS, c=GC)
                complex_powers(prog, "s5_in_powers", bbar, pw[:, 0], pw[:, 1],
                               p_t[:, 0].rearrange("p q i c -> p i q c"), p_t[:, 1].rearrange("p q i c -> p i q c"),
                               [(t, STEP - 1 - t) for t in range(STEP)], False)
                transpose_stage(prog, "s5_in_turn", [([p_t[:, r, q].rearrange("p i c -> p (i c)") for q in range(q0, q0 + 4)],
                                                      into[:, r, q0:q0 + 4, :])
                                                     for r in range(2) for q0 in range(0, PAIRS, 4)])
                with Stage(prog, "s5_inputs") as st:
                    product, act_c = st.counter("product"), st.counter("act_copied")

                    @st.tensor
                    def _(pe):
                        for r in range(2):
                            for b in range(4):
                                for q in range(8 * b, 8 * b + 8):
                                    for gp in range(2):
                                        m = nc.tensor.matmul(ps[gp * GP:(gp + 1) * GP, 4 * r + b, (q % 8) * NJ:(q % 8 + 1) * NJ],
                                                             into[:, r, q, gp * GP:(gp + 1) * GP], u_blk[:, 2 * q + gp, :],
                                                             start=True, stop=True)
                                m.then_inc(product, 1)

                    @st.scalar
                    def _(act):
                        for n in range(0, 8, 2):
                            act.wait_ge(product, n + 1)
                            nc.scalar.activation(e_all[:, :, n // 4, 8 * (n % 4):8 * (n % 4) + 8].rearrange("p j q -> p q j"),
                                                 ps[:, n, :].rearrange("p (q j) -> p q j", j=NJ), ACT.Copy)

                    @st.vector
                    def _(dve):
                        for n in range(1, 8, 2):
                            dve.wait_ge(product, n + 1)
                            nc.vector.tensor_copy(e_all[:, :, n // 4, 8 * (n % 4):8 * (n % 4) + 8].rearrange("p j q -> p q j"),
                                                  ps[:, n, :].rearrange("p (q j) -> p q j", j=NJ))
            with ExitStack() as phase:
                q_re, q_im = (new(f"s5_q{r}", [P, PAIRS, STEP + 1, GC], phase) for r in range(2))
                t12 = new("s5_t12", [P, 2, 2, PAIRS], phase)
                with Stage(prog, "s5_scan") as st:
                    link_sem = st.counter("dve_link")

                    @st.vector
                    def _(dve):
                        link = linker(dve, link_sem)
                        link(nc.vector.memset(h_all[:, 0], 0.0))
                        for j in range(NJ - 1):
                            h = h_all[:, j]
                            nc.vector.tensor_tensor(t12[:, 0], h, a8[:, 0], ALU.mult)
                            nc.vector.tensor_tensor(t12[:, 1, 0], h[:, 1], a8[:, 1, 0], ALU.mult)
                            link(nc.vector.tensor_tensor(t12[:, 1, 1], h[:, 0], a8[:, 1, 1], ALU.mult))
                            link(nc.vector.tensor_tensor(t12[:, 0], t12[:, 0], e_all[:, j], ALU.add))
                            link(nc.vector.tensor_tensor(h_all[:, j + 1], t12[:, 0], t12[:, 1], ALU.add))
                complex_powers(prog, "s5_out_powers", bc_in[:, 2:4], pw[:, 0], pw[:, 1],
                               q_re[:, :, :, :].rearrange("p q i c -> p i q c"), q_im[:, :, :, :].rearrange("p q i c -> p i q c"),
                               [(t, t) for t in range(STEP + 1)], True)
                s5_outputs(prog, "s5_outputs", bbar, q_re, q_im, u_blk, h_all, he[:, 1, :])
        s5_glu(prog, inp, u_feat, d_skip)


def s5_outputs(prog, name, bbar, q_re, q_im, u_blk, h_all, spare):
    nc, ps = prog.nc, prog.ps
    lag = spare[:, 0:2 * GSTEP * P].rearrange("p (b g n) -> p b g n", b=2, n=P)
    mix = spare[:, 2 * GSTEP * P:].rearrange("p (b g n) -> p b g n", b=2, n=P)
    y = prog.acc[:, :, :].rearrange("p t n -> p (t n)").rearrange("p (g j) -> p g j", j=NJ)
    NS = GROUPS // GSTEP

    def flat(x):
        return x.rearrange("p i c -> p (i c)")

    def of_parity(x, gp):
        return x.rearrange("p (g b) n -> p b g n", b=2)[:, gp]
    with Stage(prog, name) as st:
        zeroed, lag_ready, lag_copied = st.counter("zeroed"), st.counter("lag_ready"), st.counter("lag_copied")
        placed = [st.counter(f"placed_{b}") for b in range(2)]
        y_ready, y_copied = st.counter("y_ready"), st.counter("y_copied")

        @st.vector
        def _(dve):
            nc.vector.memset(mix, 0.0).then_inc(zeroed, 1)
            for s in range(NS):
                dve.wait_ge(lag_ready, s + 1)
                if s >= 2:
                    dve.wait_ge(placed[s % 2], 16 * STEP * (s // 2))
                for gp in range(2):
                    m = nc.vector.tensor_copy(of_parity(lag[0:GC, s % 2], gp),
                                              ps[0:GC, 2 * (s % 2) + gp, :].rearrange("p (g n) -> p g n", n=P))
                m.then_inc(lag_copied, 1)

        @st.sync
        def _(sp):
            sp.wait_ge(zeroed, 1)
            for s in range(NS):
                sp.wait_ge(lag_copied, s + 1)
                if s >= 2:
                    sp.wait_ge(y_ready, s - 1)
                for i in range(STEP):
                    n = (STEP - i) * GC
                    sp.dma_start(mix[i * GC:(i + 1) * GC, s % 2, :, i * GC:], lag[0:GC, s % 2, :, 0:n]
                                 ).then_inc(placed[s % 2], 16)

        @st.tensor
        def _(pe):
            def lags(s):
                if s >= 2:
                    pe.wait_ge(lag_copied, s - 1)
                for g in range(GSTEP):
                    q, gp = divmod(s * GSTEP + g, 2)
                    rows = slice(gp * GP, (gp + 1) * GP)
                    out = ps[0:GC, 2 * (s % 2) + gp, (g // 2) * P:(g // 2 + 1) * P]
                    nc.tensor.matmul(out, bbar[rows, 0, q, :], flat(q_re[rows, q, 0:STEP, :]), start=True, stop=False)
                    m = nc.tensor.matmul(out, bbar[rows, 1, q, :], flat(q_im[rows, q, 0:STEP, :]), start=False, stop=True)
                m.then_inc(lag_ready, 1)

            def outs(s):
                pe.wait_ge(placed[s % 2], 16 * STEP * (s // 2 + 1))
                if s >= 2:
                    pe.wait_ge(y_copied, s - 1)
                for g in range(GSTEP):
                    q, gp = divmod(s * GSTEP + g, 2)
                    rows = slice(gp * GP, (gp + 1) * GP)
                    out = ps[:, 4 + 2 * (s % 2) + gp, (g // 2) * NJ:(g // 2 + 1) * NJ]
                    nc.tensor.matmul(out, mix[:, s % 2, g, :], u_blk[:, 2 * q + gp, :], start=True, stop=False)
                    nc.tensor.matmul(out, flat(q_re[rows, q, 1:STEP + 1, :]), h_all[rows, :, 0, q], start=False, stop=False)
                    m = nc.tensor.matmul(out, flat(q_im[rows, q, 1:STEP + 1, :]), h_all[rows, :, 1, q], start=False, stop=True)
                m.then_inc(y_ready, 1)
            lags(0)
            for s in range(NS):
                if s + 1 < NS:
                    lags(s + 1)
                outs(s)

        @st.scalar
        def _(act):
            for s in range(NS):
                act.wait_ge(y_ready, s + 1)
                for gp in range(2):
                    m = nc.scalar.activation(of_parity(y[:, s * GSTEP:(s + 1) * GSTEP, :], gp),
                                             ps[:, 4 + 2 * (s % 2) + gp, 0:GSTEP // 2 * NJ].rearrange("p (g j) -> p g j", j=NJ),
                                             ACT.Copy)
                m.then_inc(y_copied, 1)


def s5_glu(prog, inp, u_feat, d_skip):
    nc, ps, W = prog.nc, prog.ps, prog.weights
    with ExitStack() as own:
        y_feat = prog.sbuf("s5_yfeat", [P, KD, STEP, NJ], own)
        hid = prog.sbuf("s5_hid", [P, KD, S], own)
        with Stage(prog, "s5_y_turn") as st:
            stored, landed, skipped = st.counter("stored"), st.counter("landed"), st.counter("skipped")

            @st.sync
            def _(sp):
                sp.dma_start(prog.y_dram, prog.acc[:, :, :].rearrange("p t n -> p (t n)")).then_inc(stored, 16)
                sp.wait_ge(stored, 16)
                src = prog.y_dram.rearrange("(i c) (f g j) -> f g c i j", c=GC, g=STEP, j=NJ)
                for f in range(KD):
                    for g in range(STEP):
                        sp.dma_start(y_feat[g * GC:(g + 1) * GC, f], src[f, g]).then_inc(landed, 16)
                sp.wait_ge(landed, 16 * KD * STEP)

        with Stage(prog, "s5_gelu") as st:
            skipped = st.counter("skipped")

            @st.vector
            def _(dve):
                for f in range(KD):
                    nc.vector.scalar_tensor_tensor(out=y_feat[:, f].rearrange("p i j -> p (i j)"),
                                                   in0=u_feat[:, f].rearrange("p i j -> p (i j)"),
                                                   scalar=d_skip[:, f:f + 1], in1=y_feat[:, f].rearrange("p i j -> p (i j)"),
                                                   op0=ALU.mult, op1=ALU.add).then_inc(skipped, 1)

            @st.scalar
            def _(act):
                for f in range(KD):
                    act.wait_ge(skipped, f + 1)
                    nc.scalar.activation(hid[:, f, :].rearrange("p (j i) -> p i j", i=STEP), y_feat[:, f], ACT.Gelu)

        sig = prog.sbuf("s5_sig", [P, 2, UP_COLS], own)
        with Stage(prog, "s5_glu") as st:
            product, gated = st.counter("product"), st.counter("gated")
            multiplied, summed = st.counter("multiplied"), st.counter("summed")
            NG = D // UP_COLS

            @st.tensor
            def _(pe):
                for c in range(NG):
                    w = [W.take(pe, "s5_glu", 2 * c + r) for r in range(2)]
                    for t in range(NT):
                        n = c * NT + t
                        if n >= 4:
                            pe.wait_ge(multiplied, n - 3)
                        for r in range(2):
                            for k in range(KD):
                                m = nc.tensor.matmul(ps[:, 2 * (n % 4) + r, 0:UP_COLS], hid[:, k, t * P:(t + 1) * P],
                                                     w[r][:, k, :], start=(k == 0), stop=(k == KD - 1))
                                if k == 0 and r == 1 and t == NT - 1:
                                    W.leave(m, "s5_glu", 2 * c)
                                if k == 0 and r == 0 and t == 0 and c:
                                    W.leave(m, "s5_glu", 2 * c - 1)
                            m.then_inc(product, 1)

            @st.scalar
            def _(act):
                for n in range(NG * NT):
                    act.wait_ge(product, 2 * n + 2)
                    if n >= 2:
                        act.wait_ge(summed, n - 1)
                    nc.scalar.activation(sig[:, n % 2, :], ps[:, 2 * (n % 4) + 1, 0:UP_COLS], ACT.Sigmoid).then_inc(gated, 1)

            @st.vector
            def _(dve):
                for n in range(NG * NT):
                    c, t = divmod(n, NT)
                    cs = slice(c * UP_COLS, (c + 1) * UP_COLS)
                    dve.wait_ge(gated, n + 1)
                    nc.vector.tensor_tensor(sig[:, n % 2, :], sig[:, n % 2, :], ps[:, 2 * (n % 4), 0:UP_COLS], ALU.mult
                                            ).then_inc(multiplied, 1)
                    dve.wait_ge(multiplied, n + 1)
                    nc.vector.scalar_tensor_tensor(out=prog.acc[:, t, cs], in0=prog.x_tok[:, t, cs], scalar=ALPHA,
                                                   in1=sig[:, n % 2, :], op0=ALU.mult, op1=ALU.add).then_inc(summed, 1)



def router(prog, inp, gates):
    nc, ps = prog.nc, prog.ps
    PAD = 2 * EXPERTS
    FILL, TAKEN = -3.0e38, -2.0e38
    with ExitStack() as own:
        w = prog.sbuf("moe_wr", [P, KD, EXPERTS], own)
        bias = prog.sbuf("moe_br", [P, EXPERTS], own)
        logit = prog.sbuf("moe_logit", [P, NT, PAD], own)
        left = prog.sbuf("moe_left", [P, NT, PAD], own)
        top = prog.sbuf("moe_top", [P, NT, 8], own)
        neg = prog.sbuf("moe_neg", [P, NT], own)
        den = prog.sbuf("moe_den", [P, NT], own)
        e = prog.sbuf("moe_e", [P, NT, EXPERTS], own)
        load_stage(prog, "moe_params", [(w[:, :, :], inp["moe_wr"]), (bias[:, :], inp["moe_br"])])
        with Stage(prog, "moe_router") as st:
            product, link_sem, neg_ready, exped = (st.counter(n) for n in ("product", "dve_link", "neg_ready", "exped"))

            @st.tensor
            def _(pe):
                for t in range(NT):
                    for k in range(KD):
                        m = nc.tensor.matmul(ps[:, t, 0:EXPERTS], prog.x_feat[:, k, t * P:(t + 1) * P], w[:, k, :],
                                             start=(k == 0), stop=(k == KD - 1))
                    m.then_inc(product, 1)

            @st.vector
            def _(dve):
                link = linker(dve, link_sem)
                nc.vector.memset(logit[:, :, EXPERTS:], FILL)
                for t in range(NT):
                    dve.wait_ge(product, t + 1)
                    m = nc.vector.tensor_tensor(logit[:, t, 0:EXPERTS], ps[:, t, 0:EXPERTS], bias[:, :], ALU.add)
                link(m)
                for t in range(NT):
                    m = nc.vector.max(top[:, t, :], logit[:, t, 0:EXPERTS])
                link(m)
                nc.vector.tensor_scalar(neg[:, :], top[:, :, 0], -1.0, None, ALU.mult).then_inc(neg_ready, 1)
                link(nc.vector.memset(top[:, :, 2:], FILL))
                for t in range(NT):
                    m = nc.vector.match_replace(left[:, t, :], top[:, t, :], logit[:, t, :], TAKEN)
                link(m)
                link(nc.vector.tensor_scalar(left[:, :, 0:EXPERTS], left[:, :, 0:EXPERTS], TAKEN, None, ALU.is_equal))
                dve.wait_ge(exped, NT)
                link(nc.vector.tensor_tensor(e[:, :, :], e[:, :, :], left[:, :, 0:EXPERTS], ALU.mult))
                link(nc.vector.tensor_reduce(den[:, :], e[:, :, :], AX_X, ALU.add))
                link(nc.vector.reciprocal(den[:, :], den[:, :]))
                nc.vector.tensor_tensor(gates[:, :, :], e[:, :, :], den[:, :].unsqueeze(2).to_broadcast([P, NT, EXPERTS]),
                                        ALU.mult)

            @st.scalar
            def _(act):
                act.wait_ge(neg_ready, 1)
                for t in range(NT):
                    nc.scalar.activation(e[:, t, :], logit[:, t, 0:EXPERTS], ACT.Exp, bias=neg[:, t:t + 1]).then_inc(exped, 1)


def moe_layer(prog, inp):
    with ExitStack() as own:
        gates = prog.sbuf("moe_gates", [P, NT, EXPERTS], own)
        router(prog, inp, gates)
        swiglu_parts(prog, "moe", EXPERTS, inp["moe_w1"][0], inp["moe_w3"][0], inp["moe_w2"][0], gates)



NEG = -1.0e30
A_HEADS, A_NOPE, A_ROPE, A_V = 6, 64, 32, 64
Q_LORA, KV_LORA = 768, 256
B_HEADS, C_HEADS, HD = 6, 4, 64
IDX_HEADS, IDX_DIM = 8, 64
TOPK = min(256, S // 4)
ROPE_THETA = 10000.0
DILATED = ((128, 1), (512, 4), (2048, 16))
A_SCALE, BC_SCALE = (A_NOPE + A_ROPE) ** -0.5, HD ** -0.5
SPLIT = (Q_LORA, KV_LORA, A_ROPE, B_HEADS * HD, B_HEADS * HD, B_HEADS * HD, C_HEADS * HD, C_HEADS * HD, C_HEADS * HD,
         IDX_HEADS * IDX_DIM, IDX_DIM, IDX_HEADS, D)
AT = [sum(SPLIT[:i]) for i in range(len(SPLIT) + 1)]
N_BIAS = 1 + B_HEADS + C_HEADS


def attention_constants():
    dist = np.arange(P)[:, None] + (S - P) - np.arange(S)[None, :]
    causal = np.where(dist >= 0, 0.0, NEG)
    slopes = 2.0 ** (-8.0 * np.arange(1, B_HEADS + C_HEADS + 1) / (B_HEADS + C_HEADS))
    count = sum(((dist >= 0) & (dist <= w) & (dist % d == 0)).astype(np.float64) for w, d in DILATED)
    windows = np.where(count > 0, np.log(np.maximum(count, 1)), NEG)
    tables = [causal / A_SCALE]
    tables += [(windows - s * dist * (count > 0)) / BC_SCALE for s in slopes[:B_HEADS]]
    tables += [(causal - s * dist * (dist >= 0)) / BC_SCALE for s in slopes[B_HEADS:]]
    half = A_ROPE // 2
    freqs = ROPE_THETA ** (-np.arange(0, A_ROPE, 2) / A_ROPE)
    angle = (np.arange(S, dtype=np.float32)[None, :] * np.tile(freqs, 2).astype(np.float32)[:, None]).astype(np.float32)
    rot = np.zeros((A_ROPE, A_ROPE))
    for m in range(half):
        rot[m + half, m] = -1.0
        rot[m, m + half] = 1.0
    rope = np.zeros((P, 2 * S + A_ROPE))
    rope[A_NOPE:A_NOPE + A_ROPE] = np.concatenate([np.cos(angle), np.sin(angle), rot], axis=1)
    return np.stack(tables, axis=1).astype(np.float32), rope.astype(np.float32)


def in_columns():
    names = ("cq", "ckv", "kr", "qb", "kb", "vb", "qc", "kc", "vc", "qi", "ki", "wi", "gate")
    order = ("cq", "ckv", "kr", "qb", "kb", "qc", "kc", "qi", "ki", "vb", "vc", "wi", "gate")
    out = []
    for n in order:
        a, b = AT[names.index(n)], AT[names.index(n) + 1]
        out += [(n, c - a, c, min(c + UP_COLS, b)) for c in range(a, b, UP_COLS)]
    return out


def plan_attention(W, inp, l):
    w_in = inp["w_in_2"][l]
    W.plan(f"ada{l}", col_tiles(inp["w_ada_2"][l], UP_COLS))
    W.plan(f"in{l}", [w_in[:, c0:c1].rearrange("(k p) n -> p k n", p=P) for _, _, c0, c1 in in_columns()])
    W.plan(f"uq{l}", col_tiles(inp["w_uq_2"][l], 3 * (A_NOPE + A_ROPE)))
    W.plan(f"ukv{l}", col_tiles(inp["w_uk_2"][l], A_HEADS * A_NOPE) + col_tiles(inp["w_uv_2"][l], A_HEADS * A_V))


def modulation(prog, name, par, gate):
    nc, ps, W = prog.nc, prog.ps, prog.weights
    with ExitStack() as own:
        sc = prog.sbuf(name + "_sc", [P, KD], own)
        mod = prog.sbuf(name + "_mod", [P, 2 * KD], own)
        with Stage(prog, name) as st:
            activated, vector_ready, gate_ready = st.counter("activated"), st.counter("vector_ready"), st.counter("gate_ready")
            link_sem = st.counter("dve_link")

            @st.scalar
            def _(act):
                nc.scalar.activation(sc[:, :], par[:, 0:KD], ACT.Silu).then_inc(activated, 1)

            @st.tensor
            def _(pe):
                pe.wait_ge(activated, 1)
                for j in range(12):
                    w = W.take(pe, name, j)
                    if j < 8:
                        for h in range(2):
                            n = 2 * j + h
                            for k in range(KD):
                                m = nc.tensor.matmul(ps[:, 0, n:n + 1], w[:, k, h * P:(h + 1) * P], sc[:, k:k + 1],
                                                     start=(k == 0), stop=(k == KD - 1))
                                if j and h == 0 and k == 0:
                                    W.leave(m, name, j - 1)
                        if j == 7:
                            m.then_inc(vector_ready, 1)
                    else:
                        for k in range(KD):
                            m = nc.tensor.matmul(ps[:, 1 + (j - 8) // 2, (j % 2) * UP_COLS:(j % 2 + 1) * UP_COLS],
                                                 bc(sc[:, k:k + 1], [P, P]), w[:, k, :], start=(k == 0), stop=(k == KD - 1))
                            if k == 0:
                                W.leave(m, name, j - 1)
                m.then_inc(gate_ready, 1)

            @st.vector
            def _(dve):
                link = linker(dve, link_sem)
                dve.wait_ge(vector_ready, 1)
                link(nc.vector.tensor_tensor(mod[:, :], ps[:, 0, 0:2 * KD], par[:, KD:3 * KD], ALU.add))
                link(nc.vector.tensor_scalar(mod[:, KD:], mod[:, KD:], 1.0, None, ALU.add))
                for k in range(KD):
                    nc.vector.tensor_scalar(prog.x_feat[:, k, :], prog.x_feat[:, k, :], mod[:, KD + k:KD + k + 1],
                                            mod[:, k:k + 1], ALU.mult, ALU.add)
                dve.wait_ge(gate_ready, 1)
                for h in range(2):
                    cs = slice(h * BANK, (h + 1) * BANK)
                    nc.vector.tensor_tensor(gate[:, cs], ps[:, 1 + h, :], par[:, 3 * KD + h * BANK:3 * KD + (h + 1) * BANK],
                                            ALU.add)


def latent_norms(prog, name, c_all, g):
    nc, ps = prog.nc, prog.ps
    nq = Q_LORA // P
    sq, rs = (prog.scratch[:, i * 2 * S:(i + 1) * 2 * S].rearrange("p (a n) -> p a n", a=2) for i in range(2))
    with Stage(prog, name) as st:
        squared, summed, part_done = st.counter("squared"), st.counter("summed"), st.counter("part_done")
        rooted, link_sem = st.counter("rooted"), st.counter("dve_link")

        @st.gpsimd
        def _(pool):
            for k in range(KD):
                if k >= 2:
                    pool.wait_ge(summed, k - 1)
                nc.gpsimd.tensor_tensor(sq[:, k % 2, :], c_all[:, k, :], c_all[:, k, :], ALU.mult).then_inc(squared, 1)

        @st.tensor
        def _(pe):
            for k in range(KD):
                pe.wait_ge(squared, k + 1)
                nc.tensor.matmul(ps[:, int(k >= nq), :], prog.ones, sq[:, k % 2, :], start=k in (0, nq),
                                 stop=k in (nq - 1, KD - 1)).then_inc(summed, 1)

        @st.scalar
        def _(act):
            for i, (k, n) in enumerate(((nq, Q_LORA), (KD, KV_LORA))):
                act.wait_ge(summed, k)
                nc.scalar.activation(rs[:, i, :], ps[:, i, :], ACT.Sqrt, scale=1.0 / n, bias=prog.eps_norm
                                     ).then_inc(rooted, 1)

        @st.vector
        def _(dve):
            link = linker(dve, link_sem)
            for i, ks in enumerate((range(nq), range(nq, KD))):
                dve.wait_ge(rooted, i + 1)
                link(nc.vector.reciprocal(rs[:, i, :], rs[:, i, :]))
                dve.wait_ge(summed, ks[-1] + 1)
                for k in ks:
                    nc.vector.scalar_tensor_tensor(out=c_all[:, k, :], in0=c_all[:, k, :], scalar=g[:, k:k + 1],
                                                   in1=rs[:, i, :], op0=ALU.mult, op1=ALU.mult)


def rotate(prog, name, rope, qa, ka, kr):
    nc, ps = prog.nc, prog.ps
    rows = slice(A_NOPE, A_NOPE + A_ROPE)
    cos, sin, rot = rope[rows, 0:S], rope[rows, S:2 * S], rope[rows, 2 * S:]
    xs = [kr[rows, :]] + [qa[rows, h, :] for h in range(A_HEADS)]
    tmp = prog.scratch[:, 0:2 * S].rearrange("p (a n) -> p a n", a=2)
    with Stage(prog, name) as st:
        turned, cosined, sined, rotated = (st.counter(n) for n in ("turned", "cosined", "sined", "rotated"))

        @st.tensor
        def _(pe):
            for i, x in enumerate(xs):
                nc.tensor.matmul(ps[rows, i, :], rot, x, start=True, stop=True).then_inc(turned, 1)

        @st.gpsimd
        def _(pool):
            for i, x in enumerate(xs):
                pool.wait_ge(turned, i + 1)
                nc.gpsimd.tensor_tensor(x, x, cos, ALU.mult).then_inc(cosined, 1)

        @st.vector
        def _(dve):
            for i, x in enumerate(xs):
                dve.wait_ge(turned, i + 1)
                if i >= 2:
                    dve.wait_ge(rotated, i - 1)
                nc.vector.tensor_tensor(tmp[rows, i % 2, :], ps[rows, i, :], sin, ALU.mult).then_inc(sined, 1)
                dve.wait_ge(sined, i + 1)
                dve.wait_ge(cosined, i + 1)
                nc.vector.tensor_tensor(x, x, tmp[rows, i % 2, :], ALU.add).then_inc(rotated, 1)

        @st.scalar
        def _(act):
            act.wait_ge(rotated, 1)
            for h in range(A_HEADS):
                nc.scalar.activation(ka[rows, h, :], kr[rows, :], ACT.Copy)


def index_select(prog, name, qi, ki, wi, causal, sel):
    nc, ps = prog.nc, prog.ps
    TAKEN = -3.0e38
    relu, score = (prog.scratch[:, i * 2 * S:(i + 1) * 2 * S].rearrange("p (a n) -> p a n", a=2) for i in range(2))
    with ExitStack() as own:
        top = prog.sbuf(name + "_top", [P, 2, 8], own)
        with Stage(prog, name) as st:
            product, relued, summed = st.counter("product"), st.counter("relued"), st.counter("summed")
            link_sem = st.counter("dve_link")
            tiles = range(1, NT)

            @st.tensor
            def _(pe):
                for n, (t, i) in enumerate((t, i) for t in tiles for i in range(IDX_HEADS)):
                    rows = slice((i % 2) * IDX_DIM, (i % 2 + 1) * IDX_DIM)
                    if n >= IDX_HEADS:
                        pe.wait_ge(relued, n - IDX_HEADS + 1)
                    nc.tensor.matmul(ps[:, i, 0:(t + 1) * P], qi[rows, i // 2, t * P:(t + 1) * P], ki[rows, 0:(t + 1) * P],
                                     start=True, stop=True).then_inc(product, 1)

            @st.scalar
            def _(act):
                for n, (t, i) in enumerate((t, i) for t in tiles for i in range(IDX_HEADS)):
                    act.wait_ge(product, n + 1)
                    if n >= 2:
                        act.wait_ge(summed, n - 1)
                    nc.scalar.activation(relu[:, n % 2, 0:(t + 1) * P], ps[:, i, 0:(t + 1) * P], ACT.Relu,
                                         scale=IDX_DIM ** -0.5).then_inc(relued, 1)

            @st.vector
            def _(dve):
                link = linker(dve, link_sem)
                link(nc.vector.tensor_scalar(wi[:, :, :], wi[:, :, :], IDX_HEADS ** -0.5, None, ALU.mult))
                n = 0
                for t in tiles:
                    w = (t + 1) * P
                    x, y = score[:, 0, 0:w], score[:, 1, 0:w]
                    for i in range(IDX_HEADS):
                        before = causal[:, S - w:S] if i == 0 else x
                        dve.wait_ge(relued, n + 1)
                        if n:
                            dve.wait_ge(summed, n)
                        nc.vector.scalar_tensor_tensor(out=x, in0=relu[:, n % 2, 0:w], scalar=wi[:, t, i:i + 1], in1=before,
                                                       op0=ALU.mult, op1=ALU.add).then_inc(summed, 1)
                        n += 1
                    dve.wait_ge(summed, n)
                    for r in range(TOPK // 8):
                        link(nc.vector.max(top[:, 0, :], x))
                        link(nc.vector.match_replace(y, top[:, 0, :], x, TAKEN))
                        x, y = y, x
                    link(nc.vector.tensor_scalar(sel[:, t, 0:w], x, TAKEN / 2, NEG, ALU.is_gt, ALU.mult))


def attend(prog, name, heads, bias, sel, gate, y):
    nc, ps = prog.nc, prog.ps
    units = [(h, t) for h in range(len(heads)) for t in range(NT)]
    U = len(units)
    with ExitStack() as own:
        s_sb = prog.sbuf(name + "_s", [P, 3, S], own)
        p_t = prog.sbuf(name + "_pt", [P, 2, S], own)
        small = prog.sbuf(name + "_small", [P, 4, 4], own)
        with Stage(prog, name) as st:
            s_ready, s_read, neg_ready, p_ready, pt_ready, pt_copied, o_ready, o_read, link_sem, p_read = (
                st.counter(n) for n in ("s_ready", "s_read", "neg_ready", "p_ready", "pt_ready", "pt_copied",
                                       "o_ready", "o_read", "dve_link", "p_read"))

            def keys(u):
                return (units[u][1] + 1) * P

            @st.tensor
            def _(pe):
                def scores(u):
                    h, t = units[u]
                    q, k = heads[h][0], heads[h][1]
                    if u >= 3:
                        pe.wait_ge(s_read, u - 2)
                    nc.tensor.matmul(ps[:, u % 3, 0:keys(u)], q(t * P, (t + 1) * P), k(0, keys(u)), start=True, stop=True
                                     ).then_inc(s_ready, 1)

                def turn(u):
                    pe.wait_ge(p_ready, u + 1)
                    if u >= 2:
                        pe.wait_ge(pt_copied, u - 1)
                    for b in range(keys(u) // P):
                        m = nc.tensor.transpose(ps[:, 3 + u % 2, b * P:(b + 1) * P], s_sb[:, u % 3, b * P:(b + 1) * P],
                                                prog.ident)
                    m.then_inc(pt_ready, 1)

                def values(u):
                    pe.wait_ge(pt_copied, u + 1)
                    if u >= 2:
                        pe.wait_ge(o_read, u - 1)
                    v = heads[units[u][0]][2]
                    nb = keys(u) // P
                    for b in range(nb):
                        m = nc.tensor.matmul(ps[:, 5 + u % 2, 0:HD], p_t[:, u % 2, b * P:(b + 1) * P], v(b),
                                             start=(b == 0), stop=(b == nb - 1))
                    m.then_inc(o_ready, 1)
                for step in range(U + 2):
                    if step < U:
                        scores(step)
                    if 1 <= step <= U:
                        turn(step - 1)
                    if step >= 2:
                        values(step - 2)

            @st.vector
            def _(dve):
                link = linker(dve, link_sem)

                def read_scores(u):
                    h, t = units[u]
                    w, scale, selected = keys(u), heads[h][3], heads[h][5]
                    x, mx, neg = s_sb[:, u % 3, 0:w], small[:, u % 4, 0:1], small[:, u % 4, 1:2]
                    table = bias[:, heads[h][4], S - w:S]
                    dve.wait_ge(s_ready, u + 1)
                    if u >= 3:
                        dve.wait_ge(pt_ready, u - 2)
                    if u >= 4:
                        dve.wait_ge(o_read, u - 3)
                    if selected and t > 0:
                        nc.vector.tensor_tensor(x, ps[:, u % 3, 0:w], table, ALU.add).then_inc(s_read, 1)
                        dve.wait_ge(s_read, u + 1)
                        link(nc.vector.tensor_tensor_reduce(out=x, in0=x, in1=sel[:, t, 0:w], scale=1.0, scalar=-3.0e38,
                                                            op0=ALU.add, op1=ALU.max, accum_out=mx))
                    else:
                        nc.vector.tensor_tensor_reduce(out=x, in0=ps[:, u % 3, 0:w], in1=table, scale=1.0, scalar=-3.0e38,
                                                       op0=ALU.add, op1=ALU.max, accum_out=mx).then_inc(s_read, 1)
                        dve.wait_ge(s_read, u + 1)
                    nc.vector.tensor_scalar(neg, mx, -scale, None, ALU.mult).then_inc(neg_ready, 1)

                def output(u):
                    h, t = units[u]
                    den, inv = small[:, u % 4, 2:3], small[:, u % 4, 3:4]
                    cs = slice(h * HD, (h + 1) * HD)
                    dve.wait_ge(p_ready, u + 1)
                    link(nc.vector.reciprocal(inv, den))
                    dve.wait_ge(o_ready, u + 1)
                    nc.vector.scalar_tensor_tensor(out=y[:, t, cs], in0=ps[:, 5 + u % 2, 0:HD], scalar=inv,
                                                   in1=gate[:, t, cs], op0=ALU.mult, op1=ALU.mult).then_inc(o_read, 1)
                for step in range(U + 2):
                    if step < U:
                        read_scores(step)
                    if step >= 2:
                        output(step - 2)

            @st.scalar
            def _(act):
                for step in range(U + 1):
                    if step < U:
                        u = step
                        x = s_sb[:, u % 3, 0:keys(u)]
                        act.wait_ge(neg_ready, u + 1)
                        nc.scalar.activation(x, x, ACT.Exp, bias=small[:, u % 4, 1:2], scale=heads[units[u][0]][3],
                                             accum_out=small[:, u % 4, 2:3]).then_inc(p_ready, 1)
                    if step >= 1:
                        u = step - 1
                        act.wait_ge(pt_ready, u + 1)
                        if u >= 2:
                            act.wait_ge(o_ready, u - 1)
                        nc.scalar.activation(p_t[:, u % 2, 0:keys(u)], ps[:, 3 + u % 2, 0:keys(u)], ACT.Copy
                                             ).then_inc(pt_copied, 1)


def attention_layer(prog, inp, l, last):
    def new(name, shape, c):
        return prog.sbuf(f"{name}_{l}", shape, c)
    with ExitStack() as own:
        mod_gate = new("mod_gate", [P, D], own)
        with ExitStack() as heads_ctx:
            qa, ka = new("qa", [P, A_HEADS, S], heads_ctx), new("ka", [P, A_HEADS, S], heads_ctx)
            va, vb = new("va", [P, NT, A_HEADS * A_V], heads_ctx), new("vb", [P, NT, B_HEADS * HD], heads_ctx)
            vc = new("vc", [P, NT, C_HEADS * HD], heads_ctx)
            qb, kb = (new(n, [P, B_HEADS // 2, S], heads_ctx) for n in ("qb", "kb"))
            qc, kc = (new(n, [P, C_HEADS // 2, S], heads_ctx) for n in ("qc", "kc"))
            gate, sel = new("gate", [P, NT, D], heads_ctx), new("sel", [P, NT, S], heads_ctx)
            with ExitStack() as early:
                par = new("par", [P, 4 * KD + D], early)
                load_stage(prog, f"att_params{l}", [(par[:, :], inp["att_par"][l])])
                modulation(prog, f"ada{l}", par, mod_gate)
            with ExitStack() as early:
                c_all = new("c_all", [P, KD, S], early)
                qi, ki = new("qi", [P, IDX_HEADS // 2, S], early), new("ki", [P, S], early)
                wi, g = new("wi", [P, NT, IDX_HEADS], early), new("lat_g", [P, KD], early)
                kr = new("kr", [P, S], early)
                feat = {"cq": c_all, "ckv": c_all[:, Q_LORA // P:, :], "qb": qb, "kb": kb, "qc": qc, "kc": kc, "qi": qi}
                groups = []
                for i, (part, at, c0, c1) in enumerate(in_columns()):
                    n = c1 - c0
                    if part in feat:
                        groups += [(i, c, P, None, 0, feat[part][:, (at + c) // P, :], None) for c in range(0, n, P)]
                    elif part == "kr":
                        groups.append((i, 0, A_ROPE, None, A_NOPE, kr[A_NOPE:A_NOPE + A_ROPE, :], None))
                    elif part == "ki":
                        groups += [(i, 0, IDX_DIM, None, r, ki[r:r + IDX_DIM, :], None) for r in (0, IDX_DIM)]
                    else:
                        dst, func = {"vb": (vb, None), "vc": (vc, None), "wi": (wi, None), "gate": (gate, ACT.Silu)}[part]
                        groups += [(i, 0, n, t, 0, dst[:, t, at:at + n], func) for t in range(NT)]
                project(prog, f"in{l}", prog.x_feat, KD, groups)
                load_stage(prog, f"lat_params{l}", [(g[:, :], inp["lat_g"][l])])
                latent_norms(prog, f"lat{l}", c_all, g)
                project(prog, f"uq{l}", c_all[:, 0:Q_LORA // P, :], Q_LORA // P,
                        [(h // 3, (h % 3) * (A_NOPE + A_ROPE), A_NOPE + A_ROPE, None, 0, qa[0:A_NOPE + A_ROPE, h, :], None)
                         for h in range(A_HEADS)])
                project(prog, f"ukv{l}", c_all[:, Q_LORA // P:, :], KV_LORA // P,
                        [(0, h * A_NOPE, A_NOPE, None, 0, ka[0:A_NOPE, h, :], None) for h in range(A_HEADS)]
                        + [(1, 0, A_HEADS * A_V, t, 0, va[:, t, :], None) for t in range(NT)])
                rope, causal = prog.scratch[:, 4 * S:6 * S + A_ROPE], prog.scratch[:, 7 * S:8 * S]
                load_stage(prog, f"tables_in{l}", [(rope, inp["rope"]), (causal, inp["bias"][:, 0, :])])
                rotate(prog, f"rope{l}", rope, qa, ka, kr)
                index_select(prog, f"index{l}", qi, ki, wi, causal, sel)
            with ExitStack() as late:
                bias = new("bias", [P, N_BIAS, S], late)
                load_stage(prog, f"bias_in{l}", [(bias[:, :, :], inp["bias"])])

                def cols(x, rows, h):
                    return lambda a, b: x[rows, h, a:b]

                def vals(x, h):
                    return lambda b: x[:, b, h * HD:(h + 1) * HD]
                full = slice(0, A_NOPE + A_ROPE)
                heads = [(cols(qa, full, h), cols(ka, full, h), vals(va, h), A_SCALE, 0, False) for h in range(A_HEADS)]
                for q, k, v, n, b0, s in ((qb, kb, vb, B_HEADS, 1, False), (qc, kc, vc, C_HEADS, 1 + B_HEADS, True)):
                    for h in range(n):
                        rows = slice((h % 2) * HD, (h % 2 + 1) * HD)
                        heads.append((cols(q, rows, h // 2), cols(k, rows, h // 2), vals(v, h), BC_SCALE, b0 + h, s))
                attend(prog, f"attend{l}", heads, bias, sel, gate, prog.acc)
        transpose_stage(prog, f"att_turn{l}", [([prog.acc[:, t, k * P:(k + 1) * P] for t in range(NT)], prog.x_feat[:, k, :])
                                               for k in range(KD)])
        down_project(prog, f"att_out{l}", prog.x_feat, inp["w_out_2"][l], mod_gate)
        layer_norm(prog, f"att_ln{l}", inp["ln_gb"][4 + l], last)


BIG = ["x", "gdn_w_in", "gdn_w_out", "ffn_w1", "ffn_w3", "ffn_w2", "s5_w_in", "s5_w_glu", "moe_w1", "moe_w3", "moe_w2",
       "w_ada_2", "w_in_2", "w_uq_2", "w_uk_2", "w_uv_2", "w_out_2"]


def plan_rest(prog, W, inp, plan_swiglu):
    W.plan("s5_u", col_tiles(inp["s5_w_in"][0], UP_COLS))
    glu = col_tiles(inp["s5_w_glu"][0], UP_COLS)
    W.plan("s5_glu", [t for pair in zip(glu[:D // UP_COLS], glu[D // UP_COLS:]) for t in pair])
    plan_swiglu("moe", inp["moe_w1"][0], inp["moe_w3"][0], EXPERTS)
    for l in range(DEPTH):
        plan_attention(W, inp, l)
    prog.u_dram = prog.nc.dram_tensor("u_turn", (KD, P, S), F32).ap()
    prog.y_dram = prog.nc.dram_tensor("y_turn", (P, GROUPS * NJ), F32).ap()


def rest_steps(prog, inp):
    return [lambda: s5_layer(prog, inp),
            lambda: layer_norm(prog, "s5_ln", inp["ln_gb"][2]),
            lambda: moe_layer(prog, inp),
            lambda: layer_norm(prog, "moe_ln", inp["ln_gb"][3]),
            lambda: attention_layer(prog, inp, 0, False),
            lambda: attention_layer(prog, inp, 1, True)]


def lay_out_rest(f, arr, rep):
    def lanes(a):
        a = a.reshape((PAIRS, 2, GP) + a.shape[2:])
        return np.moveaxis(a, 0, 2).reshape((P, PAIRS) + a.shape[3:])
    vec = [lanes(f["s5_lam_re"][0]), lanes(f["s5_lam_im"][0]),
           lanes(np.broadcast_to(f["s5_log_dt"][0][:, None], (GROUPS, GP)))]
    arr["s5_par"] = np.concatenate([f["s5_d"][0].reshape(KD, P).T] + vec + [rep(np.arange(STEP + 1, dtype=np.float32))], axis=1)
    arr["s5_bc"] = np.stack([lanes(f["s5_b_re"][0]), lanes(f["s5_b_im"][0]),
                             lanes(f["s5_c_re"][0].transpose(0, 2, 1)), lanes(f["s5_c_im"][0].transpose(0, 2, 1))], axis=1)
    arr["moe_wr"] = f["moe_w_router"][0].reshape(KD, P, EXPERTS).transpose(1, 0, 2)
    arr["moe_br"] = rep(f["moe_b_router"][0])

    def feat(a):
        return a.reshape(-1, P).T
    arr["att_par"] = np.stack([np.concatenate([feat(f["c_2"][0]), feat(f["b_ada_2"][l, 0:2 * D]), rep(f["b_ada_2"][l, 2 * D:]),
                                               np.zeros((P, KD), np.float32)], axis=1) for l in range(DEPTH)])
    arr["lat_g"] = np.stack([np.concatenate([feat(f["q_norm_g_2"][l]), feat(f["kv_norm_g_2"][l])], axis=1)
                             for l in range(DEPTH)])
    arr["bias"], arr["rope"] = attention_constants()



def constants():
    i = np.arange(P)
    ident = np.eye(P)
    ones = np.ones((P, P))
    tri = (i[:, None] <= i[None, :]) * 1.0
    levels = []
    for level in range(LEVELS):
        b = 1 << level
        s, c = i[:, None], i[None, :]
        levels.append((s // (2 * b) == c // (2 * b)) & (s % (2 * b) < b) & (c % (2 * b) >= b))
    return np.concatenate([ident, ones, tri] + [m * 1.0 for m in levels], axis=1).astype(np.float32)


def build(nc, inp, out):
    with ExitStack() as ctx:
        prog = Program(nc, ctx)
        prog.out = out
        prog.ps = ctx.enter_context(nc.psum_tensor("ps", [P, 8, BANK], F32))
        ring = prog.sbuf("ring", [P, RING, RING_COLS])
        loaded = [ctx.enter_context(nc.semaphore(f"weights_loaded_{i}")) for i in range(RING)]
        used = ctx.enter_context(nc.semaphore("weights_used"))
        W = prog.weights = Weights(ring, loaded, used)
        prog.x_tok = prog.sbuf("x_tok", [P, NT, D])
        prog.x_feat = prog.sbuf("x_feat", [P, KD, S])
        prog.acc = prog.sbuf("acc", [P, NT, D])
        prog.scratch = prog.acc[:, :, :].rearrange("p t n -> p (t n)")
        cst = prog.sbuf("cst", [P, (3 + LEVELS) * P])
        prog.ident, prog.ones, prog.tri = (cst[:, i * P:(i + 1) * P] for i in range(3))
        prog.level_masks = cst[:, 3 * P:(3 + LEVELS) * P].rearrange("p (l n) -> p l n", n=P)
        eps = prog.sbuf("eps", [P, 2])
        prog.eps_norm, prog.eps_qk = eps[:, 0:1], eps[:, 1:2]

        w_in = inp["gdn_w_in"][0]
        QKV = 3 * HEADS * P
        W.plan("gdn_conv", col_tiles(w_in[:, 0:QKV], UP_COLS))
        W.plan("gdn_ba", col_tiles(w_in[:, QKV + D:QKV + D + 2 * HEADS], UP_COLS))
        W.plan("gdn_z", col_tiles(w_in[:, QKV:QKV + D], UP_COLS))

        def plan_swiglu(name, w1, w3, parts):
            srcs = []
            for e in range(parts):
                for a, b in zip(col_tiles(w1[e], UP_COLS), col_tiles(w3[e], UP_COLS)):
                    srcs += [a, b]
            W.plan(name, srcs, align=True)
        ffn1, ffn3 = (inp[n][0].rearrange("k (e n) -> e k n", n=FF_PART) for n in ("ffn_w1", "ffn_w3"))
        ffn2 = inp["ffn_w2"][0].rearrange("(e k) n -> e k n", k=FF_PART)
        plan_swiglu("ffn", ffn1, ffn3, 2)
        plan_rest(prog, W, inp, plan_swiglu)

        with Stage(prog, "setup") as st:
            landed, eps_set = st.counter("landed"), st.counter("eps_set")

            @st.sync
            def _(sp):
                sp.dma_start(prog.x_tok[:, :, :], inp["x"][0].rearrange("(t p) n -> p t n", p=P)).then_inc(landed, 16)
                sp.dma_start(cst[:, :], inp["cst"]).then_inc(landed, 16)
                sp.wait_ge(landed, 32)

            @st.gpsimd
            def _(pool):
                nc.gpsimd.memset(eps[:, 0:1], NORM_EPS)
                nc.gpsimd.memset(eps[:, 1:2], NORM_EPS * P)
        turn_x = [([prog.x_tok[:, t, k * P:(k + 1) * P] for t in range(NT)], prog.x_feat[:, k, :]) for k in range(KD)]
        transpose_stage(prog, "setup_turn", turn_x)

        steps = [
            lambda: gdn_layer(prog, inp),
            lambda: layer_norm(prog, "gdn_ln", inp["ln_gb"][0]),
            lambda: swiglu_parts(prog, "ffn", 2, ffn1, ffn3, ffn2),
            lambda: layer_norm(prog, "ffn_ln", inp["ln_gb"][1]),
        ] + rest_steps(prog, inp)
        for step in steps:
            step()



def lay_out(inputs):
    f = {n: np.ascontiguousarray(np.asarray(a)) for n, a in inputs.items()}
    arr = {n: f[n] for n in BIG}

    def rep(a):
        return np.broadcast_to(a, (P,) + a.shape)
    taps = f["gdn_conv_w"][0].T.reshape(3 * HEADS, P, 4).transpose(1, 0, 2).reshape(P, -1)
    arr["gdn_taps"] = taps
    arr["gdn_par"] = rep(np.concatenate([f["gdn_dt_bias"][0], f["gdn_a_log"][0], f["gdn_norm_g"][0]]))
    gb = np.stack([f["ln_g"].reshape(4, D), f["ln_b"].reshape(4, D)], axis=1)
    gb2 = np.stack([f["ln_g_2"], f["ln_b_2"]], axis=1)
    arr["ln_gb"] = np.stack([rep(a) for a in np.concatenate([gb, gb2])])
    arr["cst"] = constants()
    lay_out_rest(f, arr, rep)
    return {n: np.ascontiguousarray(a) for n, a in arr.items()}


def kernel(**inputs):
    import concourse.bacc as bacc
    from concourse.bass_utils import run_bass_kernel_spmd

    nc = bacc.Bacc("TRN2", target_bir_lowering=False, num_devices=1)
    arrays = {f"in_{n}": a for n, a in lay_out(inputs).items()}
    inp = {n[3:]: nc.dram_tensor(n, a.shape, F32, kind="ExternalInput").ap() for n, a in arrays.items()}
    out = nc.dram_tensor("out_0", (S, D), F32, kind="ExternalOutput").ap()
    build(nc, inp, out)
    r = run_bass_kernel_spmd(nc, [arrays], core_ids=[0])
    return r.results[0]["out_0"].reshape(1, S, D)
```

```python
from contextlib import ExitStack

import numpy as np

import concourse.bass as bass
from concourse import mybir

F32 = mybir.dt.float32
ALU = mybir.AluOpType
ACT = mybir.ActivationFunctionType
AX_X = mybir.AxisListType.X

P = 128
D = 1024
KD = D // P
S = 512
NT = S // P
BANK = 512
DEPTH = 2
ALPHA = (2 * DEPTH) ** 0.25
LN_EPS = 1e-5
NORM_EPS = 1e-6

HEADS = 8
CH = 128
NCH = S // CH
LEVELS = 7
HG = 4

FF_PART = 1408
FT = FF_PART // P
EXPERTS = 8

RING = 4
RING_COLS = 2048
UP_COLS = 256


class Weights:

    def __init__(self, ring, loaded, used):
        self.ring, self.loaded, self.used = ring, loaded, used
        self.tiles, self.first, self.size, self.holds = [], {}, {}, {}
        self.n_loads = [0] * RING
        self.released, self.n_released, self.issued, self.passed = {}, 0, 0, 0

    def hold(self, stage):
        self.holds[len(self.tiles)] = self.holds.get(len(self.tiles), []) + [stage]

    def plan(self, stage, sources):
        self.first[stage], self.size[stage] = len(self.tiles), len(sources)
        for src in sources:
            slot = len(self.tiles) % RING
            self.n_loads[slot] += 1
            self.tiles.append((src, slot, 16 * self.n_loads[slot]))

    def view(self, index):
        src, slot, _ = self.tiles[index]
        k, n = src.shape[1], src.shape[2]
        return self.ring[:, slot, 0:k * n].rearrange("p (k n) -> p k n", n=n)

    def take(self, pe, stage, i):
        index = self.first[stage] + i
        _, slot, ready = self.tiles[index]
        pe.wait_ge(self.loaded[slot], ready)
        return self.view(index)

    def leave(self, matmul, stage, i):
        matmul.then_inc(self.used, 1)
        self.n_released += 1
        self.released[self.first[stage] + i] = self.n_released

    def load(self, sp, index):
        src, slot, _ = self.tiles[index]
        sp.dma_start(self.view(index), src).then_inc(self.loaded[slot], 16)

    def fill(self, sp, stage):
        while self.issued < len(self.tiles):
            n, old = self.issued, self.issued - RING
            if self.holds.get(n):
                break
            if old >= self.passed:
                if old not in self.released:
                    break
                sp.wait_ge(self.used, self.released[old])
            self.load(sp, n)
            self.issued += 1
        for stages in self.holds.values():
            if stage in stages:
                stages.remove(stage)
        if stage in self.first:
            self.passed = self.first[stage] + self.size[stage]


class Program:

    def __init__(self, nc, ctx):
        self.nc, self.ctx = nc, ctx
        self.sets = [[ctx.enter_context(nc.semaphore(f"{w}_{i}")) for i in range(56)] for w in ("even", "odd")]
        self.turn, self.dirty = 0, []

    def sbuf(self, name, shape, ctx=None):
        return (ctx or self.ctx).enter_context(self.nc.sbuf_tensor(name, shape, F32))


class Stage:

    def __init__(self, prog, name):
        self.prog, self.name = prog, name
        self.loads, self.after = None, None

    def __enter__(self):
        self.block_ctx = self.prog.nc.Block()
        self.block = self.block_ctx.__enter__()
        self.free = list(self.prog.sets[self.prog.turn])
        self.taken = []
        self.tensor, self.vector = self.block.tensor, self.block.vector
        self.scalar, self.gpsimd = self.block.scalar, self.block.gpsimd
        return self

    def counter(self, name):
        self.taken.append(self.free.pop(0))
        return self.taken[-1]

    def sync(self, f):
        self.loads = f
        return f

    def __exit__(self, *exc):
        if exc[0] is not None:
            return False

        @self.block.sync
        def _(sp):
            for s in self.prog.dirty:
                sp.sem_clear(s)
            if self.loads:
                self.loads(sp)
            self.prog.weights.fill(sp, self.name)
        self.block_ctx.__exit__(None, None, None)
        self.prog.dirty, self.prog.turn = self.taken, 1 - self.prog.turn
        return False


def linker(eng, sem):
    count = [0]

    def link(ins):
        count[0] += 1
        ins.then_inc(sem, 1)
        eng.wait_ge(sem, count[0])
    return link


def bc(ap, shape):
    return ap.to_broadcast(shape)


def col_tiles(w, width):
    n = w.shape[1]
    return [w[:, c:min(c + width, n)].rearrange("(k p) n -> p k n", p=P) for c in range(0, n, width)]



def project(prog, name, src, k_tiles, groups):
    nc, W, ps = prog.nc, prog.weights, prog.ps
    NB = 8
    by_act = [g[6] is not None or i % 2 == 0 for i, g in enumerate(groups)]
    order = [sum(by_act[:i + 1]) if a else i + 1 - sum(by_act[:i + 1]) for i, a in enumerate(by_act)]

    def out_of(i):
        _, _, width, tok, part, _, _ = groups[i]
        return ps[part:part + width, i % NB, :] if tok is None else ps[:, i % NB, 0:width]

    with Stage(prog, name) as st:
        product = st.counter("product")
        act_copied = st.counter("act_copied")
        dve_copied = st.counter("dve_copied")

        @st.tensor
        def _(pe):
            held, w = None, None
            for i, (tile, c, width, tok, part, _, _) in enumerate(groups):
                left = held if tile != held else None
                if tile != held:
                    w = W.take(pe, name, tile)
                    held = tile
                if i >= NB:
                    pe.wait_ge(act_copied if by_act[i - NB] else dve_copied, order[i - NB])
                for k in range(k_tiles):
                    if tok is None:
                        m = nc.tensor.matmul(out_of(i), w[:, k, c:c + width], src[:, k, :],
                                             start=(k == 0), stop=(k == k_tiles - 1))
                    else:
                        m = nc.tensor.matmul(out_of(i), src[:, k, tok * P:(tok + 1) * P], w[:, k, c:c + width],
                                             start=(k == 0), stop=(k == k_tiles - 1))
                    if k == 0 and left is not None:
                        W.leave(m, name, left)
                m.then_inc(product, 1)

        @st.scalar
        def _(act):
            for i, g in enumerate(groups):
                if by_act[i]:
                    act.wait_ge(product, i + 1)
                    nc.scalar.activation(g[5], out_of(i), g[6] or ACT.Copy).then_inc(act_copied, 1)

        @st.vector
        def _(dve):
            for i, g in enumerate(groups):
                if not by_act[i]:
                    dve.wait_ge(product, i + 1)
                    nc.vector.tensor_copy(g[5], out_of(i)).then_inc(dve_copied, 1)


def transpose_stage(prog, name, jobs):
    nc, ps, ident = prog.nc, prog.ps, prog.ident
    with Stage(prog, name) as st:
        turned = st.counter("turned")
        act_copied = st.counter("act_copied")
        dve_copied = st.counter("dve_copied")

        @st.tensor
        def _(pe):
            for i, (sources, _) in enumerate(jobs):
                if i >= 8:
                    pe.wait_ge((act_copied, dve_copied)[i % 2], (i - 8) // 2 + 1)
                for j, s in enumerate(sources):
                    m = nc.tensor.transpose(ps[:, i % 8, j * P:(j + 1) * P], s, ident)
                m.then_inc(turned, 1)

        def out(i):
            return ps[:, i % 8, 0:len(jobs[i][0]) * P]

        def fit(dst, src):
            return src.rearrange("p (a b) -> p a b", b=dst.shape[-1]) if len(dst.shape) == 3 else src

        @st.scalar
        def _(act):
            for i in range(0, len(jobs), 2):
                act.wait_ge(turned, i + 1)
                nc.scalar.activation(jobs[i][1], fit(jobs[i][1], out(i)), ACT.Copy).then_inc(act_copied, 1)

        @st.vector
        def _(dve):
            for i in range(1, len(jobs), 2):
                dve.wait_ge(turned, i + 1)
                nc.vector.tensor_copy(jobs[i][1], fit(jobs[i][1], out(i))).then_inc(dve_copied, 1)


def load_stage(prog, name, pairs):
    with Stage(prog, name) as st:
        landed = st.counter("landed")

        @st.sync
        def _(sp):
            for dst, src in pairs:
                sp.dma_start(dst, src).then_inc(landed, 16)
            sp.wait_ge(landed, 16 * len(pairs))


def down_project(prog, name, src_feat, w, gate=None):
    nc, ps = prog.nc, prog.ps
    with ExitStack() as own:
        dw = prog.sbuf(name + "_w", [P, KD, D], own)
        with Stage(prog, name) as st:
            landed = [st.counter(f"landed_{q}") for q in range(4)]
            product, summed = st.counter("product"), st.counter("summed")

            @st.sync
            def _(sp):
                for q in range(4):
                    sp.dma_start(dw[:, 2 * q:2 * q + 2, :],
                                 w[2 * q * P:(2 * q + 2) * P, :].rearrange("(k p) n -> p k n", p=P)
                                 ).then_inc(landed[q], 16)

            @st.tensor
            def _(pe):
                for k in range(KD):
                    if k % 2 == 0:
                        pe.wait_ge(landed[k // 2], 16)
                    for i in range(2 * NT):
                        m = nc.tensor.matmul(ps[:, i, :], src_feat[:, k, (i // 2) * P:(i // 2 + 1) * P],
                                             dw[:, k, (i % 2) * BANK:(i % 2 + 1) * BANK],
                                             start=(k == 0), stop=(k == KD - 1))
                        if k == KD - 1:
                            m.then_inc(product, 1)

            @st.vector
            def _(dve):
                for i in range(2 * NT):
                    t, c = i // 2, slice((i % 2) * BANK, (i % 2 + 1) * BANK)
                    dve.wait_ge(product, i + 1)
                    out = prog.acc[:, t, c]
                    if gate is None:
                        nc.vector.scalar_tensor_tensor(out=out, in0=prog.x_tok[:, t, c], scalar=ALPHA,
                                                       in1=ps[:, i, :], op0=ALU.mult, op1=ALU.add)
                    else:
                        nc.vector.scalar_tensor_tensor(out=out, in0=gate[:, c], scalar=1.0, in1=ps[:, i, :],
                                                       op0=ALU.add, op1=ALU.mult).then_inc(summed, 1)
                if gate is not None:
                    dve.wait_ge(summed, 2 * NT)
                    for t in range(NT):
                        nc.vector.scalar_tensor_tensor(out=prog.acc[:, t, :], in0=prog.x_tok[:, t, :], scalar=ALPHA,
                                                       in1=prog.acc[:, t, :], op0=ALU.mult, op1=ALU.add)


def layer_norm(prog, name, gb_src, last=False):
    nc, ps, acc, x_tok = prog.nc, prog.ps, prog.acc, prog.x_tok
    with ExitStack() as own:
        gb = prog.sbuf(name + "_gb", [P, 2, D], own)
        stats = prog.sbuf(name + "_stats", [P, NT, 12], own)
        mv = prog.sbuf(name + "_mv", [P, NT, 2], own)
        var = prog.sbuf(name + "_var", [P, NT], own)
        sd = prog.sbuf(name + "_sd", [P, NT], own)
        rs = prog.sbuf(name + "_rs", [P, NT], own)
        with Stage(prog, name) as st:
            landed = st.counter("landed")
            dve_link, var_ready = st.counter("dve_link"), st.counter("var_ready")
            sd_ready, normed = st.counter("sd_ready"), st.counter("normed")
            done, stored = st.counter("done"), st.counter("stored")
            turned, act_copied, dve_copied = st.counter("turned"), st.counter("act_copied"), st.counter("dve_copied")

            @st.sync
            def _(sp):
                sp.dma_start(gb[:, :, :], gb_src).then_inc(landed, 16)
                if last:
                    for t in range(NT):
                        sp.wait_ge(done, t + 1)
                        sp.dma_start(prog.out[t * P:(t + 1) * P, :], x_tok[:, t, :]).then_inc(stored, 16)
                    sp.wait_ge(stored, 16 * NT)

            def copy_out(dve, t):
                dve.wait_ge(turned, 2 * t + 2)
                nc.vector.tensor_copy(prog.x_feat[:, 4:8, t * P:(t + 1) * P],
                                      ps[:, 2 * t + 1, :].rearrange("p (k n) -> p k n", n=P)).then_inc(dve_copied, 1)

            @st.vector
            def _(dve):
                link = linker(dve, dve_link)
                for t in range(NT):
                    for h in range(2):
                        m = nc.vector.bn_stats(stats[:, t, 6 * h:6 * h + 6], acc[:, t, h * BANK:(h + 1) * BANK])
                link(m)
                for t in range(NT):
                    m = nc.vector.bn_aggr(mv[:, t, :], stats[:, t, :])
                link(m)
                nc.vector.tensor_scalar(var[:, :], mv[:, :, 1], LN_EPS, None, ALU.add).then_inc(var_ready, 1)
                dve.wait_ge(sd_ready, 1)
                link(nc.vector.reciprocal(rs[:, :], sd[:, :]))
                dve.wait_ge(landed, 16)
                for t in range(NT):
                    link(nc.vector.tensor_scalar(acc[:, t, :], acc[:, t, :], mv[:, t, 0:1], rs[:, t:t + 1],
                                                 ALU.subtract, ALU.mult))
                    nc.vector.tensor_tensor(acc[:, t, :], acc[:, t, :], gb[:, 0, :], ALU.mult).then_inc(normed, 1)
                    if not last and t >= 1:
                        copy_out(dve, t - 1)
                if not last:
                    copy_out(dve, NT - 1)

            @st.gpsimd
            def _(pool):
                pool.wait_ge(landed, 16)
                for t in range(NT):
                    pool.wait_ge(normed, t + 1)
                    nc.gpsimd.tensor_tensor(x_tok[:, t, :], acc[:, t, :], gb[:, 1, :], ALU.add).then_inc(done, 1)

            @st.scalar
            def _(act):
                act.wait_ge(var_ready, 1)
                nc.scalar.activation(sd[:, :], var[:, :], ACT.Sqrt).then_inc(sd_ready, 1)
                if not last:
                    for t in range(NT):
                        act.wait_ge(turned, 2 * t + 1)
                        nc.scalar.activation(prog.x_feat[:, 0:4, t * P:(t + 1) * P],
                                             ps[:, 2 * t, :].rearrange("p (k n) -> p k n", n=P), ACT.Copy
                                             ).then_inc(act_copied, 1)

            @st.tensor
            def _(pe):
                if not last:
                    for t in range(NT):
                        pe.wait_ge(done, t + 1)
                        for k in range(KD):
                            m = nc.tensor.transpose(ps[:, 2 * t + k // 4, (k % 4) * P:(k % 4 + 1) * P],
                                                    x_tok[:, t, k * P:(k + 1) * P], prog.ident)
                            if k % 4 == 3:
                                m.then_inc(turned, 1)



def gdn_conv(prog, name, dests, taps):
    nc, W, ps = prog.nc, prog.weights, prog.ps
    NF, PAD = len(dests), 3
    with ExitStack() as own:
        padded = prog.sbuf(name + "_padded", [P, 2, PAD + S], own)
        conv = prog.sbuf(name + "_conv", [P, 2, S], own)
        with Stage(prog, name) as st:
            product, copied = st.counter("product"), st.counter("copied")
            convolved, activated = st.counter("convolved"), st.counter("activated")
            zeroed, dve_link = st.counter("zeroed"), st.counter("dve_link")

            @st.gpsimd
            def _(pool):
                nc.gpsimd.memset(padded[:, :, 0:PAD], 0.0).then_inc(zeroed, 1)

            @st.tensor
            def _(pe):
                for f in range(NF):
                    if f % 2 == 0:
                        w = W.take(pe, name, f // 2)
                    if f >= 4:
                        pe.wait_ge(copied, f - 3)
                    for k in range(KD):
                        m = nc.tensor.matmul(ps[:, f % 4, :], w[:, k, (f % 2) * P:(f % 2 + 1) * P],
                                             prog.x_feat[:, k, :], start=(k == 0), stop=(k == KD - 1))
                        if k == 0 and f % 2 == 0 and f:
                            W.leave(m, name, f // 2 - 1)
                    m.then_inc(product, 1)

            @st.scalar
            def _(act):
                def silu(f):
                    act.wait_ge(convolved, f + 1)
                    nc.scalar.activation(dests[f], conv[:, f % 2, :], ACT.Silu).then_inc(activated, 1)
                for f in range(NF):
                    act.wait_ge(product, f + 1)
                    if f >= 2:
                        act.wait_ge(convolved, f - 1)
                    nc.scalar.activation(padded[:, f % 2, PAD:PAD + S], ps[:, f % 4, :], ACT.Copy).then_inc(copied, 1)
                    if f:
                        silu(f - 1)
                silu(NF - 1)

            @st.vector
            def _(dve):
                link = linker(dve, dve_link)
                dve.wait_ge(zeroed, 1)
                for f in range(NF):
                    dve.wait_ge(copied, f + 1)
                    if f >= 2:
                        dve.wait_ge(activated, f - 1)
                    out, x = conv[:, f % 2, :], padded[:, f % 2, :]
                    link(nc.vector.tensor_scalar(out, x[:, 0:S], taps[:, 4 * f:4 * f + 1], None, ALU.mult))
                    for j in (1, 2, 3):
                        m = nc.vector.scalar_tensor_tensor(out=out, in0=x[:, j:j + S], scalar=taps[:, 4 * f + j:4 * f + j + 1],
                                                           in1=out, op0=ALU.mult, op1=ALU.add)
                        if j < 3:
                            link(m)
                    m.then_inc(convolved, 1)


def gdn_norms(prog, name, tiles):
    nc, ps = prog.nc, prog.ps
    with ExitStack() as own:
        sq = prog.sbuf(name + "_sq", [P, 2, S], own)
        sd = prog.sbuf(name + "_sd", [P, 2, S], own)
        with Stage(prog, name) as st:
            squared, summed, rooted = st.counter("squared"), st.counter("summed"), st.counter("rooted")
            inverted, done = st.counter("inverted"), st.counter("done")
            n = len(tiles)

            @st.gpsimd
            def _(pool):
                for i, (x, _) in enumerate(tiles):
                    if i >= 2:
                        pool.wait_ge(summed, i - 1)
                    nc.gpsimd.tensor_tensor(sq[:, i % 2, :], x, x, ALU.mult).then_inc(squared, 1)

            @st.tensor
            def _(pe):
                for i in range(n):
                    pe.wait_ge(squared, i + 1)
                    if i >= 4:
                        pe.wait_ge(rooted, i - 3)
                    nc.tensor.matmul(ps[:, i % 4, :], prog.ones, sq[:, i % 2, :], start=True, stop=True).then_inc(summed, 1)

            @st.scalar
            def _(act):
                for i, (_, scale) in enumerate(tiles):
                    act.wait_ge(summed, i + 1)
                    if i >= 2:
                        act.wait_ge(done, i - 1)
                    c = scale ** -2.0
                    nc.scalar.activation(sd[:, i % 2, :], ps[:, i % 4, :], ACT.Sqrt, scale=c,
                                         bias=prog.eps_qk if c != 1.0 else prog.eps_norm).then_inc(rooted, 1)

            @st.vector
            def _(dve):
                for i, (x, _) in enumerate(tiles):
                    dve.wait_ge(rooted, i + 1)
                    nc.vector.reciprocal(sd[:, i % 2, :], sd[:, i % 2, :]).then_inc(inverted, 1)
                    dve.wait_ge(inverted, i + 1)
                    nc.vector.tensor_tensor(x, x, sd[:, i % 2, :], ALU.mult).then_inc(done, 1)


def gdn_gates(prog, name, ba, params, small):
    nc, ps = prog.nc, prog.ps
    g, beta, G, beG, kd, eL, t0, t1, neg_a = small
    b, a = ba[:, :, 0:HEADS], ba[:, :, HEADS:2 * HEADS]
    dt_bias, a_log = params[:, 0:HEADS], params[:, HEADS:2 * HEADS]
    rep = [P, NCH, HEADS]

    def over(x):
        return x.unsqueeze(1).to_broadcast(rep)

    def flat(x):
        return x.rearrange("p c h -> p (c h)")
    with Stage(prog, name) as st:
        acted, link_sem = st.counter("acted"), st.counter("dve_link")
        x_ready, a_ready, e_ready = st.counter("x_ready"), st.counter("a_ready"), st.counter("e_ready")
        g_ready, sums, diff = st.counter("g_ready"), st.counter("sums"), st.counter("diff")

        @st.scalar
        def _(act):
            nc.scalar.activation(beta, b, ACT.Sigmoid).then_inc(acted, 1)
            nc.scalar.activation(neg_a, a_log, ACT.Exp).then_inc(acted, 1)
            act.wait_ge(x_ready, 1)
            nc.scalar.activation(t1, t1, ACT.Exp, scale=-1.0).then_inc(acted, 1)
            act.wait_ge(acted, 3)
            nc.scalar.activation(t1, t1, ACT.Ln, bias=1.0).then_inc(acted, 1)
            act.wait_ge(diff, 1)
            nc.scalar.activation(kd, kd, ACT.Exp).then_inc(acted, 1)
            nc.scalar.activation(eL, ps[:, 1, 0:NCH * HEADS].rearrange("p (c h) -> p c h", h=HEADS), ACT.Exp
                                 ).then_inc(acted, 1)
            nc.scalar.activation(beG, G, ACT.Exp).then_inc(acted, 1)

        @st.vector
        def _(dve):
            link = linker(dve, link_sem)
            link(nc.vector.tensor_tensor(t0, a, over(dt_bias), ALU.add))
            link(nc.vector.tensor_scalar(t1, t0, -1.0, None, ALU.mult))
            nc.vector.tensor_tensor(t1, t0, t1, ALU.max).then_inc(x_ready, 1)
            link(nc.vector.tensor_scalar(t0, t0, 0.0, None, ALU.max))
            dve.wait_ge(acted, 4)
            link(nc.vector.tensor_tensor(t0, t0, t1, ALU.add))
            nc.vector.scalar_tensor_tensor(out=g, in0=t0, scalar=-1.0, in1=over(neg_a),
                                           op0=ALU.mult, op1=ALU.mult).then_inc(g_ready, 1)
            dve.wait_ge(sums, 2)
            link(nc.vector.tensor_copy(flat(G), ps[:, 0, 0:NCH * HEADS]))
            nc.vector.tensor_tensor(flat(kd), ps[:, 1, 0:NCH * HEADS], flat(G), ALU.subtract).then_inc(diff, 1)
            dve.wait_ge(acted, 7)
            link(nc.vector.tensor_tensor(beG, beG, beta, ALU.mult))

        @st.tensor
        def _(pe):
            pe.wait_ge(g_ready, 1)
            nc.tensor.matmul(ps[:, 0, 0:NCH * HEADS], prog.tri, flat(g), start=True, stop=True).then_inc(sums, 1)
            nc.tensor.matmul(ps[:, 1, 0:NCH * HEADS], prog.ones, flat(g), start=True, stop=True).then_inc(sums, 1)


def gdn_decays(prog, name, h0, q, k, g, G, dec, att, am):
    nc, ps = prog.nc, prog.ps
    with ExitStack() as own:
        eg = prog.sbuf(name + "_eg", [P, 2, S], own)
        with Stage(prog, name) as st:
            product = st.counter("product")
            shifted, decayed, masked = st.counter("shifted"), st.counter("decayed"), st.counter("masked")
            grown, scaled, weighted = st.counter("grown"), st.counter("scaled"), st.counter("weighted")

            @st.tensor
            def _(pe):
                for i in range(HG):
                    b0 = 4 * (i % 2)
                    if i >= 2:
                        pe.wait_ge(weighted, 2 * (i - 1))
                        pe.wait_ge(grown, i - 1)
                        pe.wait_ge(shifted, i - 1)
                    for c in range(NCH):
                        m = nc.tensor.matmul(ps[:, b0, c * P:(c + 1) * P], bc(g[:, c, h0 + i:h0 + i + 1], [P, P]), prog.tri,
                                             start=True, stop=True)
                    m.then_inc(product, 1)
                    for j, other in ((1, k), (2, q)):
                        for c in range(NCH):
                            cs = slice(c * P, (c + 1) * P)
                            m = nc.tensor.matmul(ps[:, b0 + j, cs], k[:, h0 + i, cs], other[:, h0 + i, cs],
                                                 start=True, stop=True)
                        m.then_inc(product, 1)

            @st.vector
            def _(dve):
                for i in range(HG):
                    b0 = 4 * (i % 2)
                    dve.wait_ge(product, 3 * i + 1)
                    for c in range(NCH):
                        m = nc.vector.tensor_scalar(dec[:, i, c * P:(c + 1) * P], ps[:, b0, c * P:(c + 1) * P],
                                                    G[:, c, h0 + i:h0 + i + 1], 0.0, ALU.subtract, ALU.min)
                    m.then_inc(shifted, 1)
                    dve.wait_ge(masked, i + 1)
                    dve.wait_ge(product, 3 * i + 3)
                    for out, j in ((am, 1), (att, 2)):
                        nc.vector.tensor_tensor(out[:, i, :], ps[:, b0 + j, :], dec[:, i, :], ALU.mult
                                                ).then_inc(weighted, 1)

            @st.scalar
            def _(act):
                for i in range(HG):
                    act.wait_ge(shifted, i + 1)
                    nc.scalar.activation(dec[:, i, :], dec[:, i, :], ACT.Exp).then_inc(decayed, 1)
                    if i >= 2:
                        act.wait_ge(scaled, i - 1)
                    nc.scalar.activation(eg[:, i % 2, :], ps[:, 4 * (i % 2), :], ACT.Exp).then_inc(grown, 1)

            @st.gpsimd
            def _(pool):
                for i in range(HG):
                    d = dec[:, i, :].rearrange("p (c n) -> p c n", n=P)
                    pool.wait_ge(decayed, i + 1)
                    nc.gpsimd.tensor_tensor(d, d, prog.tri.unsqueeze(1).to_broadcast([P, NCH, P]), ALU.mult
                                            ).then_inc(masked, 1)
                    pool.wait_ge(grown, i + 1)
                    pool.wait_ge(product, 3 * i + 3)
                    nc.gpsimd.tensor_tensor(q[:, h0 + i, :], q[:, h0 + i, :], eg[:, i % 2, :], ALU.mult
                                            ).then_inc(scaled, 1)


def gdn_inverse(prog, name, h0, beta, am, inv, inv_t, prod):
    nc, ps = prog.nc, prog.ps
    N = LEVELS * HG

    def blocks(x):
        return x.rearrange("p (c n) -> p c n", n=P)
    with ExitStack() as own:
        part = prog.sbuf(name + "_part", [P, 2, S], own)
        with Stage(prog, name) as st:
            start, cut = st.counter("start"), st.counter("cut")
            u_ready, u_copied = st.counter("u_ready"), st.counter("u_copied")
            p_ready, updated = st.counter("p_ready"), st.counter("updated")

            @st.gpsimd
            def _(pool):
                for n in range(N):
                    level, i = divmod(n, HG)
                    if n >= 2:
                        pool.wait_ge(u_ready, n - 1)
                    nc.gpsimd.tensor_tensor(blocks(part[:, n % 2, :]), blocks(am[:, i, :]),
                                            prog.level_masks[:, level, :].unsqueeze(1).to_broadcast([P, NCH, P]),
                                            ALU.mult).then_inc(cut, 1)

            @st.tensor
            def _(pe):
                def chunks():
                    return [slice(c * P, (c + 1) * P) for c in range(NCH)]

                def u(n):
                    i = n % HG
                    pe.wait_ge(cut, n + 1)
                    pe.wait_ge(start, HG)
                    if n >= HG:
                        pe.wait_ge(updated, 2 * (n - HG + 1))
                    for cs in chunks():
                        m = nc.tensor.matmul(ps[:, i, cs], part[:, n % 2, cs], inv[:, i, cs], start=True, stop=True)
                    m.then_inc(u_ready, 1)

                def p(n):
                    i, b = n % HG, 4 + 2 * (n % 2)
                    pe.wait_ge(u_copied, n + 1)
                    if n >= 2:
                        pe.wait_ge(updated, 2 * (n - 1))
                    for cs in chunks():
                        m = nc.tensor.matmul(ps[:, b, cs], inv_t[:, i, cs], prod[:, i, cs], start=True, stop=True)
                    m.then_inc(p_ready, 1)
                    for cs in chunks():
                        m = nc.tensor.matmul(ps[:, b + 1, cs], prod[:, i, cs], inv_t[:, i, cs], start=True, stop=True)
                    m.then_inc(p_ready, 1)

                for level in range(LEVELS):
                    for i in range(HG):
                        u(level * HG + i)
                    for i in range(HG):
                        p(level * HG + i)

            @st.vector
            def _(dve):
                for i in range(HG):
                    for x in (inv, inv_t):
                        m = nc.vector.tensor_copy(blocks(x[:, i, :]), prog.ident.unsqueeze(1).to_broadcast([P, NCH, P]))
                    m.then_inc(start, 1)
                for level in range(LEVELS):
                    for i in range(HG):
                        n = level * HG + i
                        dve.wait_ge(u_ready, n + 1)
                        if n >= HG:
                            dve.wait_ge(u_copied, n - HG + 1)
                        scale = beta[:, :, h0 + i:h0 + i + 1].to_broadcast([P, NCH, P])
                        nc.vector.tensor_tensor(blocks(prod[:, i, :]), blocks(ps[:, i, :]), scale, ALU.mult
                                                ).then_inc(u_copied, 1)
                    for i in range(HG):
                        n = level * HG + i
                        b = 4 + 2 * (n % 2)
                        dve.wait_ge(start, HG)
                        if n >= HG:
                            dve.wait_ge(updated, 2 * (n - HG + 1))
                        dve.wait_ge(p_ready, 2 * n + 2)
                        nc.vector.tensor_tensor(inv[:, i, :], inv[:, i, :], ps[:, b, :], ALU.subtract).then_inc(updated, 1)
                        nc.vector.tensor_tensor(inv_t[:, i, :], inv_t[:, i, :], ps[:, b + 1, :], ALU.subtract
                                                ).then_inc(updated, 1)


def gdn_uw(prog, name, h0, k_tok, v_tok, beta, beG, kd, inv_t, vb, kb, u, w_t):
    nc, ps = prog.nc, prog.ps
    hs = slice(h0 * P, (h0 + HG) * P)

    def heads(x):
        return x.rearrange("p (h n) -> p h n", n=P)
    with Stage(prog, name) as st:
        vb_ready, kb_ready = st.counter("vb_ready"), st.counter("kb_ready")
        u_ready, w_ready, u_copied, w_copied = (st.counter(x) for x in ("u_ready", "w_ready", "u_copied", "w_copied"))

        @st.vector
        def _(dve):
            for c in range(NCH):
                nc.vector.tensor_tensor(heads(vb[:, c, :]), heads(v_tok[:, c, hs]),
                                        beta[:, c, h0:h0 + HG].unsqueeze(2).to_broadcast([P, HG, P]),
                                        ALU.mult).then_inc(vb_ready, 1)
            for c in range(NCH):
                dve.wait_ge(u_ready, c + 1)
                nc.vector.tensor_copy(u[:, c, :], ps[:, c, :]).then_inc(u_copied, 1)

        @st.gpsimd
        def _(pool):
            for c in range(NCH):
                nc.gpsimd.tensor_tensor(heads(kb[:, c, :]), heads(k_tok[:, c, hs]),
                                        beG[:, c, h0:h0 + HG].unsqueeze(2).to_broadcast([P, HG, P]),
                                        ALU.mult).then_inc(kb_ready, 1)
            pool.wait_ge(kb_ready, NCH)
            for c in range(NCH):
                nc.gpsimd.tensor_tensor(heads(k_tok[:, c, hs]), heads(k_tok[:, c, hs]),
                                        kd[:, c, h0:h0 + HG].unsqueeze(2).to_broadcast([P, HG, P]), ALU.mult)

        @st.tensor
        def _(pe):
            for c in range(NCH):
                cs = slice(c * P, (c + 1) * P)
                pe.wait_ge(vb_ready, c + 1)
                for i in range(HG):
                    m = nc.tensor.matmul(ps[:, c, i * P:(i + 1) * P], inv_t[:, i, cs], vb[:, c, i * P:(i + 1) * P],
                                         start=True, stop=True)
                m.then_inc(u_ready, 1)
            pe.wait_ge(kb_ready, NCH)
            for i in range(HG):
                for c in range(NCH):
                    cs = slice(c * P, (c + 1) * P)
                    m = nc.tensor.matmul(ps[:, 4 + i, cs], kb[:, c, i * P:(i + 1) * P], inv_t[:, i, cs],
                                         start=True, stop=True)
                m.then_inc(w_ready, 1)

        @st.scalar
        def _(act):
            for i in range(HG):
                act.wait_ge(w_ready, i + 1)
                nc.scalar.activation(w_t[:, i, :], ps[:, 4 + i, :], ACT.Copy).then_inc(w_copied, 1)


def gdn_scan(prog, name, h0, q, att, k_tok, eL, u, w_t, out):
    nc, ps = prog.nc, prog.ps
    with ExitStack() as own:
        state = prog.sbuf(name + "_state", [P, HG * P], own)
        with Stage(prog, name) as st:
            ws, v_new, o_ready = st.counter("ws"), st.counter("v_new"), st.counter("o_ready")
            o_copied, kv, s_new = st.counter("o_copied"), st.counter("kv"), st.counter("s_new")

            @st.tensor
            def _(pe):
                for c in range(NCH):
                    cs = slice(c * P, (c + 1) * P)
                    if c:
                        pe.wait_ge(s_new, c)
                        pe.wait_ge(v_new, c)
                        for i in range(HG):
                            m = nc.tensor.matmul(ps[:, 0, i * P:(i + 1) * P], w_t[:, i, cs], state[:, i * P:(i + 1) * P],
                                                 start=True, stop=True)
                        m.then_inc(ws, 1)
                    if c >= 2:
                        pe.wait_ge(o_copied, c - 1)
                    pe.wait_ge(v_new, c + 1)
                    for i in range(HG):
                        hp = slice(i * P, (i + 1) * P)
                        if c:
                            nc.tensor.matmul(ps[:, 1 + c % 2, hp], q[:, h0 + i, cs], state[:, hp], start=True, stop=False)
                        m = nc.tensor.matmul(ps[:, 1 + c % 2, hp], att[:, i, cs], u[:, c, hp], start=(c == 0), stop=True)
                    m.then_inc(o_ready, 1)
                    if c < NCH - 1:
                        for i in range(HG):
                            hp = slice(i * P, (i + 1) * P)
                            m = nc.tensor.matmul(ps[:, 3, hp], k_tok[:, c, (h0 + i) * P:(h0 + i + 1) * P], u[:, c, hp],
                                                 start=True, stop=True)
                        m.then_inc(kv, 1)

            @st.vector
            def _(dve):
                for c in range(NCH):
                    if c == 0:
                        dve.sem_inc(v_new, 1)
                    else:
                        dve.wait_ge(ws, c)
                        nc.vector.tensor_tensor(u[:, c, :], u[:, c, :], ps[:, 0, :], ALU.subtract).then_inc(v_new, 1)
                    if c < NCH - 1:
                        dve.wait_ge(kv, c + 1)
                        if c == 0:
                            nc.vector.tensor_copy(state[:, :], ps[:, 3, :]).then_inc(s_new, 1)
                        else:
                            dve.wait_ge(s_new, c)
                            dve.wait_ge(o_ready, c + 1)
                            for i in range(HG):
                                hp = slice(i * P, (i + 1) * P)
                                m = nc.vector.scalar_tensor_tensor(out=state[:, hp], in0=state[:, hp],
                                                                   scalar=eL[:, c, h0 + i:h0 + i + 1], in1=ps[:, 3, hp],
                                                                   op0=ALU.mult, op1=ALU.add)
                            m.then_inc(s_new, 1)

            @st.scalar
            def _(act):
                for c in range(NCH):
                    act.wait_ge(o_ready, c + 1)
                    nc.scalar.activation(out[:, c, h0 * P:(h0 + HG) * P], ps[:, 1 + c % 2, :], ACT.Copy
                                         ).then_inc(o_copied, 1)


def gdn_output_gate(prog, name, o, z, norm_g):
    nc = prog.nc
    with ExitStack() as own:
        sq = prog.sbuf(name + "_sq", [P, NT, D], own)
        ms = prog.sbuf(name + "_ms", [P, NT, HEADS], own)
        with Stage(prog, name) as st:
            squared, summed, rooted = st.counter("squared"), st.counter("summed"), st.counter("rooted")
            dve_link, gained, sd = st.counter("dve_link"), st.counter("gained"), None

            def heads(x):
                return x.rearrange("p (h n) -> p h n", n=P)

            @st.scalar
            def _(act):
                for t in range(NT):
                    nc.scalar.activation(sq[:, t, :], o[:, t, :], ACT.Square).then_inc(squared, 1)
                act.wait_ge(summed, NT)
                nc.scalar.activation(ms[:, :, :], ms[:, :, :], ACT.Sqrt, scale=1.0 / P, bias=prog.eps_norm).then_inc(rooted, 1)

            @st.gpsimd
            def _(pool):
                for t in range(NT):
                    nc.gpsimd.tensor_tensor(heads(z[:, t, :]), heads(z[:, t, :]),
                                            norm_g.unsqueeze(1).to_broadcast([P, HEADS, P]), ALU.mult).then_inc(gained, 1)

            @st.vector
            def _(dve):
                link = linker(dve, dve_link)
                for t in range(NT):
                    dve.wait_ge(squared, t + 1)
                    nc.vector.tensor_reduce(ms[:, t, :], heads(sq[:, t, :]), AX_X, ALU.add).then_inc(summed, 1)
                dve.wait_ge(rooted, 1)
                link(nc.vector.reciprocal(ms[:, :, :], ms[:, :, :]))
                for t in range(NT):
                    link(nc.vector.tensor_tensor(heads(o[:, t, :]), heads(o[:, t, :]),
                                                 ms[:, t, :].unsqueeze(2).to_broadcast([P, HEADS, P]), ALU.mult))
                    dve.wait_ge(gained, t + 1)
                    nc.vector.tensor_tensor(o[:, t, :], o[:, t, :], z[:, t, :], ALU.mult)


def gdn_layer(prog, inp):
    w_in = inp["gdn_w_in"][0]
    with ExitStack() as own:
        def new(name, shape, c=own):
            return prog.sbuf(name, shape, c)
        small = new("gdn_small", [P, 9, NCH * HEADS])
        tabs = [small[:, i, :].rearrange("p (c h) -> p c h", h=HEADS) for i in range(8)] + [small[:, 8, 0:HEADS]]
        g, beta, G, beG, kd, eL = tabs[:6]
        par = new("gdn_par", [P, 16 + P])
        with ExitStack() as mid:
            q, k = new("gdn_q", [P, HEADS, S], mid), new("gdn_k", [P, HEADS, S], mid)
            k_tok, v_tok = new("gdn_ktok", [P, NT, D], mid), new("gdn_vtok", [P, NT, D], mid)
            with ExitStack() as early:
                v = new("gdn_v", [P, HEADS, S], early)
                taps = new("gdn_taps", [P, 96], early)
                ba = new("gdn_ba", [P, NT, 2 * HEADS], early)
                load_stage(prog, "gdn_params", [(taps[:, :], inp["gdn_taps"]), (par[:, :], inp["gdn_par"])])
                gdn_conv(prog, "gdn_conv", [x[:, h, :] for x in (q, k, v) for h in range(HEADS)], taps)
                project(prog, "gdn_ba", prog.x_feat, KD,
                        [(0, 0, 2 * HEADS, t, 0, ba[:, t, :], None) for t in range(NT)])
                gdn_norms(prog, "gdn_norms", [(q[:, h, :], P ** -0.5) for h in range(HEADS)]
                          + [(k[:, h, :], 1.0) for h in range(HEADS)])
                gdn_gates(prog, "gdn_gates", ba, par, tabs)
                transpose_stage(prog, "gdn_turn", [([x[:, h, t * P:(t + 1) * P] for h in range(hh, hh + 4)],
                                                    y[:, t, hh * P:(hh + 4) * P])
                                                   for x, y in ((k, k_tok), (v, v_tok)) for t in range(NT) for hh in (0, 4)])
            for h0 in range(0, HEADS, HG):
                with ExitStack() as grp:
                    dec, att, am, inv, inv_t = (new(f"gdn_{n}{h0}", [P, HG, S], grp) for n in ("dec", "att", "am", "inv", "invt"))
                    gdn_decays(prog, f"gdn_decays{h0}", h0, q, k, g, G, dec, att, am)
                    gdn_inverse(prog, f"gdn_inverse{h0}", h0, beta, am, inv, inv_t, dec)
                    kb = new(f"gdn_kb{h0}", [P, HG, S], grp)
                    gdn_uw(prog, f"gdn_uw{h0}", h0, k_tok, v_tok, beta, beG, kd, inv_t, inv, kb, dec, am)
                    gdn_scan(prog, f"gdn_scan{h0}", h0, q, att, k_tok, eL, dec, am, prog.acc)
        z, o_feat = new("gdn_z", [P, NT, D]), new("gdn_ofeat", [P, KD, S])
        project(prog, "gdn_z", prog.x_feat, KD,
                [(c, 0, UP_COLS, t, 0, z[:, t, c * UP_COLS:(c + 1) * UP_COLS], ACT.Silu)
                 for c in range(4) for t in range(NT)])
        gdn_output_gate(prog, "gdn_gate", prog.acc, z, par[:, 16:16 + P])
        transpose_stage(prog, "gdn_turn_o", [([prog.acc[:, t, kk * P:(kk + 1) * P] for t in range(NT)], o_feat[:, kk, :])
                                             for kk in range(KD)])
        down_project(prog, "gdn_out", o_feat, inp["gdn_w_out"][0])



GROUPS, GC, GP = 64, 16, 64
PAIRS = GROUPS // 2
STEP = P // GC
NJ = S // STEP
TWO_PI = 2 * np.pi
MAGIC = 1.5 * 2.0 ** 23
TWO_PI_HI = 6.28125
TWO_PI_LO = TWO_PI - TWO_PI_HI
PI_IN = 3.1415925
GSTEP = 8


def reduce_angle(nc, link, x, tmp, shift=0.0):
    if shift:
        link(nc.vector.tensor_scalar(x, x, shift, None, ALU.add))
    link(nc.vector.tensor_scalar(tmp, x, 1.0 / TWO_PI, MAGIC, ALU.mult, ALU.add))
    link(nc.vector.tensor_scalar(tmp, tmp, MAGIC, None, ALU.subtract))
    link(nc.vector.scalar_tensor_tensor(out=x, in0=tmp, scalar=-TWO_PI_HI, in1=x, op0=ALU.mult, op1=ALU.add))
    link(nc.vector.scalar_tensor_tensor(out=x, in0=tmp, scalar=-TWO_PI_LO, in1=x, op0=ALU.mult, op1=ALU.add))
    link(nc.vector.tensor_scalar(x, x, PI_IN, -PI_IN, ALU.min, ALU.max))


def s5_tables(prog, name, lanes, taus, pow_re, pow_im, bbar, b):
    nc = prog.nc
    NTAU = STEP + 1
    with ExitStack() as own:
        w = prog.sbuf(name + "_w", [P, 12, PAIRS], own)
        ang = prog.sbuf(name + "_ang", [P, 3, NTAU, PAIRS], own)
        tmp_b = prog.sbuf(name + "_tb", [P, 4, PAIRS, GC], own)
        with Stage(prog, name) as st:
            link_sem, acted = st.counter("dve_link"), st.counter("acted")
            to_act = st.counter("to_act")
            lr, li, ldt = (lanes[:, i, :] for i in range(3))
            dt, xr, xi, t, em1, half, m1c, den, fr, fi, s0, s1 = (w[:, i, :] for i in range(12))
            mag, cos, tmp = (ang[:, i, :, :] for i in range(3))

            @st.scalar
            def _(act):
                nc.scalar.activation(dt, ldt, ACT.Exp).then_inc(acted, 1)
                act.wait_ge(to_act, 1)
                nc.scalar.activation(t, xr, ACT.Tanh, scale=0.5).then_inc(acted, 1)
                nc.scalar.activation(mag, mag, ACT.Exp).then_inc(acted, 1)
                act.wait_ge(to_act, 2)
                nc.scalar.activation(half, xi, ACT.Sin, scale=0.5).then_inc(acted, 1)
                nc.scalar.activation(pow_im, pow_im, ACT.Sin).then_inc(acted, 1)
                nc.scalar.activation(cos, cos, ACT.Sin).then_inc(acted, 1)

            @st.vector
            def _(dve):
                link = linker(dve, link_sem)
                tt, ts = nc.vector.tensor_tensor, nc.vector.tensor_scalar
                rep = [P, NTAU, PAIRS]
                dve.wait_ge(acted, 1)
                link(tt(xr, lr, dt, ALU.mult))
                link(tt(xi, li, dt, ALU.mult))
                tau = taus.unsqueeze(2).to_broadcast(rep)
                tt(mag, xr.unsqueeze(1).to_broadcast(rep), tau, ALU.mult).then_inc(to_act, 1)
                reduce_angle(nc, link, xi, s0)
                link(tt(pow_im, xi.unsqueeze(1).to_broadcast(rep), tau, ALU.mult))
                reduce_angle(nc, link, pow_im, tmp)
                link(nc.vector.tensor_copy(cos, pow_im))
                reduce_angle(nc, link, cos, tmp, np.pi / 2)
                nc.vector.memset(s1, 0.0).then_inc(to_act, 1)
                dve.wait_ge(acted, 6)
                link(tt(pow_re, mag, cos, ALU.mult))
                link(tt(pow_im, mag, pow_im, ALU.mult))
                link(ts(s0, t, -1.0, 1.0, ALU.mult, ALU.add))
                link(nc.vector.reciprocal(s0, s0))
                link(nc.vector.scalar_tensor_tensor(out=em1, in0=t, scalar=2.0, in1=s0, op0=ALU.mult, op1=ALU.mult))
                link(tt(m1c, em1, cos[:, 1, :], ALU.mult))
                link(tt(s0, half, half, ALU.mult))
                link(nc.vector.scalar_tensor_tensor(out=m1c, in0=s0, scalar=-2.0, in1=m1c, op0=ALU.mult, op1=ALU.add))
                link(tt(den, lr, lr, ALU.mult))
                link(tt(s0, li, li, ALU.mult))
                link(tt(den, den, s0, ALU.add))
                link(nc.vector.reciprocal(den, den))
                ai = pow_im[:, 1, :]
                link(tt(fr, m1c, lr, ALU.mult))
                link(tt(s0, ai, li, ALU.mult))
                link(tt(fr, fr, s0, ALU.add))
                link(tt(fr, fr, den, ALU.mult))
                link(tt(fi, ai, lr, ALU.mult))
                link(tt(s0, m1c, li, ALU.mult))
                link(tt(fi, fi, s0, ALU.subtract))
                link(tt(fi, fi, den, ALU.mult))
                rep = [P, PAIRS, GC]
                frb, fib = fr.unsqueeze(2).to_broadcast(rep), fi.unsqueeze(2).to_broadcast(rep)
                for i, (f, x) in enumerate(((frb, 0), (fib, 1), (frb, 1), (fib, 0))):
                    m = tt(tmp_b[:, i], b[:, x], f, ALU.mult)
                link(m)
                tt(bbar[:, 0], tmp_b[:, 0], tmp_b[:, 1], ALU.subtract)
                tt(bbar[:, 1], tmp_b[:, 2], tmp_b[:, 3], ALU.add)


def complex_powers(prog, name, x, pow_re, pow_im, out_re, out_im, taus, conj):
    nc = prog.nc
    with ExitStack() as own:
        tmp = prog.acc[:, 0:2, :].rearrange("p a (b q c) -> p a b q c", b=2, c=GC)
        with Stage(prog, name) as st:
            v_link, p_link = st.counter("dve_link"), st.counter("pool_link")

            def rep(p, tau):
                return p[:, tau, :].unsqueeze(2).to_broadcast([P, PAIRS, GC])

            @st.vector
            def _(dve):
                link = linker(dve, v_link)
                for tau, at in taus:
                    nc.vector.tensor_tensor(tmp[:, 0, 0], x[:, 0], rep(pow_re, tau), ALU.mult)
                    link(nc.vector.tensor_tensor(tmp[:, 0, 1], x[:, 1], rep(pow_im, tau), ALU.mult))
                    link(nc.vector.tensor_tensor(out_re[:, at], tmp[:, 0, 0], tmp[:, 0, 1], ALU.subtract))

            @st.gpsimd
            def _(pool):
                link = linker(pool, p_link)
                for tau, at in taus:
                    nc.gpsimd.tensor_tensor(tmp[:, 1, 0], x[:, 0], rep(pow_im, tau), ALU.mult)
                    link(nc.gpsimd.tensor_tensor(tmp[:, 1, 1], x[:, 1], rep(pow_re, tau), ALU.mult))
                    m = nc.gpsimd.tensor_tensor(out_im[:, at], tmp[:, 1, 0], tmp[:, 1, 1], ALU.add)
                    if conj:
                        link(m)
                        m = nc.gpsimd.tensor_scalar(out_im[:, at], out_im[:, at], -1.0, None, ALU.mult)
                    link(m)


def s5_layer(prog, inp):
    nc, ps, W = prog.nc, prog.ps, prog.weights
    u_dram, y_dram = prog.u_dram, prog.y_dram
    with ExitStack() as own:
        def new(name, shape, c=own):
            return prog.sbuf(name, shape, c)
        u_feat = new("s5_ufeat", [P, KD, STEP, NJ])
        par = new("s5_par", [P, KD + 3 * PAIRS + STEP + 1])
        d_skip = par[:, 0:KD]
        lanes = par[:, KD:KD + 3 * PAIRS].rearrange("p (a q) -> p a q", q=PAIRS)
        taus = par[:, KD + 3 * PAIRS:]
        with ExitStack() as core:
            bc_in = new("s5_bc", [P, 4, PAIRS, GC], core)
            bbar = new("s5_bbar", [P, 2, PAIRS, GC], core)
            pw = new("s5_pow", [P, 2, STEP + 1, PAIRS], core)
            a8 = new("s5_a8", [P, 2, 2, PAIRS], core)
            u_blk = new("s5_ublk", [P, GROUPS, NJ], core)
            he = new("s5_he", [P, 2, NJ * 2 * PAIRS], core)
            h_all = he[:, 0, :].rearrange("p (j r q) -> p j r q", r=2, q=PAIRS)
            e_all = he[:, 1, :].rearrange("p (j r q) -> p j r q", r=2, q=PAIRS)
            load_stage(prog, "s5_params", [(par[:, :], inp["s5_par"]), (bc_in[:, :, :, :], inp["s5_bc"])])
            project(prog, "s5_u", prog.x_feat, KD,
                    [(f // 2, (f % 2) * P, P, None, 0, u_feat[:, f].rearrange("p i j -> p j i"), None)
                     for f in range(KD)])
            s5_tables(prog, "s5_tables", lanes, taus, pw[:, 0], pw[:, 1], bbar, bc_in[:, 0:2])

            with Stage(prog, "s5_u_turn") as st:
                stored, landed = st.counter("stored"), st.counter("landed")
                a8_ready = st.counter("a8_ready")

                @st.sync
                def _(sp):
                    sp.dma_start(u_dram.rearrange("f p n -> p f n"), u_feat[:, :].rearrange("p f i j -> p f (i j)")
                                 ).then_inc(stored, 16)
                    sp.wait_ge(stored, 16)
                    src = u_dram.rearrange("f (g c) (i j) -> i c (f g) j", c=GC, j=NJ)
                    for i in range(STEP):
                        sp.dma_start(u_blk[i * GC:(i + 1) * GC, :, :], src[i]).then_inc(landed, 16)
                    sp.wait_ge(landed, 16 * STEP)

                @st.vector
                def _(dve):
                    for r in range(2):
                        nc.vector.tensor_copy(a8[:, 0, r, :], pw[:, 0, STEP, :]).then_inc(a8_ready, 1)
                    nc.vector.tensor_scalar(a8[:, 1, 0, :], pw[:, 1, STEP, :], -1.0, None, ALU.mult)
                    nc.vector.tensor_copy(a8[:, 1, 1, :], pw[:, 1, STEP, :])

            with ExitStack() as phase:
                into = new("s5_into", [P, 2, PAIRS, P], phase)
                p_t = he[:, :, :].rearrange("p r (q i c) -> p r q i c", q=PAIRS, c=GC)
                complex_powers(prog, "s5_in_powers", bbar, pw[:, 0], pw[:, 1],
                               p_t[:, 0].rearrange("p q i c -> p i q c"), p_t[:, 1].rearrange("p q i c -> p i q c"),
                               [(t, STEP - 1 - t) for t in range(STEP)], False)
                transpose_stage(prog, "s5_in_turn", [([p_t[:, r, q].rearrange("p i c -> p (i c)") for q in range(q0, q0 + 4)],
                                                      into[:, r, q0:q0 + 4, :])
                                                     for r in range(2) for q0 in range(0, PAIRS, 4)])
                with Stage(prog, "s5_inputs") as st:
                    product, act_c = st.counter("product"), st.counter("act_copied")

                    @st.tensor
                    def _(pe):
                        for r in range(2):
                            for b in range(4):
                                for q in range(8 * b, 8 * b + 8):
                                    for gp in range(2):
                                        m = nc.tensor.matmul(ps[gp * GP:(gp + 1) * GP, 4 * r + b, (q % 8) * NJ:(q % 8 + 1) * NJ],
                                                             into[:, r, q, gp * GP:(gp + 1) * GP], u_blk[:, 2 * q + gp, :],
                                                             start=True, stop=True)
                                m.then_inc(product, 1)

                    @st.scalar
                    def _(act):
                        for n in range(0, 8, 2):
                            act.wait_ge(product, n + 1)
                            nc.scalar.activation(e_all[:, :, n // 4, 8 * (n % 4):8 * (n % 4) + 8].rearrange("p j q -> p q j"),
                                                 ps[:, n, :].rearrange("p (q j) -> p q j", j=NJ), ACT.Copy)

                    @st.vector
                    def _(dve):
                        for n in range(1, 8, 2):
                            dve.wait_ge(product, n + 1)
                            nc.vector.tensor_copy(e_all[:, :, n // 4, 8 * (n % 4):8 * (n % 4) + 8].rearrange("p j q -> p q j"),
                                                  ps[:, n, :].rearrange("p (q j) -> p q j", j=NJ))
            with ExitStack() as phase:
                q_re, q_im = (new(f"s5_q{r}", [P, PAIRS, STEP + 1, GC], phase) for r in range(2))
                t12 = new("s5_t12", [P, 2, 2, PAIRS], phase)
                with Stage(prog, "s5_scan") as st:
                    link_sem = st.counter("dve_link")

                    @st.vector
                    def _(dve):
                        link = linker(dve, link_sem)
                        link(nc.vector.memset(h_all[:, 0], 0.0))
                        for j in range(NJ - 1):
                            h = h_all[:, j]
                            nc.vector.tensor_tensor(t12[:, 0], h, a8[:, 0], ALU.mult)
                            nc.vector.tensor_tensor(t12[:, 1, 0], h[:, 1], a8[:, 1, 0], ALU.mult)
                            link(nc.vector.tensor_tensor(t12[:, 1, 1], h[:, 0], a8[:, 1, 1], ALU.mult))
                            link(nc.vector.tensor_tensor(t12[:, 0], t12[:, 0], e_all[:, j], ALU.add))
                            link(nc.vector.tensor_tensor(h_all[:, j + 1], t12[:, 0], t12[:, 1], ALU.add))
                complex_powers(prog, "s5_out_powers", bc_in[:, 2:4], pw[:, 0], pw[:, 1],
                               q_re[:, :, :, :].rearrange("p q i c -> p i q c"), q_im[:, :, :, :].rearrange("p q i c -> p i q c"),
                               [(t, t) for t in range(STEP + 1)], True)
                s5_outputs(prog, "s5_outputs", bbar, q_re, q_im, u_blk, h_all, he[:, 1, :])
        s5_glu(prog, inp, u_feat, d_skip)


def s5_outputs(prog, name, bbar, q_re, q_im, u_blk, h_all, spare):
    nc, ps = prog.nc, prog.ps
    lag = spare[:, 0:2 * GSTEP * P].rearrange("p (b g n) -> p b g n", b=2, n=P)
    mix = spare[:, 2 * GSTEP * P:].rearrange("p (b g n) -> p b g n", b=2, n=P)
    y = prog.acc[:, :, :].rearrange("p t n -> p (t n)").rearrange("p (g j) -> p g j", j=NJ)
    NS = GROUPS // GSTEP

    def flat(x):
        return x.rearrange("p i c -> p (i c)")

    def of_parity(x, gp):
        return x.rearrange("p (g b) n -> p b g n", b=2)[:, gp]
    with Stage(prog, name) as st:
        zeroed, lag_ready, lag_copied = st.counter("zeroed"), st.counter("lag_ready"), st.counter("lag_copied")
        placed = [st.counter(f"placed_{b}") for b in range(2)]
        y_ready, y_copied = st.counter("y_ready"), st.counter("y_copied")

        @st.vector
        def _(dve):
            nc.vector.memset(mix, 0.0).then_inc(zeroed, 1)
            for s in range(NS):
                dve.wait_ge(lag_ready, s + 1)
                if s >= 2:
                    dve.wait_ge(placed[s % 2], 16 * STEP * (s // 2))
                for gp in range(2):
                    m = nc.vector.tensor_copy(of_parity(lag[0:GC, s % 2], gp),
                                              ps[0:GC, 2 * (s % 2) + gp, :].rearrange("p (g n) -> p g n", n=P))
                m.then_inc(lag_copied, 1)

        @st.sync
        def _(sp):
            sp.wait_ge(zeroed, 1)
            for s in range(NS):
                sp.wait_ge(lag_copied, s + 1)
                if s >= 2:
                    sp.wait_ge(y_ready, s - 1)
                for i in range(STEP):
                    n = (STEP - i) * GC
                    sp.dma_start(mix[i * GC:(i + 1) * GC, s % 2, :, i * GC:], lag[0:GC, s % 2, :, 0:n]
                                 ).then_inc(placed[s % 2], 16)

        @st.tensor
        def _(pe):
            def lags(s):
                if s >= 2:
                    pe.wait_ge(lag_copied, s - 1)
                for g in range(GSTEP):
                    q, gp = divmod(s * GSTEP + g, 2)
                    rows = slice(gp * GP, (gp + 1) * GP)
                    out = ps[0:GC, 2 * (s % 2) + gp, (g // 2) * P:(g // 2 + 1) * P]
                    nc.tensor.matmul(out, bbar[rows, 0, q, :], flat(q_re[rows, q, 0:STEP, :]), start=True, stop=False)
                    m = nc.tensor.matmul(out, bbar[rows, 1, q, :], flat(q_im[rows, q, 0:STEP, :]), start=False, stop=True)
                m.then_inc(lag_ready, 1)

            def outs(s):
                pe.wait_ge(placed[s % 2], 16 * STEP * (s // 2 + 1))
                if s >= 2:
                    pe.wait_ge(y_copied, s - 1)
                for g in range(GSTEP):
                    q, gp = divmod(s * GSTEP + g, 2)
                    rows = slice(gp * GP, (gp + 1) * GP)
                    out = ps[:, 4 + 2 * (s % 2) + gp, (g // 2) * NJ:(g // 2 + 1) * NJ]
                    nc.tensor.matmul(out, mix[:, s % 2, g, :], u_blk[:, 2 * q + gp, :], start=True, stop=False)
                    nc.tensor.matmul(out, flat(q_re[rows, q, 1:STEP + 1, :]), h_all[rows, :, 0, q], start=False, stop=False)
                    m = nc.tensor.matmul(out, flat(q_im[rows, q, 1:STEP + 1, :]), h_all[rows, :, 1, q], start=False, stop=True)
                m.then_inc(y_ready, 1)
            lags(0)
            for s in range(NS):
                if s + 1 < NS:
                    lags(s + 1)
                outs(s)

        @st.scalar
        def _(act):
            for s in range(NS):
                act.wait_ge(y_ready, s + 1)
                for gp in range(2):
                    m = nc.scalar.activation(of_parity(y[:, s * GSTEP:(s + 1) * GSTEP, :], gp),
                                             ps[:, 4 + 2 * (s % 2) + gp, 0:GSTEP // 2 * NJ].rearrange("p (g j) -> p g j", j=NJ),
                                             ACT.Copy)
                m.then_inc(y_copied, 1)


def s5_glu(prog, inp, u_feat, d_skip):
    nc, ps, W = prog.nc, prog.ps, prog.weights
    with ExitStack() as own:
        y_feat = prog.sbuf("s5_yfeat", [P, KD, STEP, NJ], own)
        hid = prog.sbuf("s5_hid", [P, KD, S], own)
        with Stage(prog, "s5_y_turn") as st:
            stored, landed, skipped = st.counter("stored"), st.counter("landed"), st.counter("skipped")

            @st.sync
            def _(sp):
                sp.dma_start(prog.y_dram, prog.acc[:, :, :].rearrange("p t n -> p (t n)")).then_inc(stored, 16)
                sp.wait_ge(stored, 16)
                src = prog.y_dram.rearrange("(i c) (f g j) -> f g c i j", c=GC, g=STEP, j=NJ)
                for f in range(KD):
                    for g in range(STEP):
                        sp.dma_start(y_feat[g * GC:(g + 1) * GC, f], src[f, g]).then_inc(landed, 16)
                sp.wait_ge(landed, 16 * KD * STEP)

        with Stage(prog, "s5_gelu") as st:
            skipped = st.counter("skipped")

            @st.vector
            def _(dve):
                for f in range(KD):
                    nc.vector.scalar_tensor_tensor(out=y_feat[:, f].rearrange("p i j -> p (i j)"),
                                                   in0=u_feat[:, f].rearrange("p i j -> p (i j)"),
                                                   scalar=d_skip[:, f:f + 1], in1=y_feat[:, f].rearrange("p i j -> p (i j)"),
                                                   op0=ALU.mult, op1=ALU.add).then_inc(skipped, 1)

            @st.scalar
            def _(act):
                for f in range(KD):
                    act.wait_ge(skipped, f + 1)
                    nc.scalar.activation(hid[:, f, :].rearrange("p (j i) -> p i j", i=STEP), y_feat[:, f], ACT.Gelu)

        sig = prog.sbuf("s5_sig", [P, 2, UP_COLS], own)
        with Stage(prog, "s5_glu") as st:
            product, gated = st.counter("product"), st.counter("gated")
            multiplied, summed = st.counter("multiplied"), st.counter("summed")
            NG = D // UP_COLS

            @st.tensor
            def _(pe):
                for c in range(NG):
                    w = [W.take(pe, "s5_glu", 2 * c + r) for r in range(2)]
                    for t in range(NT):
                        n = c * NT + t
                        if n >= 4:
                            pe.wait_ge(multiplied, n - 3)
                        for r in range(2):
                            for k in range(KD):
                                m = nc.tensor.matmul(ps[:, 2 * (n % 4) + r, 0:UP_COLS], hid[:, k, t * P:(t + 1) * P],
                                                     w[r][:, k, :], start=(k == 0), stop=(k == KD - 1))
                                if k == 0 and r == 1 and t == NT - 1:
                                    W.leave(m, "s5_glu", 2 * c)
                                if k == 0 and r == 0 and t == 0 and c:
                                    W.leave(m, "s5_glu", 2 * c - 1)
                            m.then_inc(product, 1)

            @st.scalar
            def _(act):
                for n in range(NG * NT):
                    act.wait_ge(product, 2 * n + 2)
                    if n >= 2:
                        act.wait_ge(summed, n - 1)
                    nc.scalar.activation(sig[:, n % 2, :], ps[:, 2 * (n % 4) + 1, 0:UP_COLS], ACT.Sigmoid).then_inc(gated, 1)

            @st.vector
            def _(dve):
                for n in range(NG * NT):
                    c, t = divmod(n, NT)
                    cs = slice(c * UP_COLS, (c + 1) * UP_COLS)
                    dve.wait_ge(gated, n + 1)
                    nc.vector.tensor_tensor(sig[:, n % 2, :], sig[:, n % 2, :], ps[:, 2 * (n % 4), 0:UP_COLS], ALU.mult
                                            ).then_inc(multiplied, 1)
                    dve.wait_ge(multiplied, n + 1)
                    nc.vector.scalar_tensor_tensor(out=prog.acc[:, t, cs], in0=prog.x_tok[:, t, cs], scalar=ALPHA,
                                                   in1=sig[:, n % 2, :], op0=ALU.mult, op1=ALU.add).then_inc(summed, 1)



F32R = mybir.dt.float32r
I32 = mybir.dt.int32
CHUNKS = [(c, min(c + UP_COLS, FF_PART)) for c in range(0, FF_PART, UP_COLS)]
N_UP = 2 * len(CHUNKS)
N_DOWN = (FT + 1) // 2
N_TILES = N_UP + N_DOWN
RAW = 3
SPLITS = 2
SLOTS = 192
SLOT_PAD = 256
assert N_TILES % RAW == 0 and N_TILES % SPLITS == 0


def tile_rows(j):
    if j < N_UP:
        return KD, CHUNKS[j // 2][1] - CHUNKS[j // 2][0]
    return min(2, FT - 2 * (j - N_UP)), D


def tiles_of_chunk(c):
    return range(2 * c, min(2 * c + 2, FT))


class PartStream:

    def __init__(self, prog, st, parts, w1, w3, w2, hi, lo):
        self.prog, self.parts, self.w = prog, parts, (w1, w3, w2)
        self.hi, self.lo = hi, lo
        self.landed = [st.counter(f"landed_{i}") for i in range(RAW)]
        self.hi_done, self.lo_done = st.counter("hi_done"), st.counter("lo_done")
        self.slot_free = st.counter("slot_free")
        self.tile_used = st.counter("tile_used")

    def view(self, buf, slot, j):
        k, n = tile_rows(j)
        return buf[:, slot, 0:k * n].rearrange("p (k n) -> p k n", n=n)

    def flat(self, buf, slot, j):
        k, n = tile_rows(j)
        return buf[:, slot, 0:k * n]

    def load(self, sp, e, j):
        w1, w3, w2 = self.w
        if j < N_UP:
            c0, c1 = CHUNKS[j // 2]
            src = (w1, w3)[j % 2][bass.ds(e, 1), :, c0:c1]
        else:
            r = 2 * (j - N_UP)
            src = w2[bass.ds(e, 1), r * P:min(r + 2, FT) * P, :]
        sp.dma_start(self.view(self.prog.weights.ring, j % RAW, j), src.rearrange("a (k p) n -> p (a k) n", p=P)
                     ).then_inc(self.landed[j % RAW], 16)

    def loads(self, sp):
        for j in range(RAW):
            self.load(sp, 0, j)

        def part(here, after, values, count):
            for j in range(count):
                sp.wait_ge(self.lo_done, values[j])
                sp.sem_inc(self.slot_free, 1)
                ahead = j + RAW
                self.load(sp, *((here, ahead) if ahead < N_TILES else (after, ahead - N_TILES)))
        with sp.Fori(0, self.parts - 1) as e:
            values = [sp.snap(e * N_TILES + (j + 1)) for j in range(N_TILES)]
            part(e, sp.snap(e + 1), values, N_TILES)
        part(self.parts - 1, None, [(self.parts - 1) * N_TILES + j + 1 for j in range(N_TILES)], N_TILES - RAW)

    def split_hi(self, act, e, j):
        act.wait_ge(self.landed[j % RAW], e * (16 * N_TILES // RAW) + 16 * (j // RAW + 1))
        act.wait_ge(self.tile_used, e * N_TILES + (j + 1))
        self.prog.nc.scalar.activation(self.flat(self.hi, j % SPLITS, j), self.flat(self.prog.weights.ring, j % RAW, j),
                                       ACT.Copy).then_inc(self.hi_done, 1)

    def split_lo(self, dve, e, j):
        dve.wait_ge(self.hi_done, e * N_TILES + (j + 1))
        self.prog.nc.vector.tensor_tensor(self.flat(self.lo, j % SPLITS, j), self.flat(self.prog.weights.ring, j % RAW, j),
                                          self.flat(self.hi, j % SPLITS, j).bitcast(F32), ALU.subtract
                                          ).then_inc(self.lo_done, 1)

    def take(self, pe, e, j):
        pe.wait_ge(self.lo_done, e * N_TILES + (j + 1))
        return self.view(self.hi, j % SPLITS, j), self.view(self.lo, j % SPLITS, j)


def three_pass(nc, out, left, right, first, last, leave=None):
    (lh, ll), (rh, rl) = left, right
    m = nc.tensor.matmul(out, lh, rh, start=first, stop=False)
    if leave is not None:
        m.then_inc(leave, 1)
    nc.tensor.matmul(out, lh, rl, start=False, stop=False)
    return nc.tensor.matmul(out, ll, rh, start=False, stop=last)


def dense_parts(prog, st, buf, parts, w1, w3, w2, gates):
    nc, ps = prog.nc, prog.ps
    x_hi, x_lo, hid_hi, hid_lo, sig, prod, hi, lo = buf
    S_ = PartStream(prog, st, parts, w1, w3, w2, hi, lo)
    prepared, x_split = st.counter("prepared"), st.counter("x_split")
    up_ready, silu_done = st.counter("up_ready"), st.counter("silu_done")
    mult_done = st.counter("mult_done")
    hid_ready = st.counter("hid_ready")
    hi_ready = st.counter("hid_hi_ready")
    down_ready, added = st.counter("down_ready"), st.counter("added")

    def bank(m, which):
        return 4 * ((m // 2) % 2) + 2 * which + m % 2

    def tensor(pe):
        pe.wait_ge(x_split, 1)
        with pe.Fori(0, parts) as e:
            for j in range(N_UP):
                c, which = divmod(j, 2)
                wh, wl = S_.take(pe, e, j)
                if which == 0:
                    if c < 2:
                        pe.wait_ge(added, e * 8 + (4, 8)[c])
                    else:
                        pe.wait_ge(mult_done, e * FT + (2 * c + 2))
                for m in tiles_of_chunk(c):
                    cs = slice((m % 2) * P, (m % 2 + 1) * P)
                    for k in range(KD):
                        mm = three_pass(nc, ps[:, bank(m, which), :], (wh[:, k, cs], wl[:, k, cs]),
                                        (x_hi[:, k, :], x_lo[:, k, :]), k == 0, k == KD - 1,
                                        S_.tile_used if j and k == 0 and m % 2 == 0 else None)
                    mm.then_inc(up_ready, 1)
            pe.wait_ge(mult_done, e * FT + (FT + 4))
            for j in range(N_UP, N_TILES):
                wh, wl = S_.take(pe, e, j)
                for r in range(tile_rows(j)[0]):
                    m = 2 * (j - N_UP) + r
                    pe.wait_ge(hid_ready, e * FT + (m + 3))
                    for i in range(2 * NT):
                        t, cs = slice((i // 2) * P, (i // 2 + 1) * P), slice((i % 2) * BANK, (i % 2 + 1) * BANK)
                        mm = three_pass(nc, ps[:, i, :], (hid_hi[:, m, t], hid_lo[:, m, t]), (wh[:, r, cs], wl[:, r, cs]),
                                        m == 0, m == FT - 1, S_.tile_used if r == 0 and i == 0 else None)
                        if m == FT - 1 and i < 2 * NT - 1:
                            mm.then_inc(down_ready, 1)
            mm.then_inc(down_ready, 1)
            pe.wait_ge(added, e * 8 + 9)
            nc.tensor.matmul(ps[:, 0, 0:2], x_hi[:, 0, 0:P], x_hi[:, 0, 0:2], start=True, stop=True).then_inc(S_.tile_used, 1)

    def scalar(act):
        with act.Fori(0, parts) as e:
            S_.split_hi(act, e, 0)
            S_.split_hi(act, e, 1)
            for c in range(len(CHUNKS)):
                S_.split_hi(act, e, 2 * c + 2)
                for m in tiles_of_chunk(c):
                    act.wait_ge(up_ready, up_count(e, m, 0))
                    act.wait_ge(mult_done, e * FT + (4 if m == 0 else m + 3))
                    nc.scalar.activation(sig[:, m % 2, :], ps[:, bank(m, 0), :], ACT.Silu).then_inc(silu_done, 1)
                S_.split_hi(act, e, 2 * c + 3)
            for j in range(N_UP + 2, N_TILES):
                S_.split_hi(act, e, j)

    def up_count(e, m, which):
        n = len(tiles_of_chunk(m // 2))
        return e * (2 * FT) + (4 * (m // 2) + which * n + m % 2 + 1)

    def vector(dve):
        dve.sem_inc(S_.tile_used, SPLITS)
        dve.sem_inc(mult_done, 4)
        dve.sem_inc(hid_ready, 2)
        dve.sem_inc(added, 8)
        for k in range(KD):
            ins = nc.vector.tensor_copy(x_hi[:, k, :], prog.x_feat[:, k, :])
        ins.then_inc(prepared, 1)
        dve.wait_ge(prepared, 1)
        for k in range(KD):
            nc.vector.tensor_tensor(x_lo[:, k, :], prog.x_feat[:, k, :], x_hi[:, k, :].bitcast(F32), ALU.subtract)
        for t in range(NT):
            ins = nc.vector.tensor_scalar(prog.acc[:, t, :], prog.x_tok[:, t, :], ALPHA, None, ALU.mult)
        ins.then_inc(x_split, 1)
        dve.wait_ge(x_split, 1)
        with dve.Fori(0, parts) as e:
            S_.split_lo(dve, e, 0)
            S_.split_lo(dve, e, 1)
            for c in range(len(CHUNKS)):
                S_.split_lo(dve, e, 2 * c + 2)
                for m in tiles_of_chunk(c):
                    dve.wait_ge(up_ready, up_count(e, m, 1))
                    dve.wait_ge(silu_done, e * FT + (m + 1))
                    dve.wait_ge(hid_ready, e * FT + (2 if m == 0 else m + 1))
                    nc.vector.tensor_tensor(prod[:, m % 2, :], sig[:, m % 2, :], ps[:, bank(m, 1), :], ALU.mult
                                            ).then_inc(mult_done, 1)
                S_.split_lo(dve, e, 2 * c + 3)
            for j in range(N_UP + 2, N_TILES):
                S_.split_lo(dve, e, j)
            dve.wait_ge(added, e * 8 + 8)
            for i in range(2 * NT):
                t, cs = i // 2, slice((i % 2) * BANK, (i % 2 + 1) * BANK)
                dve.wait_ge(down_ready, e * 8 + (i + 1))
                if gates is None:
                    ins = nc.vector.tensor_tensor(prog.acc[:, t, cs], ps[:, i, :], prog.acc[:, t, cs], ALU.add)
                else:
                    ins = nc.vector.scalar_tensor_tensor(out=prog.acc[:, t, cs], in0=ps[:, i, :],
                                                         scalar=gates[:, t, bass.ds(e, 1)], in1=prog.acc[:, t, cs],
                                                         op0=ALU.mult, op1=ALU.add)
                ins.then_inc(added, 1)

    def gpsimd(pool):
        with pool.Fori(0, parts) as e:
            for m in range(FT):
                pool.wait_ge(mult_done, e * FT + (m + 5))
                nc.gpsimd.tensor_tensor(hid_hi[:, m, :], prod[:, m % 2, :],
                                        prog.ones[:, 0:1].to_broadcast([P, S]), ALU.mult).then_inc(hi_ready, 1)
                pool.wait_ge(hi_ready, e * FT + (m + 1))
                nc.gpsimd.tensor_tensor(hid_lo[:, m, :], prod[:, m % 2, :], hid_hi[:, m, :].bitcast(F32), ALU.subtract
                                        ).then_inc(hid_ready, 1)
    return S_.loads, tensor, scalar, vector, gpsimd


def sparse_parts(prog, st, buf, w1, w3, w2, gates, place, iota):
    nc, ps = prog.nc, prog.ps
    xt_hi, xt_lo, xy_hi, xy_lo, hid_hi, hid_lo, sig, prod, hi, lo, pick, put, ident_r = buf
    S_ = PartStream(prog, st, EXPERTS, w1, w3, w2, hi, lo)
    names = ("prepared", "pick_ready", "gathered", "g_hi", "g_lo", "put_ready", "put_act", "put_dve", "up_ready",
             "silu_done", "mult_done", "hi_ready", "hid_ready", "down_ready", "y_hi", "y_lo", "back_ready", "back_done")
    (prepared, pick_ready, gathered, g_hi, g_lo, put_ready, put_act, put_dve, up_ready, silu_done, mult_done,
     hi_ready, hid_ready, down_ready, y_hi, y_lo, back_ready, back_done) = (st.counter(n) for n in names)
    acc_ready = st.counter("acc_ready")
    NC = len(CHUNKS)
    xg = [b[:, 0:KD * SLOTS].rearrange("p (k n) -> p k n", n=SLOTS) for b in (xy_hi, xy_lo)]
    y = [b[:, :].rearrange("p (s n) -> p s n", n=D) for b in (xy_hi, xy_lo)]

    def pair(c):
        return len(tiles_of_chunk(c)) * SLOTS

    def gather_view(r, part):
        return ps[:, 2 * part:2 * part + 2, 0:2 * SLOTS].rearrange("p b (k n) -> p b k n", n=SLOTS)

    def gather_dst(r, part):
        return xg[part][:, 4 * r:4 * r + 4, :].rearrange("p (b k) n -> p b k n", b=2)

    def tensor(pe):
        pe.wait_ge(prepared, 2)
        with pe.Fori(0, EXPERTS) as e:
            pe.wait_ge(pick_ready, e + 1)
            for r in range(2):
                if r == 0:
                    pe.wait_ge(mult_done, e * NC + 2)
                else:
                    pe.wait_ge(g_hi, e * 2 + 1)
                    pe.wait_ge(g_lo, e * 2 + 1)
                for part, x in enumerate((xt_hi, xt_lo)):
                    for k in range(4 * r, 4 * r + 4):
                        out = ps[:, 2 * part + (k % 4) // 2, (k % 2) * SLOTS:(k % 2 + 1) * SLOTS]
                        for t in range(NT):
                            mm = nc.tensor.matmul(out, x[:, t, k * P:(k + 1) * P], pick[:, t, 0:SLOTS],
                                                  start=(t == 0), stop=(t == NT - 1))
                mm.then_inc(gathered, 1)
            pe.wait_ge(back_done, e * 8 + 4)
            for s in range(2):
                for t in range(NT):
                    mm = nc.tensor.matmul(ps[:, 4 + s, t * P:(t + 1) * P], pick[:, t, s * P:(s + 1) * P], ident_r,
                                          start=True, stop=True)
            mm.then_inc(put_ready, 1)
            pe.wait_ge(g_hi, e * 2 + 2)
            pe.wait_ge(g_lo, e * 2 + 2)
            for j in range(N_UP):
                c, which = divmod(j, 2)
                wh, wl = S_.take(pe, e, j)
                if which == 0 and c >= 2:
                    pe.wait_ge(mult_done, e * NC + (c + 1))
                for m in tiles_of_chunk(c):
                    cs = slice((m % 2) * P, (m % 2 + 1) * P)
                    out = ps[:, 2 * (c % 2) + which, (m % 2) * SLOTS:(m % 2 + 1) * SLOTS]
                    for k in range(KD):
                        mm = three_pass(nc, out, (wh[:, k, cs], wl[:, k, cs]), (xg[0][:, k, :], xg[1][:, k, :]),
                                        k == 0, k == KD - 1, S_.tile_used if j and k == 0 and m % 2 == 0 else None)
                mm.then_inc(up_ready, 1)
            pe.wait_ge(put_act, e + 1)
            pe.wait_ge(put_dve, e + 1)
            for j in range(N_UP, N_TILES):
                wh, wl = S_.take(pe, e, j)
                pe.wait_ge(hid_ready, e * NC + (j - N_UP + 3))
                for r in range(tile_rows(j)[0]):
                    m = 2 * (j - N_UP) + r
                    for i in range(4):
                        s, cs = slice((i // 2) * P, (i // 2 + 1) * P), slice((i % 2) * BANK, (i % 2 + 1) * BANK)
                        mm = three_pass(nc, ps[:, 4 + i, :], (hid_hi[:, m, s], hid_lo[:, m, s]), (wh[:, r, cs], wl[:, r, cs]),
                                        m == 0, m == FT - 1, S_.tile_used if r == 0 and i == 0 else None)
                        if m == FT - 1:
                            mm.then_inc(down_ready, 1)
            pe.wait_ge(y_hi, e * 4 + 4)
            pe.wait_ge(y_lo, e * 4 + 4)
            for i in range(2 * NT):
                t, cs = slice((i // 2) * P, (i // 2 + 1) * P), slice((i % 2) * BANK, (i % 2 + 1) * BANK)
                if i >= 4:
                    pe.wait_ge(back_done, e * 8 + (i + 1))
                for n, (s, part) in enumerate((s, part) for s in range(2) for part in range(2)):
                    mm = nc.tensor.matmul(ps[:, 4 + i % 4, :], put[:, s, t], y[part][:, s, cs], start=(n == 0), stop=(n == 3))
                    if i == 0 and n == 0:
                        mm.then_inc(S_.tile_used, 1)
                mm.then_inc(back_ready, 1)

    def scalar(act):
        with act.Fori(0, EXPERTS) as e:
            S_.split_hi(act, e, 0)
            for r in range(2):
                act.wait_ge(gathered, e * 2 + (r + 1))
                nc.scalar.activation(gather_dst(r, 0), gather_view(r, 0), ACT.Copy).then_inc(g_hi, 1)
            S_.split_hi(act, e, 1)
            act.wait_ge(put_ready, e + 1)
            nc.scalar.activation(put[:, 0, :], ps[:, 4, :], ACT.Copy).then_inc(put_act, 1)
            for c in range(NC):
                S_.split_hi(act, e, 2 * c + 2)
                act.wait_ge(up_ready, e * N_UP + (2 * c + 1))
                act.wait_ge(mult_done, e * NC + (c + 1))
                nc.scalar.activation(sig[:, c % 2, 0:pair(c)], ps[:, 2 * (c % 2), 0:pair(c)], ACT.Silu).then_inc(silu_done, 1)
                S_.split_hi(act, e, 2 * c + 3)
            for j in range(N_UP + 2, N_TILES):
                S_.split_hi(act, e, j)
            for i in range(4):
                act.wait_ge(down_ready, e * 4 + (i + 1))
                nc.scalar.activation(y[0][:, i // 2, (i % 2) * BANK:(i % 2 + 1) * BANK], ps[:, 4 + i, :], ACT.Copy
                                     ).then_inc(y_hi, 1)

    def vector(dve):
        def make_pick(e):
            for t in range(NT):
                ins = nc.vector.tensor_scalar(pick[:, t, :], iota, place[:, t, bass.ds(e, 1)], None, ALU.is_equal)
            ins.then_inc(pick_ready, 1)
        dve.sem_inc(S_.tile_used, SPLITS)
        dve.sem_inc(mult_done, 2)
        dve.sem_inc(hid_ready, 2)
        dve.sem_inc(back_done, 4)
        nc.vector.tensor_copy(ident_r, prog.ident)
        for t in range(NT):
            ins = nc.vector.tensor_copy(xt_hi[:, t, :], prog.x_tok[:, t, :])
        ins.then_inc(prepared, 1)
        dve.wait_ge(prepared, 1)
        for t in range(NT):
            ins = nc.vector.tensor_tensor(xt_lo[:, t, :], prog.x_tok[:, t, :], xt_hi[:, t, :].bitcast(F32), ALU.subtract)
        ins.then_inc(prepared, 1)
        make_pick(0)
        dve.wait_ge(pick_ready, 1)
        with dve.Fori(0, EXPERTS) as e:
            S_.split_lo(dve, e, 0)
            for r in range(2):
                dve.wait_ge(gathered, e * 2 + (r + 1))
                nc.vector.tensor_copy(gather_dst(r, 1), gather_view(r, 1)).then_inc(g_lo, 1)
            S_.split_lo(dve, e, 1)
            dve.wait_ge(put_ready, e + 1)
            nc.vector.tensor_copy(put[:, 1, :], ps[:, 5, :]).then_inc(put_dve, 1)
            for c in range(NC):
                S_.split_lo(dve, e, 2 * c + 2)
                dve.wait_ge(up_ready, e * N_UP + (2 * c + 2))
                dve.wait_ge(silu_done, e * NC + (c + 1))
                dve.wait_ge(hid_ready, e * NC + (c + 1))
                nc.vector.tensor_tensor(prod[:, c % 2, 0:pair(c)], sig[:, c % 2, 0:pair(c)],
                                        ps[:, 2 * (c % 2) + 1, 0:pair(c)], ALU.mult).then_inc(mult_done, 1)
                S_.split_lo(dve, e, 2 * c + 3)
            for j in range(N_UP + 2, N_TILES):
                S_.split_lo(dve, e, j)
            for i in range(4):
                cs = slice((i % 2) * BANK, (i % 2 + 1) * BANK)
                dve.wait_ge(y_hi, e * 4 + (i + 1))
                nc.vector.tensor_tensor(y[1][:, i // 2, cs], ps[:, 4 + i, :], y[0][:, i // 2, cs].bitcast(F32),
                                        ALU.subtract).then_inc(y_lo, 1)
            make_pick(e + 1)
            dve.wait_ge(acc_ready, 1)
            dve.wait_ge(back_done, e * 8 + 4)
            for i in range(2 * NT):
                t, cs = i // 2, slice((i % 2) * BANK, (i % 2 + 1) * BANK)
                dve.wait_ge(back_ready, e * 8 + (i + 1))
                nc.vector.scalar_tensor_tensor(out=prog.acc[:, t, cs], in0=ps[:, 4 + i % 4, :],
                                               scalar=gates[:, t, bass.ds(e, 1)], in1=prog.acc[:, t, cs],
                                               op0=ALU.mult, op1=ALU.add).then_inc(back_done, 1)

    def gpsimd(pool):
        for b in (hid_hi, hid_lo):
            nc.gpsimd.memset(b[:, :, SLOTS:].bitcast(F32), 0.0)
        for t in range(NT):
            ins = nc.gpsimd.tensor_scalar(prog.acc[:, t, :], prog.x_tok[:, t, :], ALPHA, None, ALU.mult)
        ins.then_inc(acc_ready, 1)
        with pool.Fori(0, EXPERTS) as e:
            for c in range(NC):
                ms = tiles_of_chunk(c)
                dst = [b[:, ms[0]:ms[-1] + 1, 0:SLOTS] for b in (hid_hi, hid_lo)]
                src = prod[:, c % 2, 0:pair(c)].rearrange("p (m n) -> p m n", n=SLOTS)
                pool.wait_ge(mult_done, e * NC + (c + 3))
                nc.gpsimd.tensor_tensor(dst[0], src, prog.ones[:, 0:1].unsqueeze(2).to_broadcast([P, len(ms), SLOTS]), ALU.mult
                                        ).then_inc(hi_ready, 1)
                pool.wait_ge(hi_ready, e * NC + (c + 1))
                nc.gpsimd.tensor_tensor(dst[1], src, dst[0].bitcast(F32), ALU.subtract).then_inc(hid_ready, 1)
    return S_.loads, tensor, scalar, vector, gpsimd


def dense_buffers(prog, own, name):
    def new(n, shape, dt=F32R):
        return own.enter_context(prog.nc.sbuf_tensor(f"{name}_{n}", shape, dt))
    return (new("x_hi", [P, KD, S]), new("x_lo", [P, KD, S]), new("hid_hi", [P, FT, S]), new("hid_lo", [P, FT, S]),
            new("sig", [P, 2, S], F32), new("prod", [P, 2, S], F32),
            new("w_hi", [P, SPLITS, RING_COLS]), new("w_lo", [P, SPLITS, RING_COLS]))


def dense_ffn(prog, name, w1, w3, w2, parts):
    with ExitStack() as own:
        buf = dense_buffers(prog, own, name)
        with Stage(prog, name) as st:
            loads, tensor, scalar, vector, gpsimd = dense_parts(prog, st, buf, parts, w1, w3, w2, None)
            st.sync(loads)
            st.tensor(tensor)
            st.scalar(scalar)
            st.vector(vector)
            st.gpsimd(gpsimd)


def moe_experts(prog, name, w, gates, place, flag):
    with ExitStack() as own:
        dense_buf = dense_buffers(prog, own, name + "_dense")
    with ExitStack() as own:
        def new(n, shape, dt=F32R):
            return own.enter_context(prog.nc.sbuf_tensor(f"{name}_{n}", shape, dt))
        iota = new("iota", [P, SLOT_PAD], F32)
        buf = (new("xt_hi", [P, NT, D]), new("xt_lo", [P, NT, D]), new("xy_hi", [P, 2 * D]), new("xy_lo", [P, 2 * D]),
               new("hid_hi", [P, FT, SLOT_PAD]), new("hid_lo", [P, FT, SLOT_PAD]),
               new("sig", [P, 2, 2 * SLOTS], F32), new("prod", [P, 2, 2 * SLOTS], F32),
               new("w_hi", [P, SPLITS, RING_COLS]), new("w_lo", [P, SPLITS, RING_COLS]),
               new("pick", [P, NT, SLOT_PAD]), new("put", [P, 2, S]), new("ident_r", [P, P])[:, :])
        load_stage(prog, name + "_iota", [(iota[:, :], prog.iota_in)])
        with Stage(prog, name) as st:
            sparse = sparse_parts(prog, st, buf, *w, gates, place, iota[:, :])
            dense = dense_parts(prog, st, dense_buf, EXPERTS, *w, gates)

            def either(i):
                def program(eng):
                    fits = eng.value_load(flag[0:1, 0:1], min_val=0, max_val=1)
                    with eng.If(fits > 0):
                        sparse[i](eng)
                    with eng.Else():
                        dense[i](eng)
                return program
            st.sync(either(0))
            st.tensor(either(1))
            st.scalar(either(2))
            st.vector(either(3))
            st.gpsimd(either(4))



def router(prog, inp, gates, place, flag):
    nc, ps = prog.nc, prog.ps
    PAD = 2 * EXPERTS
    FILL, TAKEN = -3.0e38, -2.0e38
    with ExitStack() as own:
        w = prog.sbuf("moe_wr", [P, KD, EXPERTS], own)
        bias = prog.sbuf("moe_br", [P, EXPERTS], own)
        logit = prog.sbuf("moe_logit", [P, NT, PAD], own)
        left = prog.sbuf("moe_left", [P, NT, PAD], own)
        top = prog.sbuf("moe_top", [P, NT, 8], own)
        neg = prog.sbuf("moe_neg", [P, NT], own)
        den = prog.sbuf("moe_den", [P, NT], own)
        e = prog.sbuf("moe_e", [P, NT, EXPERTS], own)
        load_stage(prog, "moe_params", [(w[:, :, :], inp["moe_wr"]), (bias[:, :], inp["moe_br"])])
        with Stage(prog, "moe_router") as st:
            product, link_sem, neg_ready, exped, chosen, ranked = (
                st.counter(n) for n in ("product", "dve_link", "neg_ready", "exped", "chosen", "ranked"))

            @st.tensor
            def _(pe):
                for t in range(NT):
                    for k in range(KD):
                        m = nc.tensor.matmul(ps[:, t, 0:EXPERTS], prog.x_feat[:, k, t * P:(t + 1) * P], w[:, k, :],
                                             start=(k == 0), stop=(k == KD - 1))
                    m.then_inc(product, 1)
                pe.wait_ge(chosen, 1)
                for t in range(NT):
                    for b in range(t + 1):
                        m = nc.tensor.matmul(ps[:, 4, t * EXPERTS:(t + 1) * EXPERTS], prog.tri if b == t else prog.ones,
                                             left[:, b, 0:EXPERTS], start=(b == 0), stop=(b == t))
                m.then_inc(ranked, 1)
                for t in range(NT):
                    m = nc.tensor.matmul(ps[:, 5, 0:EXPERTS], prog.ones, left[:, t, 0:EXPERTS], start=(t == 0), stop=(t == NT - 1))
                m.then_inc(ranked, 1)

            @st.vector
            def _(dve):
                link = linker(dve, link_sem)
                nc.vector.memset(logit[:, :, EXPERTS:], FILL)
                for t in range(NT):
                    dve.wait_ge(product, t + 1)
                    m = nc.vector.tensor_tensor(logit[:, t, 0:EXPERTS], ps[:, t, 0:EXPERTS], bias[:, :], ALU.add)
                link(m)
                for t in range(NT):
                    m = nc.vector.max(top[:, t, :], logit[:, t, 0:EXPERTS])
                link(m)
                nc.vector.tensor_scalar(neg[:, :], top[:, :, 0], -1.0, None, ALU.mult).then_inc(neg_ready, 1)
                link(nc.vector.memset(top[:, :, 2:], FILL))
                for t in range(NT):
                    m = nc.vector.match_replace(left[:, t, :], top[:, t, :], logit[:, t, :], TAKEN)
                link(m)
                nc.vector.tensor_scalar(left[:, :, 0:EXPERTS], left[:, :, 0:EXPERTS], TAKEN, None, ALU.is_equal
                                        ).then_inc(chosen, 1)
                dve.wait_ge(chosen, 1)
                dve.wait_ge(exped, NT)
                link(nc.vector.tensor_tensor(e[:, :, :], e[:, :, :], left[:, :, 0:EXPERTS], ALU.mult))
                link(nc.vector.tensor_reduce(den[:, :], e[:, :, :], AX_X, ALU.add))
                link(nc.vector.reciprocal(den[:, :], den[:, :]))
                nc.vector.tensor_tensor(gates, e[:, :, :], den[:, :].unsqueeze(2).to_broadcast([P, NT, EXPERTS]),
                                        ALU.mult)
                dve.wait_ge(ranked, 2)
                link(nc.vector.memset(place[:, :, EXPERTS:], -1.0))
                pl = place[:, :, 0:EXPERTS]
                link(nc.vector.tensor_tensor(pl, ps[:, 4, 0:NT * EXPERTS].rearrange("p (t n) -> p t n", n=EXPERTS),
                                             left[:, :, 0:EXPERTS], ALU.mult))
                link(nc.vector.tensor_scalar(pl, pl, 1.0, None, ALU.subtract))
                link(nc.vector.tensor_reduce(den[:, 0:1], ps[:, 5, 0:EXPERTS], AX_X, ALU.max))
                nc.vector.tensor_scalar(flag[:, :], den[:, 0:1], SLOTS + 0.5, None, ALU.is_lt)

            @st.scalar
            def _(act):
                act.wait_ge(neg_ready, 1)
                for t in range(NT):
                    nc.scalar.activation(e[:, t, :], logit[:, t, 0:EXPERTS], ACT.Exp, bias=neg[:, t:t + 1]).then_inc(exped, 1)


def moe_layer(prog, inp):
    with ExitStack() as own:
        gates, place = (prog.sbuf(n, [P, NT, EXPERTS + 1], own) for n in ("moe_gates", "moe_place"))
        flag = own.enter_context(prog.nc.sbuf_tensor("moe_fits", [P, 1], I32))
        router(prog, inp, gates[:, :, 0:EXPERTS], place, flag)
        moe_experts(prog, "moe", (inp["moe_w1"][0], inp["moe_w3"][0], inp["moe_w2"][0]), gates, place, flag)



NEG = -1.0e30
A_HEADS, A_NOPE, A_ROPE, A_V = 6, 64, 32, 64
Q_LORA, KV_LORA = 768, 256
B_HEADS, C_HEADS, HD = 6, 4, 64
IDX_HEADS, IDX_DIM = 8, 64
TOPK = min(256, S // 4)
ROPE_THETA = 10000.0
DILATED = ((128, 1), (512, 4), (2048, 16))
A_SCALE, BC_SCALE = (A_NOPE + A_ROPE) ** -0.5, HD ** -0.5
SPLIT = (Q_LORA, KV_LORA, A_ROPE, B_HEADS * HD, B_HEADS * HD, B_HEADS * HD, C_HEADS * HD, C_HEADS * HD, C_HEADS * HD,
         IDX_HEADS * IDX_DIM, IDX_DIM, IDX_HEADS, D)
AT = [sum(SPLIT[:i]) for i in range(len(SPLIT) + 1)]
N_BIAS = 1 + B_HEADS + C_HEADS


def attention_constants():
    dist = np.arange(P)[:, None] + (S - P) - np.arange(S)[None, :]
    causal = np.where(dist >= 0, 0.0, NEG)
    slopes = 2.0 ** (-8.0 * np.arange(1, B_HEADS + C_HEADS + 1) / (B_HEADS + C_HEADS))
    count = sum(((dist >= 0) & (dist <= w) & (dist % d == 0)).astype(np.float64) for w, d in DILATED)
    windows = np.where(count > 0, np.log(np.maximum(count, 1)), NEG)
    tables = [causal / A_SCALE]
    tables += [(windows - s * dist * (count > 0)) / BC_SCALE for s in slopes[:B_HEADS]]
    tables += [(causal - s * dist * (dist >= 0)) / BC_SCALE for s in slopes[B_HEADS:]]
    half = A_ROPE // 2
    freqs = ROPE_THETA ** (-np.arange(0, A_ROPE, 2) / A_ROPE)
    angle = (np.arange(S, dtype=np.float32)[None, :] * np.tile(freqs, 2).astype(np.float32)[:, None]).astype(np.float32)
    rot = np.zeros((A_ROPE, A_ROPE))
    for m in range(half):
        rot[m + half, m] = -1.0
        rot[m, m + half] = 1.0
    rope = np.zeros((P, 2 * S + A_ROPE))
    rope[A_NOPE:A_NOPE + A_ROPE] = np.concatenate([np.cos(angle), np.sin(angle), rot], axis=1)
    return np.stack(tables, axis=1).astype(np.float32), rope.astype(np.float32)


def in_columns():
    names = ("cq", "ckv", "kr", "qb", "kb", "vb", "qc", "kc", "vc", "qi", "ki", "wi", "gate")
    order = ("cq", "ckv", "kr", "qb", "kb", "qc", "kc", "qi", "ki", "vb", "vc", "wi", "gate")
    out = []
    for n in order:
        a, b = AT[names.index(n)], AT[names.index(n) + 1]
        out += [(n, c - a, c, min(c + UP_COLS, b)) for c in range(a, b, UP_COLS)]
    return out


def plan_attention(W, inp, l):
    w_in = inp["w_in_2"][l]
    W.plan(f"ada{l}", col_tiles(inp["w_ada_2"][l], UP_COLS))
    W.plan(f"in{l}", [w_in[:, c0:c1].rearrange("(k p) n -> p k n", p=P) for _, _, c0, c1 in in_columns()])
    W.plan(f"uq{l}", col_tiles(inp["w_uq_2"][l], 3 * (A_NOPE + A_ROPE)))
    W.plan(f"ukv{l}", col_tiles(inp["w_uk_2"][l], A_HEADS * A_NOPE) + col_tiles(inp["w_uv_2"][l], A_HEADS * A_V))


def modulation(prog, name, par, gate):
    nc, ps, W = prog.nc, prog.ps, prog.weights
    with ExitStack() as own:
        sc = prog.sbuf(name + "_sc", [P, KD], own)
        mod = prog.sbuf(name + "_mod", [P, 2 * KD], own)
        with Stage(prog, name) as st:
            activated, vector_ready, gate_ready = st.counter("activated"), st.counter("vector_ready"), st.counter("gate_ready")
            link_sem = st.counter("dve_link")

            @st.scalar
            def _(act):
                nc.scalar.activation(sc[:, :], par[:, 0:KD], ACT.Silu).then_inc(activated, 1)

            @st.tensor
            def _(pe):
                pe.wait_ge(activated, 1)
                for j in range(12):
                    w = W.take(pe, name, j)
                    if j < 8:
                        for h in range(2):
                            n = 2 * j + h
                            for k in range(KD):
                                m = nc.tensor.matmul(ps[:, 0, n:n + 1], w[:, k, h * P:(h + 1) * P], sc[:, k:k + 1],
                                                     start=(k == 0), stop=(k == KD - 1))
                                if j and h == 0 and k == 0:
                                    W.leave(m, name, j - 1)
                        if j == 7:
                            m.then_inc(vector_ready, 1)
                    else:
                        for k in range(KD):
                            m = nc.tensor.matmul(ps[:, 1 + (j - 8) // 2, (j % 2) * UP_COLS:(j % 2 + 1) * UP_COLS],
                                                 bc(sc[:, k:k + 1], [P, P]), w[:, k, :], start=(k == 0), stop=(k == KD - 1))
                            if k == 0:
                                W.leave(m, name, j - 1)
                m.then_inc(gate_ready, 1)

            @st.vector
            def _(dve):
                link = linker(dve, link_sem)
                dve.wait_ge(vector_ready, 1)
                link(nc.vector.tensor_tensor(mod[:, :], ps[:, 0, 0:2 * KD], par[:, KD:3 * KD], ALU.add))
                link(nc.vector.tensor_scalar(mod[:, KD:], mod[:, KD:], 1.0, None, ALU.add))
                for k in range(KD):
                    nc.vector.tensor_scalar(prog.x_feat[:, k, :], prog.x_feat[:, k, :], mod[:, KD + k:KD + k + 1],
                                            mod[:, k:k + 1], ALU.mult, ALU.add)
                dve.wait_ge(gate_ready, 1)
                for h in range(2):
                    cs = slice(h * BANK, (h + 1) * BANK)
                    nc.vector.tensor_tensor(gate[:, cs], ps[:, 1 + h, :], par[:, 3 * KD + h * BANK:3 * KD + (h + 1) * BANK],
                                            ALU.add)


def latent_norms(prog, name, c_all, g):
    nc, ps = prog.nc, prog.ps
    nq = Q_LORA // P
    sq, rs = (prog.scratch[:, i * 2 * S:(i + 1) * 2 * S].rearrange("p (a n) -> p a n", a=2) for i in range(2))
    with Stage(prog, name) as st:
        squared, summed, part_done = st.counter("squared"), st.counter("summed"), st.counter("part_done")
        rooted, link_sem = st.counter("rooted"), st.counter("dve_link")

        @st.gpsimd
        def _(pool):
            for k in range(KD):
                if k >= 2:
                    pool.wait_ge(summed, k - 1)
                nc.gpsimd.tensor_tensor(sq[:, k % 2, :], c_all[:, k, :], c_all[:, k, :], ALU.mult).then_inc(squared, 1)

        @st.tensor
        def _(pe):
            for k in range(KD):
                pe.wait_ge(squared, k + 1)
                nc.tensor.matmul(ps[:, int(k >= nq), :], prog.ones, sq[:, k % 2, :], start=k in (0, nq),
                                 stop=k in (nq - 1, KD - 1)).then_inc(summed, 1)

        @st.scalar
        def _(act):
            for i, (k, n) in enumerate(((nq, Q_LORA), (KD, KV_LORA))):
                act.wait_ge(summed, k)
                nc.scalar.activation(rs[:, i, :], ps[:, i, :], ACT.Sqrt, scale=1.0 / n, bias=prog.eps_norm
                                     ).then_inc(rooted, 1)

        @st.vector
        def _(dve):
            link = linker(dve, link_sem)
            for i, ks in enumerate((range(nq), range(nq, KD))):
                dve.wait_ge(rooted, i + 1)
                link(nc.vector.reciprocal(rs[:, i, :], rs[:, i, :]))
                dve.wait_ge(summed, ks[-1] + 1)
                for k in ks:
                    nc.vector.scalar_tensor_tensor(out=c_all[:, k, :], in0=c_all[:, k, :], scalar=g[:, k:k + 1],
                                                   in1=rs[:, i, :], op0=ALU.mult, op1=ALU.mult)


def rotate(prog, name, rope, qa, ka, kr):
    nc, ps = prog.nc, prog.ps
    rows = slice(A_NOPE, A_NOPE + A_ROPE)
    cos, sin, rot = rope[rows, 0:S], rope[rows, S:2 * S], rope[rows, 2 * S:]
    xs = [kr[rows, :]] + [qa[rows, h, :] for h in range(A_HEADS)]
    tmp = prog.scratch[:, 0:2 * S].rearrange("p (a n) -> p a n", a=2)
    with Stage(prog, name) as st:
        turned, cosined, sined, rotated = (st.counter(n) for n in ("turned", "cosined", "sined", "rotated"))

        @st.tensor
        def _(pe):
            for i, x in enumerate(xs):
                nc.tensor.matmul(ps[rows, i, :], rot, x, start=True, stop=True).then_inc(turned, 1)

        @st.gpsimd
        def _(pool):
            for i, x in enumerate(xs):
                pool.wait_ge(turned, i + 1)
                nc.gpsimd.tensor_tensor(x, x, cos, ALU.mult).then_inc(cosined, 1)

        @st.vector
        def _(dve):
            for i, x in enumerate(xs):
                dve.wait_ge(turned, i + 1)
                if i >= 2:
                    dve.wait_ge(rotated, i - 1)
                nc.vector.tensor_tensor(tmp[rows, i % 2, :], ps[rows, i, :], sin, ALU.mult).then_inc(sined, 1)
                dve.wait_ge(sined, i + 1)
                dve.wait_ge(cosined, i + 1)
                nc.vector.tensor_tensor(x, x, tmp[rows, i % 2, :], ALU.add).then_inc(rotated, 1)

        @st.scalar
        def _(act):
            act.wait_ge(rotated, 1)
            for h in range(A_HEADS):
                nc.scalar.activation(ka[rows, h, :], kr[rows, :], ACT.Copy)


def index_select(prog, name, qi, ki, wi, causal, sel):
    nc, ps = prog.nc, prog.ps
    TAKEN = -3.0e38
    relu, score = (prog.scratch[:, i * 2 * S:(i + 1) * 2 * S].rearrange("p (a n) -> p a n", a=2) for i in range(2))
    with ExitStack() as own:
        top = prog.sbuf(name + "_top", [P, 2, 8], own)
        with Stage(prog, name) as st:
            product, relued, summed = st.counter("product"), st.counter("relued"), st.counter("summed")
            link_sem = st.counter("dve_link")
            tiles = range(1, NT)

            @st.tensor
            def _(pe):
                for n, (t, i) in enumerate((t, i) for t in tiles for i in range(IDX_HEADS)):
                    rows = slice((i % 2) * IDX_DIM, (i % 2 + 1) * IDX_DIM)
                    if n >= IDX_HEADS:
                        pe.wait_ge(relued, n - IDX_HEADS + 1)
                    nc.tensor.matmul(ps[:, i, 0:(t + 1) * P], qi[rows, i // 2, t * P:(t + 1) * P], ki[rows, 0:(t + 1) * P],
                                     start=True, stop=True).then_inc(product, 1)

            @st.scalar
            def _(act):
                for n, (t, i) in enumerate((t, i) for t in tiles for i in range(IDX_HEADS)):
                    act.wait_ge(product, n + 1)
                    if n >= 2:
                        act.wait_ge(summed, n - 1)
                    nc.scalar.activation(relu[:, n % 2, 0:(t + 1) * P], ps[:, i, 0:(t + 1) * P], ACT.Relu,
                                         scale=IDX_DIM ** -0.5).then_inc(relued, 1)

            @st.vector
            def _(dve):
                link = linker(dve, link_sem)
                link(nc.vector.tensor_scalar(wi[:, :, :], wi[:, :, :], IDX_HEADS ** -0.5, None, ALU.mult))
                n = 0
                for t in tiles:
                    w = (t + 1) * P
                    x, y = score[:, 0, 0:w], score[:, 1, 0:w]
                    for i in range(IDX_HEADS):
                        before = causal[:, S - w:S] if i == 0 else x
                        dve.wait_ge(relued, n + 1)
                        if n:
                            dve.wait_ge(summed, n)
                        nc.vector.scalar_tensor_tensor(out=x, in0=relu[:, n % 2, 0:w], scalar=wi[:, t, i:i + 1], in1=before,
                                                       op0=ALU.mult, op1=ALU.add).then_inc(summed, 1)
                        n += 1
                    dve.wait_ge(summed, n)
                    for r in range(TOPK // 8):
                        link(nc.vector.max(top[:, 0, :], x))
                        link(nc.vector.match_replace(y, top[:, 0, :], x, TAKEN))
                        x, y = y, x
                    link(nc.vector.tensor_scalar(sel[:, t, 0:w], x, TAKEN / 2, NEG, ALU.is_gt, ALU.mult))


def attend(prog, name, heads, bias, sel, gate, y):
    nc, ps = prog.nc, prog.ps
    units = [(h, t) for h in range(len(heads)) for t in range(NT)]
    U = len(units)
    with ExitStack() as own:
        s_sb = prog.sbuf(name + "_s", [P, 3, S], own)
        p_t = prog.sbuf(name + "_pt", [P, 2, S], own)
        small = prog.sbuf(name + "_small", [P, 4, 4], own)
        with Stage(prog, name) as st:
            s_ready, s_read, neg_ready, p_ready, pt_ready, pt_copied, o_ready, o_read, link_sem, p_read = (
                st.counter(n) for n in ("s_ready", "s_read", "neg_ready", "p_ready", "pt_ready", "pt_copied",
                                       "o_ready", "o_read", "dve_link", "p_read"))

            def keys(u):
                return (units[u][1] + 1) * P

            @st.tensor
            def _(pe):
                def scores(u):
                    h, t = units[u]
                    q, k = heads[h][0], heads[h][1]
                    if u >= 3:
                        pe.wait_ge(s_read, u - 2)
                    nc.tensor.matmul(ps[:, u % 3, 0:keys(u)], q(t * P, (t + 1) * P), k(0, keys(u)), start=True, stop=True
                                     ).then_inc(s_ready, 1)

                def turn(u):
                    pe.wait_ge(p_ready, u + 1)
                    if u >= 2:
                        pe.wait_ge(pt_copied, u - 1)
                    for b in range(keys(u) // P):
                        m = nc.tensor.transpose(ps[:, 3 + u % 2, b * P:(b + 1) * P], s_sb[:, u % 3, b * P:(b + 1) * P],
                                                prog.ident)
                    m.then_inc(pt_ready, 1)

                def values(u):
                    pe.wait_ge(pt_copied, u + 1)
                    if u >= 2:
                        pe.wait_ge(o_read, u - 1)
                    v = heads[units[u][0]][2]
                    nb = keys(u) // P
                    for b in range(nb):
                        m = nc.tensor.matmul(ps[:, 5 + u % 2, 0:HD], p_t[:, u % 2, b * P:(b + 1) * P], v(b),
                                             start=(b == 0), stop=(b == nb - 1))
                    m.then_inc(o_ready, 1)
                for step in range(U + 2):
                    if step < U:
                        scores(step)
                    if 1 <= step <= U:
                        turn(step - 1)
                    if step >= 2:
                        values(step - 2)

            @st.vector
            def _(dve):
                link = linker(dve, link_sem)

                def read_scores(u):
                    h, t = units[u]
                    w, scale, selected = keys(u), heads[h][3], heads[h][5]
                    x, mx, neg = s_sb[:, u % 3, 0:w], small[:, u % 4, 0:1], small[:, u % 4, 1:2]
                    table = bias[:, heads[h][4], S - w:S]
                    dve.wait_ge(s_ready, u + 1)
                    if u >= 3:
                        dve.wait_ge(pt_ready, u - 2)
                    if u >= 4:
                        dve.wait_ge(o_read, u - 3)
                    if selected and t > 0:
                        nc.vector.tensor_tensor(x, ps[:, u % 3, 0:w], table, ALU.add).then_inc(s_read, 1)
                        dve.wait_ge(s_read, u + 1)
                        link(nc.vector.tensor_tensor_reduce(out=x, in0=x, in1=sel[:, t, 0:w], scale=1.0, scalar=-3.0e38,
                                                            op0=ALU.add, op1=ALU.max, accum_out=mx))
                    else:
                        nc.vector.tensor_tensor_reduce(out=x, in0=ps[:, u % 3, 0:w], in1=table, scale=1.0, scalar=-3.0e38,
                                                       op0=ALU.add, op1=ALU.max, accum_out=mx).then_inc(s_read, 1)
                        dve.wait_ge(s_read, u + 1)
                    nc.vector.tensor_scalar(neg, mx, -scale, None, ALU.mult).then_inc(neg_ready, 1)

                def output(u):
                    h, t = units[u]
                    den, inv = small[:, u % 4, 2:3], small[:, u % 4, 3:4]
                    cs = slice(h * HD, (h + 1) * HD)
                    dve.wait_ge(p_ready, u + 1)
                    link(nc.vector.reciprocal(inv, den))
                    dve.wait_ge(o_ready, u + 1)
                    nc.vector.scalar_tensor_tensor(out=y[:, t, cs], in0=ps[:, 5 + u % 2, 0:HD], scalar=inv,
                                                   in1=gate[:, t, cs], op0=ALU.mult, op1=ALU.mult).then_inc(o_read, 1)
                for step in range(U + 2):
                    if step < U:
                        read_scores(step)
                    if step >= 2:
                        output(step - 2)

            @st.scalar
            def _(act):
                for step in range(U + 1):
                    if step < U:
                        u = step
                        x = s_sb[:, u % 3, 0:keys(u)]
                        act.wait_ge(neg_ready, u + 1)
                        nc.scalar.activation(x, x, ACT.Exp, bias=small[:, u % 4, 1:2], scale=heads[units[u][0]][3],
                                             accum_out=small[:, u % 4, 2:3]).then_inc(p_ready, 1)
                    if step >= 1:
                        u = step - 1
                        act.wait_ge(pt_ready, u + 1)
                        if u >= 2:
                            act.wait_ge(o_ready, u - 1)
                        nc.scalar.activation(p_t[:, u % 2, 0:keys(u)], ps[:, 3 + u % 2, 0:keys(u)], ACT.Copy
                                             ).then_inc(pt_copied, 1)


def attention_layer(prog, inp, l, last):
    def new(name, shape, c):
        return prog.sbuf(f"{name}_{l}", shape, c)
    with ExitStack() as own:
        mod_gate = new("mod_gate", [P, D], own)
        with ExitStack() as heads_ctx:
            qa, ka = new("qa", [P, A_HEADS, S], heads_ctx), new("ka", [P, A_HEADS, S], heads_ctx)
            va, vb = new("va", [P, NT, A_HEADS * A_V], heads_ctx), new("vb", [P, NT, B_HEADS * HD], heads_ctx)
            vc = new("vc", [P, NT, C_HEADS * HD], heads_ctx)
            qb, kb = (new(n, [P, B_HEADS // 2, S], heads_ctx) for n in ("qb", "kb"))
            qc, kc = (new(n, [P, C_HEADS // 2, S], heads_ctx) for n in ("qc", "kc"))
            gate, sel = new("gate", [P, NT, D], heads_ctx), new("sel", [P, NT, S], heads_ctx)
            with ExitStack() as early:
                par = new("par", [P, 4 * KD + D], early)
                load_stage(prog, f"att_params{l}", [(par[:, :], inp["att_par"][l])])
                modulation(prog, f"ada{l}", par, mod_gate)
            with ExitStack() as early:
                c_all = new("c_all", [P, KD, S], early)
                qi, ki = new("qi", [P, IDX_HEADS // 2, S], early), new("ki", [P, S], early)
                wi, g = new("wi", [P, NT, IDX_HEADS], early), new("lat_g", [P, KD], early)
                kr = new("kr", [P, S], early)
                feat = {"cq": c_all, "ckv": c_all[:, Q_LORA // P:, :], "qb": qb, "kb": kb, "qc": qc, "kc": kc, "qi": qi}
                groups = []
                for i, (part, at, c0, c1) in enumerate(in_columns()):
                    n = c1 - c0
                    if part in feat:
                        groups += [(i, c, P, None, 0, feat[part][:, (at + c) // P, :], None) for c in range(0, n, P)]
                    elif part == "kr":
                        groups.append((i, 0, A_ROPE, None, A_NOPE, kr[A_NOPE:A_NOPE + A_ROPE, :], None))
                    elif part == "ki":
                        groups += [(i, 0, IDX_DIM, None, r, ki[r:r + IDX_DIM, :], None) for r in (0, IDX_DIM)]
                    else:
                        dst, func = {"vb": (vb, None), "vc": (vc, None), "wi": (wi, None), "gate": (gate, ACT.Silu)}[part]
                        groups += [(i, 0, n, t, 0, dst[:, t, at:at + n], func) for t in range(NT)]
                project(prog, f"in{l}", prog.x_feat, KD, groups)
                load_stage(prog, f"lat_params{l}", [(g[:, :], inp["lat_g"][l])])
                latent_norms(prog, f"lat{l}", c_all, g)
                project(prog, f"uq{l}", c_all[:, 0:Q_LORA // P, :], Q_LORA // P,
                        [(h // 3, (h % 3) * (A_NOPE + A_ROPE), A_NOPE + A_ROPE, None, 0, qa[0:A_NOPE + A_ROPE, h, :], None)
                         for h in range(A_HEADS)])
                project(prog, f"ukv{l}", c_all[:, Q_LORA // P:, :], KV_LORA // P,
                        [(0, h * A_NOPE, A_NOPE, None, 0, ka[0:A_NOPE, h, :], None) for h in range(A_HEADS)]
                        + [(1, 0, A_HEADS * A_V, t, 0, va[:, t, :], None) for t in range(NT)])
                rope, causal = prog.scratch[:, 4 * S:6 * S + A_ROPE], prog.scratch[:, 7 * S:8 * S]
                load_stage(prog, f"tables_in{l}", [(rope, inp["rope"]), (causal, inp["bias"][:, 0, :])])
                rotate(prog, f"rope{l}", rope, qa, ka, kr)
                index_select(prog, f"index{l}", qi, ki, wi, causal, sel)
            with ExitStack() as late:
                bias = new("bias", [P, N_BIAS, S], late)
                load_stage(prog, f"bias_in{l}", [(bias[:, :, :], inp["bias"])])

                def cols(x, rows, h):
                    return lambda a, b: x[rows, h, a:b]

                def vals(x, h):
                    return lambda b: x[:, b, h * HD:(h + 1) * HD]
                full = slice(0, A_NOPE + A_ROPE)
                heads = [(cols(qa, full, h), cols(ka, full, h), vals(va, h), A_SCALE, 0, False) for h in range(A_HEADS)]
                for q, k, v, n, b0, s in ((qb, kb, vb, B_HEADS, 1, False), (qc, kc, vc, C_HEADS, 1 + B_HEADS, True)):
                    for h in range(n):
                        rows = slice((h % 2) * HD, (h % 2 + 1) * HD)
                        heads.append((cols(q, rows, h // 2), cols(k, rows, h // 2), vals(v, h), BC_SCALE, b0 + h, s))
                attend(prog, f"attend{l}", heads, bias, sel, gate, prog.acc)
        transpose_stage(prog, f"att_turn{l}", [([prog.acc[:, t, k * P:(k + 1) * P] for t in range(NT)], prog.x_feat[:, k, :])
                                               for k in range(KD)])
        down_project(prog, f"att_out{l}", prog.x_feat, inp["w_out_2"][l], mod_gate)
        layer_norm(prog, f"att_ln{l}", inp["ln_gb"][4 + l], last)


BIG = ["x", "gdn_w_in", "gdn_w_out", "ffn_w1", "ffn_w3", "ffn_w2", "s5_w_in", "s5_w_glu", "moe_w1", "moe_w3", "moe_w2",
       "w_ada_2", "w_in_2", "w_uq_2", "w_uk_2", "w_uv_2", "w_out_2"]


def plan_rest(prog, W, inp):
    W.plan("s5_u", col_tiles(inp["s5_w_in"][0], UP_COLS))
    glu = col_tiles(inp["s5_w_glu"][0], UP_COLS)
    W.plan("s5_glu", [t for pair in zip(glu[:D // UP_COLS], glu[D // UP_COLS:]) for t in pair])
    W.hold("moe")
    prog.iota_in = inp["iota"]
    for l in range(DEPTH):
        plan_attention(W, inp, l)
    prog.u_dram = prog.nc.dram_tensor("u_turn", (KD, P, S), F32).ap()
    prog.y_dram = prog.nc.dram_tensor("y_turn", (P, GROUPS * NJ), F32).ap()


def rest_steps(prog, inp):
    return [lambda: s5_layer(prog, inp),
            lambda: layer_norm(prog, "s5_ln", inp["ln_gb"][2]),
            lambda: moe_layer(prog, inp),
            lambda: layer_norm(prog, "moe_ln", inp["ln_gb"][3]),
            lambda: attention_layer(prog, inp, 0, False),
            lambda: attention_layer(prog, inp, 1, True)]


def lay_out_rest(f, arr, rep):
    def lanes(a):
        a = a.reshape((PAIRS, 2, GP) + a.shape[2:])
        return np.moveaxis(a, 0, 2).reshape((P, PAIRS) + a.shape[3:])
    vec = [lanes(f["s5_lam_re"][0]), lanes(f["s5_lam_im"][0]),
           lanes(np.broadcast_to(f["s5_log_dt"][0][:, None], (GROUPS, GP)))]
    arr["s5_par"] = np.concatenate([f["s5_d"][0].reshape(KD, P).T] + vec + [rep(np.arange(STEP + 1, dtype=np.float32))], axis=1)
    arr["s5_bc"] = np.stack([lanes(f["s5_b_re"][0]), lanes(f["s5_b_im"][0]),
                             lanes(f["s5_c_re"][0].transpose(0, 2, 1)), lanes(f["s5_c_im"][0].transpose(0, 2, 1))], axis=1)
    arr["moe_wr"] = f["moe_w_router"][0].reshape(KD, P, EXPERTS).transpose(1, 0, 2)
    arr["iota"] = rep(np.arange(SLOT_PAD, dtype=np.float32))
    arr["moe_br"] = rep(f["moe_b_router"][0])

    def feat(a):
        return a.reshape(-1, P).T
    arr["att_par"] = np.stack([np.concatenate([feat(f["c_2"][0]), feat(f["b_ada_2"][l, 0:2 * D]), rep(f["b_ada_2"][l, 2 * D:]),
                                               np.zeros((P, KD), np.float32)], axis=1) for l in range(DEPTH)])
    arr["lat_g"] = np.stack([np.concatenate([feat(f["q_norm_g_2"][l]), feat(f["kv_norm_g_2"][l])], axis=1)
                             for l in range(DEPTH)])
    arr["bias"], arr["rope"] = attention_constants()



def constants():
    i = np.arange(P)
    ident = np.eye(P)
    ones = np.ones((P, P))
    tri = (i[:, None] <= i[None, :]) * 1.0
    levels = []
    for level in range(LEVELS):
        b = 1 << level
        s, c = i[:, None], i[None, :]
        levels.append((s // (2 * b) == c // (2 * b)) & (s % (2 * b) < b) & (c % (2 * b) >= b))
    return np.concatenate([ident, ones, tri] + [m * 1.0 for m in levels], axis=1).astype(np.float32)


def build(nc, inp, out):
    with ExitStack() as ctx:
        prog = Program(nc, ctx)
        prog.out = out
        prog.ps = ctx.enter_context(nc.psum_tensor("ps", [P, 8, BANK], F32))
        ring = prog.sbuf("ring", [P, RING, RING_COLS])
        loaded = [ctx.enter_context(nc.semaphore(f"weights_loaded_{i}")) for i in range(RING)]
        used = ctx.enter_context(nc.semaphore("weights_used"))
        W = prog.weights = Weights(ring, loaded, used)
        prog.x_tok = prog.sbuf("x_tok", [P, NT, D])
        prog.x_feat = prog.sbuf("x_feat", [P, KD, S])
        prog.acc = prog.sbuf("acc", [P, NT, D])
        prog.scratch = prog.acc[:, :, :].rearrange("p t n -> p (t n)")
        cst = prog.sbuf("cst", [P, (3 + LEVELS) * P])
        prog.ident, prog.ones, prog.tri = (cst[:, i * P:(i + 1) * P] for i in range(3))
        prog.level_masks = cst[:, 3 * P:(3 + LEVELS) * P].rearrange("p (l n) -> p l n", n=P)
        eps = prog.sbuf("eps", [P, 2])
        prog.eps_norm, prog.eps_qk = eps[:, 0:1], eps[:, 1:2]

        w_in = inp["gdn_w_in"][0]
        QKV = 3 * HEADS * P
        W.plan("gdn_conv", col_tiles(w_in[:, 0:QKV], UP_COLS))
        W.plan("gdn_ba", col_tiles(w_in[:, QKV + D:QKV + D + 2 * HEADS], UP_COLS))
        W.plan("gdn_z", col_tiles(w_in[:, QKV:QKV + D], UP_COLS))

        ffn1, ffn3 = (inp[n][0].rearrange("k (e n) -> e k n", n=FF_PART) for n in ("ffn_w1", "ffn_w3"))
        ffn2 = inp["ffn_w2"][0].rearrange("(e k) n -> e k n", k=FF_PART)
        W.hold("ffn")
        plan_rest(prog, W, inp)

        with Stage(prog, "setup") as st:
            landed, eps_set = st.counter("landed"), st.counter("eps_set")

            @st.sync
            def _(sp):
                sp.dma_start(prog.x_tok[:, :, :], inp["x"][0].rearrange("(t p) n -> p t n", p=P)).then_inc(landed, 16)
                sp.dma_start(cst[:, :], inp["cst"]).then_inc(landed, 16)
                sp.wait_ge(landed, 32)

            @st.gpsimd
            def _(pool):
                nc.gpsimd.memset(eps[:, 0:1], NORM_EPS)
                nc.gpsimd.memset(eps[:, 1:2], NORM_EPS * P)
        turn_x = [([prog.x_tok[:, t, k * P:(k + 1) * P] for t in range(NT)], prog.x_feat[:, k, :]) for k in range(KD)]
        transpose_stage(prog, "setup_turn", turn_x)

        steps = [
            lambda: gdn_layer(prog, inp),
            lambda: layer_norm(prog, "gdn_ln", inp["ln_gb"][0]),
            lambda: dense_ffn(prog, "ffn", ffn1, ffn3, ffn2, 2),
            lambda: layer_norm(prog, "ffn_ln", inp["ln_gb"][1]),
        ] + rest_steps(prog, inp)
        for step in steps:
            step()



def lay_out(inputs):
    f = {n: np.ascontiguousarray(np.asarray(a)) for n, a in inputs.items()}
    arr = {n: f[n] for n in BIG}

    def rep(a):
        return np.broadcast_to(a, (P,) + a.shape)
    taps = f["gdn_conv_w"][0].T.reshape(3 * HEADS, P, 4).transpose(1, 0, 2).reshape(P, -1)
    arr["gdn_taps"] = taps
    arr["gdn_par"] = rep(np.concatenate([f["gdn_dt_bias"][0], f["gdn_a_log"][0], f["gdn_norm_g"][0]]))
    gb = np.stack([f["ln_g"].reshape(4, D), f["ln_b"].reshape(4, D)], axis=1)
    gb2 = np.stack([f["ln_g_2"], f["ln_b_2"]], axis=1)
    arr["ln_gb"] = np.stack([rep(a) for a in np.concatenate([gb, gb2])])
    arr["cst"] = constants()
    lay_out_rest(f, arr, rep)
    return {n: np.ascontiguousarray(a) for n, a in arr.items()}


def kernel(**inputs):
    import concourse.bacc as bacc
    from concourse.bass_utils import run_bass_kernel_spmd

    nc = bacc.Bacc("TRN2", target_bir_lowering=False, num_devices=1)
    arrays = {f"in_{n}": a for n, a in lay_out(inputs).items()}
    inp = {n[3:]: nc.dram_tensor(n, a.shape, F32, kind="ExternalInput").ap() for n, a in arrays.items()}
    out = nc.dram_tensor("out_0", (S, D), F32, kind="ExternalOutput").ap()
    build(nc, inp, out)
    r = run_bass_kernel_spmd(nc, [arrays], core_ids=[0])
    return r.results[0]["out_0"].reshape(1, S, D)
```

```python
from contextlib import ExitStack

import numpy as np

import concourse.bass as bass
from concourse import mybir

F32 = mybir.dt.float32
F32R = mybir.dt.float32r
ALU = mybir.AluOpType
ACT = mybir.ActivationFunctionType
AX_X = mybir.AxisListType.X

P = 128
D = 1024
KD = D // P
S = 512
NT = S // P
BANK = 512
DEPTH = 2
ALPHA = (2 * DEPTH) ** 0.25
LN_EPS = 1e-5
NORM_EPS = 1e-6

HEADS = 8
CH = 128
NCH = S // CH
LEVELS = 7
HG = 4

FF_PART = 1408
FT = FF_PART // P
EXPERTS = 8

RING = 4
RING_COLS = 2048
UP_COLS = 256


class Weights:

    def __init__(self, ring, ring_r, loaded, used):
        self.ring, self.ring_r, self.loaded, self.used = ring, ring_r, loaded, used
        self.tiles, self.first, self.size, self.holds = [], {}, {}, {}
        self.n_loads = [0] * RING
        self.released, self.n_released, self.issued, self.passed = {}, 0, 0, 0

    def hold(self, stage):
        self.holds[len(self.tiles)] = self.holds.get(len(self.tiles), []) + [stage]

    def plan(self, stage, sources):
        self.first[stage], self.size[stage] = len(self.tiles), len(sources)
        for src in sources:
            slot = len(self.tiles) % RING
            self.n_loads[slot] += 1
            self.tiles.append((src, slot, 16 * self.n_loads[slot]))

    def view(self, index, lo=False):
        src, slot, _ = self.tiles[index]
        k, n = src.shape[1], src.shape[2]
        return (self.ring_r if lo else self.ring)[:, slot, 0:k * n].rearrange("p (k n) -> p k n", n=n)

    def flat(self, stage, i):
        src, slot, _ = self.tiles[self.first[stage] + i]
        return [r[:, slot, 0:src.shape[1] * src.shape[2]] for r in (self.ring, self.ring_r)]

    def arrived(self, eng, stage, i):
        _, slot, ready = self.tiles[self.first[stage] + i]
        eng.wait_ge(self.loaded[slot], ready)

    def take(self, pe, stage, i):
        self.arrived(pe, stage, i)
        return self.view(self.first[stage] + i)

    def leave(self, matmul, stage, i):
        matmul.then_inc(self.used, 1)
        self.n_released += 1
        self.released[self.first[stage] + i] = self.n_released

    def load(self, sp, index):
        src, slot, _ = self.tiles[index]
        sp.dma_start(self.view(index), src).then_inc(self.loaded[slot], 16)

    def fill(self, sp, stage):
        while self.issued < len(self.tiles):
            n, old = self.issued, self.issued - RING
            if self.holds.get(n):
                break
            if old >= self.passed:
                if old not in self.released:
                    break
                sp.wait_ge(self.used, self.released[old])
            self.load(sp, n)
            self.issued += 1
        for stages in self.holds.values():
            if stage in stages:
                stages.remove(stage)
        if stage in self.first:
            self.passed = self.first[stage] + self.size[stage]


class Program:

    def __init__(self, nc, ctx):
        self.nc, self.ctx = nc, ctx
        self.sets = [[ctx.enter_context(nc.semaphore(f"{w}_{i}")) for i in range(56)] for w in ("even", "odd")]
        self.turn, self.dirty = 0, []

    def sbuf(self, name, shape, ctx=None):
        return (ctx or self.ctx).enter_context(self.nc.sbuf_tensor(name, shape, F32))


class Stage:

    def __init__(self, prog, name):
        self.prog, self.name = prog, name
        self.loads, self.after = None, None

    def __enter__(self):
        self.block_ctx = self.prog.nc.Block()
        self.block = self.block_ctx.__enter__()
        self.free = list(self.prog.sets[self.prog.turn])
        self.taken = []
        self.tensor, self.vector = self.block.tensor, self.block.vector
        self.scalar, self.gpsimd = self.block.scalar, self.block.gpsimd
        return self

    def counter(self, name):
        self.taken.append(self.free.pop(0))
        return self.taken[-1]

    def sync(self, f):
        self.loads = f
        return f

    def __exit__(self, *exc):
        if exc[0] is not None:
            return False

        @self.block.sync
        def _(sp):
            for s in self.prog.dirty:
                sp.sem_clear(s)
            if self.loads:
                self.loads(sp)
            self.prog.weights.fill(sp, self.name)
        self.block_ctx.__exit__(None, None, None)
        self.prog.dirty, self.prog.turn = self.taken, 1 - self.prog.turn
        return False


def linker(eng, sem):
    count = [0]

    def link(ins):
        count[0] += 1
        ins.then_inc(sem, 1)
        eng.wait_ge(sem, count[0])
    return link


def bc(ap, shape):
    return ap.to_broadcast(shape)


def col_tiles(w, width):
    n = w.shape[1]
    return [w[:, c:min(c + width, n)].rearrange("(k p) n -> p k n", p=P) for c in range(0, n, width)]


class SplitTiles:
    QUARTERS = 4

    def __init__(self, prog, st, name, hi):
        self.nc, self.W, self.name, self.hi = prog.nc, prog.weights, name, hi
        self.hi_done, self.lo_done = st.counter("hi_done"), st.counter("lo_done")
        self.size, self.awaited = self.W.size[name], 0

    def pieces(self, j):
        n = self.W.flat(self.name, j)[0].shape[1]
        if j:
            return [(slice(0, n), self.QUARTERS + j)]
        q = n // self.QUARTERS
        return [(slice(i * q, (i + 1) * q), i + 1) for i in range(self.QUARTERS)]

    def split_hi(self, act, j):
        W = self.W
        if j >= self.size:
            return
        x, _ = W.flat(self.name, j)
        W.arrived(act, self.name, j)
        if j >= 2:
            act.wait_ge(W.used, W.released[W.first[self.name] + j - 2])
        for cs, _ in self.pieces(j):
            self.nc.scalar.activation(self.hi[:, j % 2, cs], x[:, cs], ACT.Copy).then_inc(self.hi_done, 1)

    def split_lo(self, dve, j):
        if j >= self.size:
            return
        x, lo = self.W.flat(self.name, j)
        for cs, n in self.pieces(j):
            dve.wait_ge(self.hi_done, n)
            self.nc.vector.tensor_tensor(lo[:, cs], x[:, cs], self.hi[:, j % 2, cs].bitcast(F32), ALU.subtract
                                         ).then_inc(self.lo_done, 1)

    def quarter(self, pe, j, q):
        if j == 0 and q >= self.awaited:
            self.awaited = q + 1
            pe.wait_ge(self.lo_done, q + 1)

    def take(self, pe, j):
        lo = self.W.view(self.W.first[self.name] + j, True)
        if j:
            pe.wait_ge(self.lo_done, self.QUARTERS + j)
        k, n = lo.shape[1], lo.shape[2]
        return self.hi[:, j % 2, 0:k * n].rearrange("p (k n) -> p k n", n=n), lo


def three_pass(nc, out, left, right, first, last, leave=None):
    (lh, ll), (rh, rl) = left, right
    m = nc.tensor.matmul(out, lh, rh, start=first, stop=False)
    if leave is not None:
        leave(m)
    nc.tensor.matmul(out, lh, rl, start=False, stop=False)
    return nc.tensor.matmul(out, ll, rh, start=False, stop=last)


def hi_slots(prog, own, name):
    return own.enter_context(prog.nc.sbuf_tensor(name, [P, 2, RING_COLS], F32R))[:, :, :]



def load_meanwhile(st, pairs):
    landed = st.counter("landed")

    @st.sync
    def _(sp):
        for dst, src in pairs:
            sp.dma_start(dst, src).then_inc(landed, 16)
        sp.wait_ge(landed, 16 * len(pairs))


def project(prog, name, srcs, groups, hi=None, meanwhile=()):
    nc, W, ps = prog.nc, prog.weights, prog.ps
    NB = 8
    by_act = [g[6] is not None or i % 2 == 0 for i, g in enumerate(groups)]
    order = [sum(by_act[:i + 1]) if a else i + 1 - sum(by_act[:i + 1]) for i, a in enumerate(by_act)]
    k_tiles = srcs[0].shape[1]
    n_tiles = W.size[name]

    def result(i):
        _, _, width, tok, rows, _, _ = groups[i]
        return ps[rows, i % NB, :] if tok is None else ps[:, i % NB, 0:width]

    with Stage(prog, name) as st:
        product = st.counter("product")
        act_copied = st.counter("act_copied")
        dve_copied = st.counter("dve_copied")
        tiles = SplitTiles(prog, st, name, hi) if hi is not None else None
        if meanwhile:
            load_meanwhile(st, meanwhile)

        @st.tensor
        def _(pe):
            held, w = None, None
            for i, (tile, c, width, tok, rows, _, _) in enumerate(groups):
                left = held if tile != held else None
                if tile != held:
                    w = tiles.take(pe, tile) if tiles else W.take(pe, name, tile)
                    held = tile

                def leave(m):
                    if left is not None:
                        W.leave(m, name, left)
                if i >= NB:
                    pe.wait_ge(act_copied if by_act[i - NB] else dve_copied, order[i - NB])
                if tiles:
                    for k in range(k_tiles):
                        tiles.quarter(pe, tile, k // 2)
                        wk = [x[:, k, c:c + width] for x in w]
                        if tok is None:
                            pair = wk, [x[:, k, :] for x in srcs]
                            out = ps[:, i % NB, :]
                        else:
                            pair = [x[:, k, tok * P:(tok + 1) * P] for x in srcs], wk
                            out = ps[:, i % NB, 0:width]
                        m = three_pass(nc, out, *pair, k == 0, k == k_tiles - 1, leave if k == 0 else None)
                else:
                    for n, (x, k) in enumerate((x, k) for x in srcs for k in range(k_tiles)):
                        last = n == len(srcs) * k_tiles - 1
                        if tok is None:
                            m = nc.tensor.matmul(result(i), w[:, k, c:c + width], x[:, k, :], start=(n == 0), stop=last)
                        else:
                            m = nc.tensor.matmul(result(i), x[:, k, tok * P:(tok + 1) * P], w[:, k, c:c + width],
                                                 start=(n == 0), stop=last)
                        if n == 0:
                            leave(m)
                m.then_inc(product, 1)

        def in_turn(split, copy_out):
            if tiles:
                split(0)
                split(1)
            for tile in range(n_tiles):
                for i, g in enumerate(groups):
                    if g[0] == tile:
                        copy_out(i, g)
                if tiles:
                    split(tile + 2)

        @st.scalar
        def _(act):
            def copy_out(i, g):
                if by_act[i]:
                    act.wait_ge(product, i + 1)
                    nc.scalar.activation(g[5], result(i), g[6] or ACT.Copy).then_inc(act_copied, 1)
            in_turn(lambda j: tiles.split_hi(act, j), copy_out)

        @st.vector
        def _(dve):
            def copy_out(i, g):
                if not by_act[i]:
                    dve.wait_ge(product, i + 1)
                    nc.vector.tensor_copy(g[5], result(i)).then_inc(dve_copied, 1)
            in_turn(lambda j: tiles.split_lo(dve, j), copy_out)


def turn_split(prog, name, jobs, meanwhile=()):
    nc, ps = prog.nc, prog.ps
    with Stage(prog, name) as st:
        turned, hi_done, lo_done = st.counter("turned"), st.counter("hi_done"), st.counter("lo_done")
        if meanwhile:
            load_meanwhile(st, meanwhile)

        @st.tensor
        def _(pe):
            for i, (sources, _, _) in enumerate(jobs):
                if i >= 8:
                    pe.wait_ge(lo_done, i - 7)
                for j, s in enumerate(sources):
                    m = nc.tensor.transpose(ps[:, i % 8, j * P:(j + 1) * P], s, prog.ident)
                m.then_inc(turned, 1)

        @st.scalar
        def _(act):
            for i, (_, hi, _) in enumerate(jobs):
                act.wait_ge(turned, i + 1)
                nc.scalar.activation(hi, ps[:, i % 8, :], ACT.Copy).then_inc(hi_done, 1)

        @st.vector
        def _(dve):
            for i, (_, hi, lo) in enumerate(jobs):
                dve.wait_ge(hi_done, i + 1)
                nc.vector.tensor_tensor(lo, ps[:, i % 8, :], hi.bitcast(F32), ALU.subtract).then_inc(lo_done, 1)


def transpose_stage(prog, name, jobs):
    nc, ps, ident = prog.nc, prog.ps, prog.ident
    with Stage(prog, name) as st:
        turned = st.counter("turned")
        act_copied = st.counter("act_copied")
        dve_copied = st.counter("dve_copied")

        @st.tensor
        def _(pe):
            for i, (sources, _) in enumerate(jobs):
                if i >= 8:
                    pe.wait_ge((act_copied, dve_copied)[i % 2], (i - 8) // 2 + 1)
                for j, s in enumerate(sources):
                    m = nc.tensor.transpose(ps[:, i % 8, j * P:(j + 1) * P], s, ident)
                m.then_inc(turned, 1)

        def out(i):
            return ps[:, i % 8, 0:len(jobs[i][0]) * P]

        def fit(dst, src):
            return src.rearrange("p (a b) -> p a b", b=dst.shape[-1]) if len(dst.shape) == 3 else src

        @st.scalar
        def _(act):
            for i in range(0, len(jobs), 2):
                act.wait_ge(turned, i + 1)
                nc.scalar.activation(jobs[i][1], fit(jobs[i][1], out(i)), ACT.Copy).then_inc(act_copied, 1)

        @st.vector
        def _(dve):
            for i in range(1, len(jobs), 2):
                dve.wait_ge(turned, i + 1)
                nc.vector.tensor_copy(jobs[i][1], fit(jobs[i][1], out(i))).then_inc(dve_copied, 1)


def row_tiles(w):
    return [w[2 * q * P:(2 * q + 2) * P, :].rearrange("(k p) n -> p k n", p=P) for q in range(KD // 2)]


def down_project(prog, name, src, gate=None):
    nc, ps, W = prog.nc, prog.ps, prog.weights
    with ExitStack() as own:
        hi = hi_slots(prog, own, name + "_hi")
        with Stage(prog, name) as st:
            product, summed = st.counter("product"), st.counter("summed")
            tiles = SplitTiles(prog, st, name, hi)

            @st.tensor
            def _(pe):
                for k in range(KD):
                    if k % 2 == 0:
                        w = tiles.take(pe, k // 2)

                    def leave(m):
                        W.leave(m, name, k // 2 - 1)
                    for i in range(2 * NT):
                        tiles.quarter(pe, k // 2, 2 * (k % 2) + i % 2)
                        m = three_pass(nc, ps[:, i, :], [x[:, k, (i // 2) * P:(i // 2 + 1) * P] for x in src],
                                       [x[:, k % 2, (i % 2) * BANK:(i % 2 + 1) * BANK] for x in w],
                                       k == 0, k == KD - 1, leave if k and k % 2 == 0 and i == 0 else None)
                        if k == KD - 1:
                            m.then_inc(product, 1)

            @st.scalar
            def _(act):
                for j in range(KD // 2):
                    tiles.split_hi(act, j)

            @st.vector
            def _(dve):
                for j in range(KD // 2):
                    tiles.split_lo(dve, j)
                for i in range(2 * NT):
                    t, c = i // 2, slice((i % 2) * BANK, (i % 2 + 1) * BANK)
                    dve.wait_ge(product, i + 1)
                    out = prog.acc[:, t, c]
                    if gate is None:
                        nc.vector.scalar_tensor_tensor(out=out, in0=prog.x_tok[:, t, c], scalar=ALPHA,
                                                       in1=ps[:, i, :], op0=ALU.mult, op1=ALU.add)
                    else:
                        nc.vector.scalar_tensor_tensor(out=out, in0=gate[:, c], scalar=1.0, in1=ps[:, i, :],
                                                       op0=ALU.add, op1=ALU.mult).then_inc(summed, 1)
                if gate is not None:
                    dve.wait_ge(summed, 2 * NT)
                    for t in range(NT):
                        nc.vector.scalar_tensor_tensor(out=prog.acc[:, t, :], in0=prog.x_tok[:, t, :], scalar=ALPHA,
                                                       in1=prog.acc[:, t, :], op0=ALU.mult, op1=ALU.add)


def layer_norm(prog, name, gb_src, last=False, split=True, meanwhile=()):
    nc, ps, acc, x_tok = prog.nc, prog.ps, prog.acc, prog.x_tok
    with ExitStack() as own:
        gb = prog.sbuf(name + "_gb", [P, 2, D], own)
        stats = prog.sbuf(name + "_stats", [P, NT, 12], own)
        mv = prog.sbuf(name + "_mv", [P, NT, 2], own)
        var = prog.sbuf(name + "_var", [P, NT], own)
        sd = prog.sbuf(name + "_sd", [P, NT], own)
        rs = prog.sbuf(name + "_rs", [P, NT], own)
        with Stage(prog, name) as st:
            landed, loaded = st.counter("landed"), st.counter("loaded")
            dve_link, var_ready = st.counter("dve_link"), st.counter("var_ready")
            sd_ready, normed = st.counter("sd_ready"), st.counter("normed")
            done, stored = st.counter("done"), st.counter("stored")
            turned, act_copied = st.counter("turned"), st.counter("act_copied")

            @st.sync
            def _(sp):
                sp.dma_start(gb[:, :, :], gb_src).then_inc(landed, 16)
                for dst, src in meanwhile:
                    sp.dma_start(dst, src).then_inc(loaded, 16)
                if meanwhile:
                    sp.wait_ge(loaded, 16 * len(meanwhile))
                if last:
                    for t in range(NT):
                        sp.wait_ge(done, t + 1)
                        sp.dma_start(prog.out[t * P:(t + 1) * P, :], x_tok[:, t, :]).then_inc(stored, 16)
                    sp.wait_ge(stored, 16 * NT)

            def bank(t, h):
                return ps[:, 2 * t + h, :].rearrange("p (k n) -> p k n", n=P)

            def dst(x, t, h):
                return x[:, 4 * h:4 * h + 4, t * P:(t + 1) * P]

            def copy_out(dve, t):
                for h in range(2) if split else (1,):
                    if split:
                        dve.wait_ge(act_copied, 2 * t + h + 1)
                        nc.vector.tensor_tensor(dst(prog.x_lo, t, h), bank(t, h), dst(prog.x_hi, t, h).bitcast(F32),
                                                ALU.subtract)
                    else:
                        dve.wait_ge(turned, 2 * t + 2)
                        nc.vector.tensor_copy(dst(prog.x_feat, t, h), bank(t, h))

            @st.vector
            def _(dve):
                link = linker(dve, dve_link)
                for t in range(NT):
                    for h in range(2):
                        m = nc.vector.bn_stats(stats[:, t, 6 * h:6 * h + 6], acc[:, t, h * BANK:(h + 1) * BANK])
                link(m)
                for t in range(NT):
                    m = nc.vector.bn_aggr(mv[:, t, :], stats[:, t, :])
                link(m)
                nc.vector.tensor_scalar(var[:, :], mv[:, :, 1], LN_EPS, None, ALU.add).then_inc(var_ready, 1)
                dve.wait_ge(sd_ready, 1)
                link(nc.vector.reciprocal(rs[:, :], sd[:, :]))
                dve.wait_ge(landed, 16)
                for t in range(NT):
                    link(nc.vector.tensor_scalar(acc[:, t, :], acc[:, t, :], mv[:, t, 0:1], rs[:, t:t + 1],
                                                 ALU.subtract, ALU.mult))
                    nc.vector.tensor_tensor(acc[:, t, :], acc[:, t, :], gb[:, 0, :], ALU.mult).then_inc(normed, 1)
                    if not last and t >= 1:
                        copy_out(dve, t - 1)
                if not last:
                    copy_out(dve, NT - 1)

            @st.gpsimd
            def _(pool):
                pool.wait_ge(landed, 16)
                for t in range(NT):
                    pool.wait_ge(normed, t + 1)
                    nc.gpsimd.tensor_tensor(x_tok[:, t, :], acc[:, t, :], gb[:, 1, :], ALU.add).then_inc(done, 1)

            @st.scalar
            def _(act):
                act.wait_ge(var_ready, 1)
                nc.scalar.activation(sd[:, :], var[:, :], ACT.Sqrt).then_inc(sd_ready, 1)
                if not last:
                    for t in range(NT):
                        for h in range(2) if split else (0,):
                            act.wait_ge(turned, 2 * t + h + 1)
                            nc.scalar.activation(dst(prog.x_hi if split else prog.x_feat, t, h), bank(t, h), ACT.Copy
                                                 ).then_inc(act_copied, 1)

            @st.tensor
            def _(pe):
                if not last:
                    for t in range(NT):
                        pe.wait_ge(done, t + 1)
                        for k in range(KD):
                            m = nc.tensor.transpose(ps[:, 2 * t + k // 4, (k % 4) * P:(k % 4 + 1) * P],
                                                    x_tok[:, t, k * P:(k + 1) * P], prog.ident)
                            if k % 4 == 3:
                                m.then_inc(turned, 1)



def gdn_conv(prog, name, dests, taps, hi):
    nc, W, ps = prog.nc, prog.weights, prog.ps
    NF, PAD = len(dests), 3
    with ExitStack() as own:
        padded = prog.sbuf(name + "_padded", [P, 2, PAD + S], own)
        conv = prog.sbuf(name + "_conv", [P, 2, S], own)
        with Stage(prog, name) as st:
            product, copied = st.counter("product"), st.counter("copied")
            convolved, activated = st.counter("convolved"), st.counter("activated")
            zeroed, dve_link = st.counter("zeroed"), st.counter("dve_link")
            tiles = SplitTiles(prog, st, name, hi)

            @st.gpsimd
            def _(pool):
                nc.gpsimd.memset(padded[:, :, 0:PAD], 0.0).then_inc(zeroed, 1)

            @st.tensor
            def _(pe):
                for f in range(NF):
                    if f % 2 == 0:
                        w = tiles.take(pe, f // 2)
                    if f >= 4:
                        pe.wait_ge(copied, f - 3)
                    for k in range(KD):
                        tiles.quarter(pe, f // 2, k // 2)
                        m = three_pass(nc, ps[:, f % 4, :], [x[:, k, (f % 2) * P:(f % 2 + 1) * P] for x in w],
                                       (prog.x_hi[:, k, :], prog.x_lo[:, k, :]), k == 0, k == KD - 1,
                                       (lambda m: W.leave(m, name, f // 2 - 1)) if k == 0 and f % 2 == 0 and f else None)
                    m.then_inc(product, 1)

            @st.scalar
            def _(act):
                def silu(f):
                    act.wait_ge(convolved, f + 1)
                    nc.scalar.activation(dests[f], conv[:, f % 2, :], ACT.Silu).then_inc(activated, 1)
                tiles.split_hi(act, 0)
                tiles.split_hi(act, 1)
                for f in range(NF):
                    if f % 2 == 0 and f:
                        tiles.split_hi(act, f // 2 + 1)
                    act.wait_ge(product, f + 1)
                    if f >= 2:
                        act.wait_ge(convolved, f - 1)
                    nc.scalar.activation(padded[:, f % 2, PAD:PAD + S], ps[:, f % 4, :], ACT.Copy).then_inc(copied, 1)
                    if f:
                        silu(f - 1)
                silu(NF - 1)

            @st.vector
            def _(dve):
                link = linker(dve, dve_link)
                dve.wait_ge(zeroed, 1)
                tiles.split_lo(dve, 0)
                tiles.split_lo(dve, 1)
                for f in range(NF):
                    if f % 2 == 0 and f:
                        tiles.split_lo(dve, f // 2 + 1)
                    dve.wait_ge(copied, f + 1)
                    if f >= 2:
                        dve.wait_ge(activated, f - 1)
                    out, x = conv[:, f % 2, :], padded[:, f % 2, :]
                    link(nc.vector.tensor_scalar(out, x[:, 0:S], taps[:, 4 * f:4 * f + 1], None, ALU.mult))
                    for j in (1, 2, 3):
                        m = nc.vector.scalar_tensor_tensor(out=out, in0=x[:, j:j + S], scalar=taps[:, 4 * f + j:4 * f + j + 1],
                                                           in1=out, op0=ALU.mult, op1=ALU.add)
                        if j < 3:
                            link(m)
                    m.then_inc(convolved, 1)


PICK_ROW = 2 * (32 + HEADS) - 1


def gdn_norms(prog, name, q, k):
    nc, ps = prog.nc, prog.ps
    K_ROW = 32
    ROWS = K_ROW + HEADS
    tiles = [(q[:, h, :], h) for h in range(HEADS)] + [(k[:, h, :], K_ROW + h) for h in range(HEADS)]
    n = len(tiles)
    with ExitStack() as own:
        sq = prog.sbuf(name + "_sq", [P, 2, S], own)
        norm = prog.sbuf(name + "_norm", [P, S], own)
        with Stage(prog, name) as st:
            squared = [st.counter(f"squared_{i}") for i in range(2)]
            summed, rooted, inverted = st.counter("summed"), st.counter("rooted"), st.counter("inverted")
            spread, done = st.counter("spread"), st.counter("done")

            @st.gpsimd
            def _(pool):
                for i in range(1, n, 2):
                    if i >= 2:
                        pool.wait_ge(summed, i - 1)
                    nc.gpsimd.tensor_tensor(sq[:, 1, :], tiles[i][0], tiles[i][0], ALU.mult).then_inc(squared[1], 1)

            @st.tensor
            def _(pe):
                for i, (_, row) in enumerate(tiles):
                    pe.wait_ge(squared[i % 2], i // 2 + 1)
                    nc.tensor.matmul(ps[0:ROWS, 0, :], prog.pick_row[:, ROWS - 1 - row:2 * ROWS - 1 - row], sq[:, i % 2, :],
                                     start=(i == 0), stop=(i == n - 1)).then_inc(summed, 1)
                pe.wait_ge(inverted, 1)
                for i, (_, row) in enumerate(tiles):
                    if i >= 4:
                        pe.wait_ge(done, i - 3)
                    nc.tensor.matmul(ps[:, 1 + i % 4, :], bc(prog.ident[0:ROWS, row:row + 1], [ROWS, P]), norm[0:ROWS, :],
                                     start=True, stop=True).then_inc(spread, 1)

            @st.scalar
            def _(act):
                for i in range(0, n, 2):
                    if i >= 2:
                        act.wait_ge(summed, i - 1)
                    nc.scalar.activation(sq[:, 0, :], tiles[i][0], ACT.Square).then_inc(squared[0], 1)
                act.wait_ge(summed, n)
                nc.scalar.activation(norm[0:ROWS, :], ps[0:ROWS, 0, :], ACT.Sqrt, bias=prog.eps_norm[0:ROWS, :]
                                     ).then_inc(rooted, 1)
                act.wait_ge(rooted, 1)
                nc.scalar.activation(norm[0:HEADS, :], ps[0:HEADS, 0, :], ACT.Sqrt, scale=float(P),
                                     bias=prog.eps_qk[0:HEADS, :]).then_inc(rooted, 1)

            @st.vector
            def _(dve):
                dve.wait_ge(rooted, 2)
                nc.vector.reciprocal(norm[0:ROWS, :], norm[0:ROWS, :]).then_inc(inverted, 1)
                for i, (x, _) in enumerate(tiles):
                    dve.wait_ge(spread, i + 1)
                    nc.vector.tensor_tensor(x, x, ps[:, 1 + i % 4, :], ALU.mult).then_inc(done, 1)


def gdn_gates(prog, name, ba, params, small):
    nc, ps = prog.nc, prog.ps
    g, beta, G, beG, kd, eL, t0, t1, neg_a = small
    b, a = ba[:, :, 0:HEADS], ba[:, :, HEADS:2 * HEADS]
    dt_bias, a_log = params[:, 0:HEADS], params[:, HEADS:2 * HEADS]
    rep = [P, NCH, HEADS]

    def over(x):
        return x.unsqueeze(1).to_broadcast(rep)

    def flat(x):
        return x.rearrange("p c h -> p (c h)")
    with Stage(prog, name) as st:
        acted, link_sem = st.counter("acted"), st.counter("dve_link")
        x_ready, a_ready, e_ready = st.counter("x_ready"), st.counter("a_ready"), st.counter("e_ready")
        g_ready, sums, diff = st.counter("g_ready"), st.counter("sums"), st.counter("diff")

        @st.scalar
        def _(act):
            nc.scalar.activation(beta, b, ACT.Sigmoid).then_inc(acted, 1)
            nc.scalar.activation(neg_a, a_log, ACT.Exp).then_inc(acted, 1)
            act.wait_ge(x_ready, 1)
            nc.scalar.activation(t1, t1, ACT.Exp, scale=-1.0).then_inc(acted, 1)
            act.wait_ge(acted, 3)
            nc.scalar.activation(t1, t1, ACT.Ln, bias=1.0).then_inc(acted, 1)
            act.wait_ge(diff, 1)
            nc.scalar.activation(kd, kd, ACT.Exp).then_inc(acted, 1)
            nc.scalar.activation(eL, ps[:, 1, 0:NCH * HEADS].rearrange("p (c h) -> p c h", h=HEADS), ACT.Exp
                                 ).then_inc(acted, 1)
            nc.scalar.activation(beG, G, ACT.Exp).then_inc(acted, 1)

        @st.vector
        def _(dve):
            link = linker(dve, link_sem)
            link(nc.vector.tensor_tensor(t0, a, over(dt_bias), ALU.add))
            link(nc.vector.tensor_scalar(t1, t0, -1.0, None, ALU.mult))
            nc.vector.tensor_tensor(t1, t0, t1, ALU.max).then_inc(x_ready, 1)
            link(nc.vector.tensor_scalar(t0, t0, 0.0, None, ALU.max))
            dve.wait_ge(acted, 4)
            link(nc.vector.tensor_tensor(t0, t0, t1, ALU.add))
            nc.vector.scalar_tensor_tensor(out=g, in0=t0, scalar=-1.0, in1=over(neg_a),
                                           op0=ALU.mult, op1=ALU.mult).then_inc(g_ready, 1)
            dve.wait_ge(sums, 2)
            link(nc.vector.tensor_copy(flat(G), ps[:, 0, 0:NCH * HEADS]))
            nc.vector.tensor_tensor(flat(kd), ps[:, 1, 0:NCH * HEADS], flat(G), ALU.subtract).then_inc(diff, 1)
            dve.wait_ge(acted, 7)
            link(nc.vector.tensor_tensor(beG, beG, beta, ALU.mult))

        @st.tensor
        def _(pe):
            pe.wait_ge(g_ready, 1)
            nc.tensor.matmul(ps[:, 0, 0:NCH * HEADS], prog.tri, flat(g), start=True, stop=True).then_inc(sums, 1)
            nc.tensor.matmul(ps[:, 1, 0:NCH * HEADS], prog.ones, flat(g), start=True, stop=True).then_inc(sums, 1)


def gdn_decays(prog, name, h0, q, k, g, G, dec, att, am):
    nc, ps = prog.nc, prog.ps
    eg = prog.acc[:, 0:2, h0 * P:(h0 + HG) * P]
    with Stage(prog, name) as st:
        product = st.counter("product")
        shifted, decayed, masked = st.counter("shifted"), st.counter("decayed"), st.counter("masked")
        grown, scaled, weighted = st.counter("grown"), st.counter("scaled"), st.counter("weighted")

        @st.tensor
        def _(pe):
            for i in range(HG):
                b0 = 4 * (i % 2)
                if i >= 2:
                    pe.wait_ge(weighted, 2 * (i - 1))
                    pe.wait_ge(grown, i - 1)
                    pe.wait_ge(shifted, i - 1)
                for c in range(NCH):
                    m = nc.tensor.matmul(ps[:, b0, c * P:(c + 1) * P], bc(g[:, c, h0 + i:h0 + i + 1], [P, P]), prog.tri,
                                         start=True, stop=True)
                m.then_inc(product, 1)
                for j, other in ((1, k), (2, q)):
                    for c in range(NCH):
                        cs = slice(c * P, (c + 1) * P)
                        m = nc.tensor.matmul(ps[:, b0 + j, cs], k[:, h0 + i, cs], other[:, h0 + i, cs],
                                             start=True, stop=True)
                    m.then_inc(product, 1)

        @st.vector
        def _(dve):
            for i in range(HG):
                b0 = 4 * (i % 2)
                dve.wait_ge(product, 3 * i + 1)
                for c in range(NCH):
                    m = nc.vector.tensor_scalar(dec[:, i, c * P:(c + 1) * P], ps[:, b0, c * P:(c + 1) * P],
                                                G[:, c, h0 + i:h0 + i + 1], 0.0, ALU.subtract, ALU.min)
                m.then_inc(shifted, 1)
                dve.wait_ge(masked, i + 1)
                dve.wait_ge(product, 3 * i + 3)
                for out, j in ((am, 1), (att, 2)):
                    nc.vector.tensor_tensor(out[:, i, :], ps[:, b0 + j, :], dec[:, i, :], ALU.mult
                                            ).then_inc(weighted, 1)

        @st.scalar
        def _(act):
            for i in range(HG):
                act.wait_ge(shifted, i + 1)
                nc.scalar.activation(dec[:, i, :], dec[:, i, :], ACT.Exp).then_inc(decayed, 1)
                if i >= 2:
                    act.wait_ge(scaled, i - 1)
                nc.scalar.activation(eg[:, i % 2, :], ps[:, 4 * (i % 2), :], ACT.Exp).then_inc(grown, 1)

        @st.gpsimd
        def _(pool):
            for i in range(HG):
                d = dec[:, i, :].rearrange("p (c n) -> p c n", n=P)
                pool.wait_ge(decayed, i + 1)
                nc.gpsimd.tensor_tensor(d, d, prog.tri.unsqueeze(1).to_broadcast([P, NCH, P]), ALU.mult
                                        ).then_inc(masked, 1)
                pool.wait_ge(grown, i + 1)
                pool.wait_ge(product, 3 * i + 3)
                nc.gpsimd.tensor_tensor(q[:, h0 + i, :], q[:, h0 + i, :], eg[:, i % 2, :], ALU.mult
                                        ).then_inc(scaled, 1)


def gdn_inverse(prog, name, h0, beta, am, inv, inv_t, prod):
    nc, ps = prog.nc, prog.ps
    N = LEVELS * HG

    def blocks(x):
        return x.rearrange("p (c n) -> p c n", n=P)
    part = prog.acc[:, 0:2, h0 * P:(h0 + HG) * P]
    with Stage(prog, name) as st:
        start, cut = st.counter("start"), st.counter("cut")
        u_ready, u_copied = st.counter("u_ready"), st.counter("u_copied")
        p_ready, updated = st.counter("p_ready"), st.counter("updated")

        @st.gpsimd
        def _(pool):
            for n in range(N):
                level, i = divmod(n, HG)
                if n >= 2:
                    pool.wait_ge(u_ready, n - 1)
                nc.gpsimd.tensor_tensor(blocks(part[:, n % 2, :]), blocks(am[:, i, :]),
                                        prog.level_masks[:, level, :].unsqueeze(1).to_broadcast([P, NCH, P]),
                                        ALU.mult).then_inc(cut, 1)

        @st.tensor
        def _(pe):
            def chunks():
                return [slice(c * P, (c + 1) * P) for c in range(NCH)]

            def u(n):
                i = n % HG
                pe.wait_ge(cut, n + 1)
                pe.wait_ge(start, HG)
                if n >= HG:
                    pe.wait_ge(updated, 2 * (n - HG + 1))
                for cs in chunks():
                    m = nc.tensor.matmul(ps[:, i, cs], part[:, n % 2, cs], inv[:, i, cs], start=True, stop=True)
                m.then_inc(u_ready, 1)

            def p(n):
                i, b = n % HG, 4 + 2 * (n % 2)
                pe.wait_ge(u_copied, n + 1)
                if n >= 2:
                    pe.wait_ge(updated, 2 * (n - 1))
                for cs in chunks():
                    m = nc.tensor.matmul(ps[:, b, cs], inv_t[:, i, cs], prod[:, i, cs], start=True, stop=True)
                m.then_inc(p_ready, 1)
                for cs in chunks():
                    m = nc.tensor.matmul(ps[:, b + 1, cs], prod[:, i, cs], inv_t[:, i, cs], start=True, stop=True)
                m.then_inc(p_ready, 1)

            for level in range(LEVELS):
                for i in range(HG):
                    u(level * HG + i)
                for i in range(HG):
                    p(level * HG + i)

        @st.vector
        def _(dve):
            for i in range(HG):
                for x in (inv, inv_t):
                    m = nc.vector.tensor_copy(blocks(x[:, i, :]), prog.ident.unsqueeze(1).to_broadcast([P, NCH, P]))
                m.then_inc(start, 1)
            for level in range(LEVELS):
                for i in range(HG):
                    n = level * HG + i
                    dve.wait_ge(u_ready, n + 1)
                    if n >= HG:
                        dve.wait_ge(u_copied, n - HG + 1)
                    scale = beta[:, :, h0 + i:h0 + i + 1].to_broadcast([P, NCH, P])
                    nc.vector.tensor_tensor(blocks(prod[:, i, :]), blocks(ps[:, i, :]), scale, ALU.mult
                                            ).then_inc(u_copied, 1)
                for i in range(HG):
                    n = level * HG + i
                    b = 4 + 2 * (n % 2)
                    dve.wait_ge(start, HG)
                    if n >= HG:
                        dve.wait_ge(updated, 2 * (n - HG + 1))
                    dve.wait_ge(p_ready, 2 * n + 2)
                    nc.vector.tensor_tensor(inv[:, i, :], inv[:, i, :], ps[:, b, :], ALU.subtract).then_inc(updated, 1)
                    nc.vector.tensor_tensor(inv_t[:, i, :], inv_t[:, i, :], ps[:, b + 1, :], ALU.subtract
                                            ).then_inc(updated, 1)


def gdn_uw(prog, name, h0, k_tok, v_tok, beta, beG, kd, inv_t, vb, kb, u, w_t):
    nc, ps = prog.nc, prog.ps
    hs = slice(h0 * P, (h0 + HG) * P)

    def heads(x):
        return x.rearrange("p (h n) -> p h n", n=P)
    with Stage(prog, name) as st:
        vb_ready, kb_ready = st.counter("vb_ready"), st.counter("kb_ready")
        u_ready, w_ready, u_copied, w_copied = (st.counter(x) for x in ("u_ready", "w_ready", "u_copied", "w_copied"))

        @st.vector
        def _(dve):
            for c in range(NCH):
                nc.vector.tensor_tensor(heads(vb[:, c, :]), heads(v_tok[:, c, hs]),
                                        beta[:, c, h0:h0 + HG].unsqueeze(2).to_broadcast([P, HG, P]),
                                        ALU.mult).then_inc(vb_ready, 1)
            for c in range(NCH):
                dve.wait_ge(u_ready, c + 1)
                nc.vector.tensor_copy(u[:, c, :], ps[:, c, :]).then_inc(u_copied, 1)

        @st.gpsimd
        def _(pool):
            for c in range(NCH):
                nc.gpsimd.tensor_tensor(heads(kb[:, c, :]), heads(k_tok[:, c, hs]),
                                        beG[:, c, h0:h0 + HG].unsqueeze(2).to_broadcast([P, HG, P]),
                                        ALU.mult).then_inc(kb_ready, 1)
            pool.wait_ge(kb_ready, NCH)
            for c in range(NCH):
                nc.gpsimd.tensor_tensor(heads(k_tok[:, c, hs]), heads(k_tok[:, c, hs]),
                                        kd[:, c, h0:h0 + HG].unsqueeze(2).to_broadcast([P, HG, P]), ALU.mult)

        @st.tensor
        def _(pe):
            for c in range(NCH):
                cs = slice(c * P, (c + 1) * P)
                pe.wait_ge(vb_ready, c + 1)
                for i in range(HG):
                    m = nc.tensor.matmul(ps[:, c, i * P:(i + 1) * P], inv_t[:, i, cs], vb[:, c, i * P:(i + 1) * P],
                                         start=True, stop=True)
                m.then_inc(u_ready, 1)
            pe.wait_ge(kb_ready, NCH)
            for i in range(HG):
                for c in range(NCH):
                    cs = slice(c * P, (c + 1) * P)
                    m = nc.tensor.matmul(ps[:, 4 + i, cs], kb[:, c, i * P:(i + 1) * P], inv_t[:, i, cs],
                                         start=True, stop=True)
                m.then_inc(w_ready, 1)

        @st.scalar
        def _(act):
            for i in range(HG):
                act.wait_ge(w_ready, i + 1)
                nc.scalar.activation(w_t[:, i, :], ps[:, 4 + i, :], ACT.Copy).then_inc(w_copied, 1)


def gdn_scan(prog, name, h0, q, att, k_tok, eL, u, w_t, state, out):
    nc, ps = prog.nc, prog.ps
    with Stage(prog, name) as st:
        ws, v_new, o_ready = st.counter("ws"), st.counter("v_new"), st.counter("o_ready")
        o_copied, kv, s_new = st.counter("o_copied"), st.counter("kv"), st.counter("s_new")

        @st.tensor
        def _(pe):
            for c in range(NCH):
                cs = slice(c * P, (c + 1) * P)
                if c:
                    pe.wait_ge(s_new, c)
                    pe.wait_ge(v_new, c)
                    for i in range(HG):
                        m = nc.tensor.matmul(ps[:, 0, i * P:(i + 1) * P], w_t[:, i, cs], state[:, i * P:(i + 1) * P],
                                             start=True, stop=True)
                    m.then_inc(ws, 1)
                if c >= 2:
                    pe.wait_ge(o_copied, c - 1)
                pe.wait_ge(v_new, c + 1)
                for i in range(HG):
                    hp = slice(i * P, (i + 1) * P)
                    if c:
                        nc.tensor.matmul(ps[:, 1 + c % 2, hp], q[:, h0 + i, cs], state[:, hp], start=True, stop=False)
                    m = nc.tensor.matmul(ps[:, 1 + c % 2, hp], att[:, i, cs], u[:, c, hp], start=(c == 0), stop=True)
                m.then_inc(o_ready, 1)
                if c < NCH - 1:
                    for i in range(HG):
                        hp = slice(i * P, (i + 1) * P)
                        m = nc.tensor.matmul(ps[:, 3, hp], k_tok[:, c, (h0 + i) * P:(h0 + i + 1) * P], u[:, c, hp],
                                             start=True, stop=True)
                    m.then_inc(kv, 1)

        @st.vector
        def _(dve):
            for c in range(NCH):
                if c == 0:
                    dve.sem_inc(v_new, 1)
                else:
                    dve.wait_ge(ws, c)
                    nc.vector.tensor_tensor(u[:, c, :], u[:, c, :], ps[:, 0, :], ALU.subtract).then_inc(v_new, 1)
                if c < NCH - 1:
                    dve.wait_ge(kv, c + 1)
                    if c == 0:
                        nc.vector.tensor_copy(state[:, :], ps[:, 3, :]).then_inc(s_new, 1)
                    else:
                        dve.wait_ge(s_new, c)
                        dve.wait_ge(o_ready, c + 1)
                        for i in range(HG):
                            hp = slice(i * P, (i + 1) * P)
                            m = nc.vector.scalar_tensor_tensor(out=state[:, hp], in0=state[:, hp],
                                                               scalar=eL[:, c, h0 + i:h0 + i + 1], in1=ps[:, 3, hp],
                                                               op0=ALU.mult, op1=ALU.add)
                        m.then_inc(s_new, 1)

        @st.scalar
        def _(act):
            for c in range(NCH):
                act.wait_ge(o_ready, c + 1)
                nc.scalar.activation(out[:, c, h0 * P:(h0 + HG) * P], ps[:, 1 + c % 2, :], ACT.Copy
                                     ).then_inc(o_copied, 1)


def gdn_output_gate(prog, name, o, z, norm_g):
    nc = prog.nc
    with ExitStack() as own:
        sq = prog.sbuf(name + "_sq", [P, NT, D], own)
        ms = prog.sbuf(name + "_ms", [P, NT, HEADS], own)
        with Stage(prog, name) as st:
            squared, summed, rooted = st.counter("squared"), st.counter("summed"), st.counter("rooted")
            dve_link, gained = st.counter("dve_link"), st.counter("gained")

            def heads(x):
                return x.rearrange("p (h n) -> p h n", n=P)

            @st.scalar
            def _(act):
                for t in range(NT):
                    nc.scalar.activation(sq[:, t, :], o[:, t, :], ACT.Square).then_inc(squared, 1)
                act.wait_ge(summed, NT)
                nc.scalar.activation(ms[:, :, :], ms[:, :, :], ACT.Sqrt, scale=1.0 / P, bias=prog.eps_norm).then_inc(rooted, 1)

            @st.gpsimd
            def _(pool):
                for t in range(NT):
                    nc.gpsimd.tensor_tensor(heads(z[:, t, :]), heads(z[:, t, :]),
                                            norm_g.unsqueeze(1).to_broadcast([P, HEADS, P]), ALU.mult).then_inc(gained, 1)

            @st.vector
            def _(dve):
                link = linker(dve, dve_link)
                for t in range(NT):
                    dve.wait_ge(squared, t + 1)
                    nc.vector.tensor_reduce(ms[:, t, :], heads(sq[:, t, :]), AX_X, ALU.add).then_inc(summed, 1)
                dve.wait_ge(rooted, 1)
                link(nc.vector.reciprocal(ms[:, :, :], ms[:, :, :]))
                for t in range(NT):
                    link(nc.vector.tensor_tensor(heads(o[:, t, :]), heads(o[:, t, :]),
                                                 ms[:, t, :].unsqueeze(2).to_broadcast([P, HEADS, P]), ALU.mult))
                    dve.wait_ge(gained, t + 1)
                    nc.vector.tensor_tensor(o[:, t, :], o[:, t, :], z[:, t, :], ALU.mult)


def gdn_layer(prog, inp):
    turn_x = [([prog.x_tok[:, t, k * P:(k + 1) * P] for t in range(NT)], prog.x_hi[:, k, :], prog.x_lo[:, k, :])
              for k in range(KD)]
    w_in = inp["gdn_w_in"][0]
    with ExitStack() as own:
        def new(name, shape, c=own):
            return prog.sbuf(name, shape, c)
        small = new("gdn_small", [P, 9, NCH * HEADS])
        tabs = [small[:, i, :].rearrange("p (c h) -> p c h", h=HEADS) for i in range(8)] + [small[:, 8, 0:HEADS]]
        g, beta, G, beG, kd, eL = tabs[:6]
        par = new("gdn_par", [P, 16 + P])
        masks = new("gdn_masks", [P, LEVELS * P])
        prog.level_masks = masks[:, :].rearrange("p (l n) -> p l n", n=P)
        with ExitStack() as mid:
            q, k = new("gdn_q", [P, HEADS, S], mid), new("gdn_k", [P, HEADS, S], mid)
            k_tok, v_tok = new("gdn_ktok", [P, NT, D], mid), new("gdn_vtok", [P, NT, D], mid)
            with ExitStack() as early:
                v = new("gdn_v", [P, HEADS, S], early)
                taps = new("gdn_taps", [P, 96], early)
                ba = new("gdn_ba", [P, NT, 2 * HEADS], early)
                pick_row = new("gdn_pick_row", [P, PICK_ROW], early)
                prog.pick_row = pick_row[:, :]
                turn_split(prog, "setup_turn", turn_x, [(taps[:, :], inp["gdn_taps"]), (par[:, :], inp["gdn_par"]),
                                                        (masks[:, :], inp["cst"][:, 3 * P:(3 + LEVELS) * P]),
                                                        (pick_row[:, :], inp["cst"][:, (3 + LEVELS) * P:])])
                gdn_conv(prog, "gdn_conv", [x[:, h, :] for x in (q, k, v) for h in range(HEADS)], taps,
                         prog.split_scratch)
                project(prog, "gdn_ba", [prog.x_hi, prog.x_lo],
                        [(0, 0, 2 * HEADS, t, None, ba[:, t, :], None) for t in range(NT)], prog.split_scratch)
                gdn_norms(prog, "gdn_norms", q, k)
                gdn_gates(prog, "gdn_gates", ba, par, tabs)
                transpose_stage(prog, "gdn_turn", [([x[:, h, t * P:(t + 1) * P] for h in range(hh, hh + 4)],
                                                    y[:, t, hh * P:(hh + 4) * P])
                                                   for x, y in ((k, k_tok), (v, v_tok)) for t in range(NT) for hh in (0, 4)])
            for h0 in range(0, HEADS, HG):
                with ExitStack() as grp:
                    dec, att, am, inv, inv_t = (new(f"gdn_{n}{h0}", [P, HG, S], grp) for n in ("dec", "att", "am", "inv", "invt"))
                    gdn_decays(prog, f"gdn_decays{h0}", h0, q, k, g, G, dec, att, am)
                    gdn_inverse(prog, f"gdn_inverse{h0}", h0, beta, am, inv, inv_t, dec)
                    kb = prog.acc[:, :, h0 * P:(h0 + HG) * P]
                    gdn_uw(prog, f"gdn_uw{h0}", h0, k_tok, v_tok, beta, beG, kd, inv_t, inv, kb, dec, am)
                    gdn_scan(prog, f"gdn_scan{h0}", h0, q, att, k_tok, eL, dec, am, inv[:, 0, :], prog.acc)
        z = new("gdn_z", [P, NT, D])
        with ExitStack() as split:
            project(prog, "gdn_z", [prog.x_hi, prog.x_lo],
                    [(c, 0, UP_COLS, t, None, z[:, t, c * UP_COLS:(c + 1) * UP_COLS], ACT.Silu)
                     for c in range(4) for t in range(NT)], hi_slots(prog, split, "gdn_z_hi"))
        gdn_output_gate(prog, "gdn_gate", prog.acc, z, par[:, 16:16 + P])
        turn_split(prog, "gdn_turn_o", [([prog.acc[:, t, kk * P:(kk + 1) * P] for t in range(NT)],
                                         prog.x_hi[:, kk, :], prog.x_lo[:, kk, :]) for kk in range(KD)])
        down_project(prog, "gdn_out", (prog.x_hi, prog.x_lo))



GROUPS, GC, GP = 64, 16, 64
PAIRS = GROUPS // 2
STEP = P // GC
NJ = S // STEP
TWO_PI = 2 * np.pi
MAGIC = 1.5 * 2.0 ** 23
TWO_PI_HI = 6.28125
TWO_PI_LO = TWO_PI - TWO_PI_HI
PI_IN = 3.1415925
GSTEP = 8


def reduce_angle(nc, link, x, tmp, shift=0.0):
    if shift:
        link(nc.vector.tensor_scalar(x, x, shift, None, ALU.add))
    link(nc.vector.tensor_scalar(tmp, x, 1.0 / TWO_PI, MAGIC, ALU.mult, ALU.add))
    link(nc.vector.tensor_scalar(tmp, tmp, MAGIC, None, ALU.subtract))
    link(nc.vector.scalar_tensor_tensor(out=x, in0=tmp, scalar=-TWO_PI_HI, in1=x, op0=ALU.mult, op1=ALU.add))
    link(nc.vector.scalar_tensor_tensor(out=x, in0=tmp, scalar=-TWO_PI_LO, in1=x, op0=ALU.mult, op1=ALU.add))
    link(nc.vector.tensor_scalar(x, x, PI_IN, -PI_IN, ALU.min, ALU.max))


def s5_tables(prog, name, lanes, taus, pow_re, pow_im, bbar, b, a8, u_feat, u_blk, into):
    nc = prog.nc
    NTAU = STEP + 1
    with ExitStack() as own:
        w = prog.sbuf(name + "_w", [P, 12, PAIRS], own)
        ang = prog.sbuf(name + "_ang", [P, 3, NTAU, PAIRS], own)
        tmp_b = prog.sbuf(name + "_tb", [P, 4, PAIRS, GC], own)
        with Stage(prog, name) as st:
            link_sem, acted = st.counter("dve_link"), st.counter("acted")
            to_act, bbar_ready, pool_link = st.counter("to_act"), st.counter("bbar_ready"), st.counter("pool_link")
            stored, landed = st.counter("stored"), st.counter("landed")
            lr, li, ldt = (lanes[:, i, :] for i in range(3))
            dt, xr, xi, t, em1, half, m1c, den, fr, fi, s0, s1 = (w[:, i, :] for i in range(12))
            mag, cos, tmp = (ang[:, i, :, :] for i in range(3))

            @st.scalar
            def _(act):
                nc.scalar.activation(dt, ldt, ACT.Exp).then_inc(acted, 1)
                act.wait_ge(to_act, 1)
                nc.scalar.activation(t, xr, ACT.Tanh, scale=0.5).then_inc(acted, 1)
                nc.scalar.activation(mag, mag, ACT.Exp).then_inc(acted, 1)
                act.wait_ge(to_act, 2)
                nc.scalar.activation(half, xi, ACT.Sin, scale=0.5).then_inc(acted, 1)
                nc.scalar.activation(pow_im, pow_im, ACT.Sin).then_inc(acted, 1)
                nc.scalar.activation(cos, cos, ACT.Sin).then_inc(acted, 1)

            @st.vector
            def _(dve):
                link = linker(dve, link_sem)
                tt, ts = nc.vector.tensor_tensor, nc.vector.tensor_scalar
                rep = [P, NTAU, PAIRS]
                dve.wait_ge(acted, 1)
                link(tt(xr, lr, dt, ALU.mult))
                link(tt(xi, li, dt, ALU.mult))
                tau = taus.unsqueeze(2).to_broadcast(rep)
                tt(mag, xr.unsqueeze(1).to_broadcast(rep), tau, ALU.mult).then_inc(to_act, 1)
                reduce_angle(nc, link, xi, s0)
                link(tt(pow_im, xi.unsqueeze(1).to_broadcast(rep), tau, ALU.mult))
                reduce_angle(nc, link, pow_im, tmp)
                link(nc.vector.tensor_copy(cos, pow_im))
                reduce_angle(nc, link, cos, tmp, np.pi / 2)
                nc.vector.memset(s1, 0.0).then_inc(to_act, 1)
                dve.wait_ge(acted, 6)
                link(tt(pow_re, mag, cos, ALU.mult))
                link(tt(pow_im, mag, pow_im, ALU.mult))
                link(ts(s0, t, -1.0, 1.0, ALU.mult, ALU.add))
                link(nc.vector.reciprocal(s0, s0))
                link(nc.vector.scalar_tensor_tensor(out=em1, in0=t, scalar=2.0, in1=s0, op0=ALU.mult, op1=ALU.mult))
                link(tt(m1c, em1, cos[:, 1, :], ALU.mult))
                link(tt(s0, half, half, ALU.mult))
                link(nc.vector.scalar_tensor_tensor(out=m1c, in0=s0, scalar=-2.0, in1=m1c, op0=ALU.mult, op1=ALU.add))
                link(tt(den, lr, lr, ALU.mult))
                link(tt(s0, li, li, ALU.mult))
                link(tt(den, den, s0, ALU.add))
                link(nc.vector.reciprocal(den, den))
                ai = pow_im[:, 1, :]
                link(tt(fr, m1c, lr, ALU.mult))
                link(tt(s0, ai, li, ALU.mult))
                link(tt(fr, fr, s0, ALU.add))
                link(tt(fr, fr, den, ALU.mult))
                link(tt(fi, ai, lr, ALU.mult))
                link(tt(s0, m1c, li, ALU.mult))
                link(tt(fi, fi, s0, ALU.subtract))
                link(tt(fi, fi, den, ALU.mult))
                rep = [P, PAIRS, GC]
                frb, fib = fr.unsqueeze(2).to_broadcast(rep), fi.unsqueeze(2).to_broadcast(rep)
                for i, (f, x) in enumerate(((frb, 0), (fib, 1), (frb, 1), (fib, 0))):
                    m = tt(tmp_b[:, i], b[:, x], f, ALU.mult)
                link(m)
                link(tt(bbar[:, 0], tmp_b[:, 0], tmp_b[:, 1], ALU.subtract))
                link(tt(bbar[:, 1], tmp_b[:, 2], tmp_b[:, 3], ALU.add))
                dve.sem_inc(bbar_ready, 1)
                for r in range(2):
                    nc.vector.tensor_copy(a8[:, 0, r, :], pow_re[:, STEP, :])
                ts(a8[:, 1, 0, :], pow_im[:, STEP, :], -1.0, None, ALU.mult)
                nc.vector.tensor_copy(a8[:, 1, 1, :], pow_im[:, STEP, :])
                real_powers(prog, dve, link, bbar, pow_re, pow_im, into[0], BACK)
                imaginary_powers(prog, nc.vector, 2, link, bbar, pow_re, pow_im, into[1], BACK[6:])

            @st.gpsimd
            def _(pool):
                pool.wait_ge(bbar_ready, 1)
                imaginary_powers(prog, nc.gpsimd, 1, linker(pool, pool_link), bbar, pow_re, pow_im, into[1], BACK[:6])

            @st.sync
            def _(sp):
                sp.dma_start(prog.u_dram.rearrange("f p n -> p f n"), u_feat[:, :].rearrange("p f i j -> p f (i j)")
                             ).then_inc(stored, 16)
                sp.wait_ge(stored, 16)
                src = prog.u_dram.rearrange("f (g c) (i j) -> i c (f g) j", c=GC, j=NJ)
                for i in range(STEP):
                    sp.dma_start(u_blk[i * GC:(i + 1) * GC, :, :], src[i]).then_inc(landed, 16)
                sp.wait_ge(landed, 16 * STEP)


BACK = [(t, STEP - 1 - t) for t in range(STEP)]


def real_powers(prog, dve, link, x, pow_re, pow_im, out, taus):
    nc = prog.nc
    tmp = prog.acc[:, 0, :].rearrange("p (b q c) -> p b q c", b=2, c=GC)
    for tau, at in taus:
        re, im = (p[:, tau, :].unsqueeze(2).to_broadcast([P, PAIRS, GC]) for p in (pow_re, pow_im))
        nc.vector.tensor_tensor(tmp[:, 0], x[:, 0], re, ALU.mult)
        link(nc.vector.tensor_tensor(tmp[:, 1], x[:, 1], im, ALU.mult))
        link(nc.vector.tensor_tensor(out[:, at], tmp[:, 0], tmp[:, 1], ALU.subtract))


def imaginary_powers(prog, eng, tmp_row, link, x, pow_re, pow_im, out, taus):
    tmp = prog.acc[:, tmp_row, :].rearrange("p (b q c) -> p b q c", b=2, c=GC)
    for tau, at in taus:
        re, im = (p[:, tau, :].unsqueeze(2).to_broadcast([P, PAIRS, GC]) for p in (pow_re, pow_im))
        eng.tensor_tensor(tmp[:, 0], x[:, 0], im, ALU.mult)
        link(eng.tensor_tensor(tmp[:, 1], x[:, 1], re, ALU.mult))
        link(eng.tensor_tensor(out[:, at], tmp[:, 0], tmp[:, 1], ALU.add))


def s5_layer(prog, inp):
    nc, ps, W = prog.nc, prog.ps, prog.weights
    with ExitStack() as own:
        def new(name, shape, c=own):
            return prog.sbuf(name, shape, c)
        u_feat = new("s5_ufeat", [P, KD, STEP, NJ])
        par = new("s5_par", [P, KD + 3 * PAIRS + STEP + 1])
        d_skip = par[:, 0:KD]
        lanes = par[:, KD:KD + 3 * PAIRS].rearrange("p (a q) -> p a q", q=PAIRS)
        taus = par[:, KD + 3 * PAIRS:]
        with ExitStack() as core:
            bc_in = new("s5_bc", [P, 4, PAIRS, GC], core)
            bbar = new("s5_bbar", [P, 2, PAIRS, GC], core)
            pw = new("s5_pow", [P, 2, STEP + 1, PAIRS], core)
            a8 = new("s5_a8", [P, 2, 2, PAIRS], core)
            u_blk = prog.x_free.rearrange("p k n -> p (k n)").rearrange("p (g j) -> p g j", j=NJ)
            he = new("s5_he", [P, 2, NJ * 2 * PAIRS], core)
            h_all = he[:, 0, :].rearrange("p (j r q) -> p j r q", r=2, q=PAIRS)
            e_all = he[:, 1, :].rearrange("p (j r q) -> p j r q", r=2, q=PAIRS)
            layer_norm(prog, "ffn_ln", inp["ln_gb"][1],
                       meanwhile=[(prog.ada_par, inp["ada_par"]), (par[:, :], inp["s5_par"]), (bc_in[:, :, :, :], inp["s5_bc"])])
            project(prog, "s5_u", [prog.x_hi, prog.x_lo],
                    [(f // 2, (f % 2) * P, P, None, slice(0, P), u_feat[:, f].rearrange("p i j -> p j i"), None)
                     for f in range(KD)], prog.split_scratch)

            with ExitStack() as phase:
                into = new("s5_into", [P, 2, PAIRS, P], phase)
                p_t = he[:, :, :].rearrange("p r (q i c) -> p r q i c", q=PAIRS, c=GC)
                s5_tables(prog, "s5_tables", lanes, taus, pw[:, 0], pw[:, 1], bbar, bc_in[:, 0:2], a8, u_feat, u_blk,
                          [p_t[:, r].rearrange("p q i c -> p i q c") for r in range(2)])
                transpose_stage(prog, "s5_in_turn", [([p_t[:, r, q].rearrange("p i c -> p (i c)") for q in range(q0, q0 + 4)],
                                                      into[:, r, q0:q0 + 4, :])
                                                     for r in range(2) for q0 in range(0, PAIRS, 4)])
                with Stage(prog, "s5_inputs") as st:
                    product, act_c = st.counter("product"), st.counter("act_copied")

                    @st.tensor
                    def _(pe):
                        for r in range(2):
                            for b in range(4):
                                for q in range(8 * b, 8 * b + 8):
                                    for gp in range(2):
                                        m = nc.tensor.matmul(ps[gp * GP:(gp + 1) * GP, 4 * r + b, (q % 8) * NJ:(q % 8 + 1) * NJ],
                                                             into[:, r, q, gp * GP:(gp + 1) * GP], u_blk[:, PAIRS * gp + q, :],
                                                             start=True, stop=True)
                                m.then_inc(product, 1)

                    @st.scalar
                    def _(act):
                        for n in range(0, 8, 2):
                            act.wait_ge(product, n + 1)
                            nc.scalar.activation(e_all[:, :, n // 4, 8 * (n % 4):8 * (n % 4) + 8].rearrange("p j q -> p q j"),
                                                 ps[:, n, :].rearrange("p (q j) -> p q j", j=NJ), ACT.Copy)

                    @st.vector
                    def _(dve):
                        for n in range(1, 8, 2):
                            dve.wait_ge(product, n + 1)
                            nc.vector.tensor_copy(e_all[:, :, n // 4, 8 * (n % 4):8 * (n % 4) + 8].rearrange("p j q -> p q j"),
                                                  ps[:, n, :].rearrange("p (q j) -> p q j", j=NJ))
            with ExitStack() as phase:
                q_re, q_im = (new(f"s5_q{r}", [P, PAIRS, STEP + 1, GC], phase) for r in range(2))
                t12 = new("s5_t12", [P, 2, 2, PAIRS], phase)
                s5_scan(prog, h_all, e_all, a8, t12, bc_in[:, 2:4], pw, q_re, q_im)
                s5_outputs(prog, "s5_outputs", bbar, q_re, q_im, u_blk, h_all, he[:, 1, :])
        s5_glu(prog, inp, u_feat, d_skip)


def s5_scan(prog, h_all, e_all, a8, t12, c, pw, q_re, q_im):
    nc, W, ps = prog.nc, prog.weights, prog.ps
    mods, silu_c, junk = prog.mods, prog.ada_par[:, 0, 0:KD], prog.ada_junk
    name, N_ADA = "s5_scan", 3 * D // UP_COLS
    with Stage(prog, name) as st:
        link_sem, pool_link, negated = st.counter("dve_link"), st.counter("pool_link"), st.counter("negated")
        activated, rowed, extracted = st.counter("activated"), st.counter("rowed"), st.counter("extracted")
        taus = [(t, t) for t in range(STEP + 1)]

        def bank(l, b):
            return (6 * l + b) % 8

        @st.vector
        def _(dve):
            link = linker(dve, link_sem)

            def extract(l):
                dve.wait_ge(rowed, l + 1)
                for n in range(3 * KD):
                    link(nc.vector.tensor_tensor_reduce(out=junk, in0=ps[:, bank(l, n // 4), (n % 4) * P:(n % 4 + 1) * P],
                                                        in1=prog.ident, scale=1.0, scalar=0.0, op0=ALU.mult, op1=ALU.add,
                                                        accum_out=mods[:, l, n:n + 1]))
                dve.sem_inc(extracted, 1)
                link(nc.vector.tensor_tensor(mods[:, l, :], mods[:, l, :], prog.ada_par[:, l, KD:], ALU.add))
                link(nc.vector.tensor_scalar(mods[:, l, KD:2 * KD], mods[:, l, KD:2 * KD], 1.0, None, ALU.add))
            nc.vector.tensor_scalar(c[:, 1], c[:, 1], -1.0, None, ALU.mult).then_inc(negated, 1)
            nc.vector.tensor_scalar(pw[:, 1], pw[:, 1], -1.0, None, ALU.mult).then_inc(negated, 1)
            link(nc.vector.memset(h_all[:, 0], 0.0))
            for j in range(NJ - 1):
                h = h_all[:, j]
                nc.vector.tensor_tensor(t12[:, 0], h, a8[:, 0], ALU.mult)
                nc.vector.tensor_tensor(t12[:, 1, 0], h[:, 1], a8[:, 1, 0], ALU.mult)
                link(nc.vector.tensor_tensor(t12[:, 1, 1], h[:, 0], a8[:, 1, 1], ALU.mult))
                link(nc.vector.tensor_tensor(t12[:, 0], t12[:, 0], e_all[:, j], ALU.add))
                link(nc.vector.tensor_tensor(h_all[:, j + 1], t12[:, 0], t12[:, 1], ALU.add))
                if j == 3 * NJ // 4:
                    extract(0)
            dve.wait_ge(negated, 2)
            real_powers(prog, dve, link, c, pw[:, 0], pw[:, 1], q_re[:, :, :, :].rearrange("p q i c -> p i q c"), taus)
            extract(1)

        @st.gpsimd
        def _(pool):
            pool.wait_ge(negated, 2)
            imaginary_powers(prog, nc.gpsimd, 1, linker(pool, pool_link), c, pw[:, 0], pw[:, 1],
                             q_im[:, :, :, :].rearrange("p q i c -> p i q c"), taus)

        @st.scalar
        def _(act):
            nc.scalar.activation(silu_c, silu_c, ACT.Silu).then_inc(activated, 1)

        @st.tensor
        def _(pe):
            pe.wait_ge(activated, 1)
            for l in range(DEPTH):
                for j in range(N_ADA):
                    w = W.take(pe, name, l * N_ADA + j)
                    if l and j == 4:
                        pe.wait_ge(extracted, 1)
                    for k in range(KD):
                        m = nc.tensor.matmul(ps[:, bank(l, j // 2), (j % 2) * UP_COLS:(j % 2 + 1) * UP_COLS],
                                             bc(silu_c[:, k:k + 1], [P, P]), w[:, k, :], start=(k == 0), stop=(k == KD - 1))
                        if k == 0 and l + j:
                            W.leave(m, name, l * N_ADA + j - 1)
                m.then_inc(rowed, 1)


def s5_outputs(prog, name, bbar, q_re, q_im, u_blk, h_all, spare):
    nc, ps = prog.nc, prog.ps
    lag = spare[:, 0:2 * GSTEP * P].rearrange("p (b g n) -> p b g n", b=2, n=P)
    mix = spare[:, 2 * GSTEP * P:].rearrange("p (b g n) -> p b g n", b=2, n=P)
    y = prog.scratch.rearrange("p (i q c) -> p q i c", i=STEP, c=GC)
    NS = GROUPS // GSTEP

    def flat(x):
        return x.rearrange("p i c -> p (i c)")

    def of_parity(x, gp):
        return x.rearrange("p (g b) n -> p b g n", b=2)[:, gp]
    with Stage(prog, name) as st:
        zeroed, lag_ready, lag_copied = st.counter("zeroed"), st.counter("lag_ready"), st.counter("lag_copied")
        placed = [st.counter(f"placed_{b}") for b in range(2)]
        y_ready, y_copied = st.counter("y_ready"), st.counter("y_copied")

        @st.vector
        def _(dve):
            nc.vector.memset(mix, 0.0).then_inc(zeroed, 1)
            for s in range(NS):
                dve.wait_ge(lag_ready, s + 1)
                if s >= 2:
                    dve.wait_ge(placed[s % 2], 16 * STEP * (s // 2))
                for gp in range(2):
                    m = nc.vector.tensor_copy(of_parity(lag[0:GC, s % 2], gp),
                                              ps[0:GC, 2 * (s % 2) + gp, :].rearrange("p (g n) -> p g n", n=P))
                m.then_inc(lag_copied, 1)

        @st.sync
        def _(sp):
            sp.wait_ge(zeroed, 1)
            for s in range(NS):
                sp.wait_ge(lag_copied, s + 1)
                if s >= 2:
                    sp.wait_ge(y_ready, s - 1)
                for i in range(STEP):
                    n = (STEP - i) * GC
                    sp.dma_start(mix[i * GC:(i + 1) * GC, s % 2, :, i * GC:], lag[0:GC, s % 2, :, 0:n]
                                 ).then_inc(placed[s % 2], 16)

        @st.tensor
        def _(pe):
            def lags(s):
                if s >= 2:
                    pe.wait_ge(lag_copied, s - 1)
                for g in range(GSTEP):
                    q, gp = divmod(s * GSTEP + g, 2)
                    rows = slice(gp * GP, (gp + 1) * GP)
                    out = ps[0:GC, 2 * (s % 2) + gp, (g // 2) * P:(g // 2 + 1) * P]
                    nc.tensor.matmul(out, bbar[rows, 0, q, :], flat(q_re[rows, q, 0:STEP, :]), start=True, stop=False)
                    m = nc.tensor.matmul(out, bbar[rows, 1, q, :], flat(q_im[rows, q, 0:STEP, :]), start=False, stop=True)
                m.then_inc(lag_ready, 1)

            def outs(s):
                pe.wait_ge(placed[s % 2], 16 * STEP * (s // 2 + 1))
                if s >= 2:
                    pe.wait_ge(y_copied, s - 1)
                for g in range(GSTEP):
                    q, gp = divmod(s * GSTEP + g, 2)
                    rows = slice(gp * GP, (gp + 1) * GP)
                    out = ps[rows, 4 + 2 * (s % 2) + gp, (g // 2) * P:(g // 2 + 1) * P]
                    nc.tensor.matmul(out, u_blk[:, PAIRS * gp + q, :], mix[:, s % 2, g, :], start=True, stop=False)
                    nc.tensor.matmul(out, h_all[rows, :, 0, q], flat(q_re[rows, q, 1:STEP + 1, :]), start=False, stop=False)
                    m = nc.tensor.matmul(out, h_all[rows, :, 1, q], flat(q_im[rows, q, 1:STEP + 1, :]), start=False, stop=True)
                m.then_inc(y_ready, 1)
            lags(0)
            for s in range(NS):
                if s + 1 < NS:
                    lags(s + 1)
                outs(s)

        @st.scalar
        def _(act):
            for s in range(NS):
                act.wait_ge(y_ready, s + 1)
                for gp in range(2):
                    rows = slice(gp * GP, (gp + 1) * GP)
                    m = nc.scalar.activation(y[rows, s * GSTEP // 2:(s + 1) * GSTEP // 2],
                                             ps[rows, 4 + 2 * (s % 2) + gp, :].rearrange("p (q i c) -> p q i c", i=STEP, c=GC),
                                             ACT.Copy)
                m.then_inc(y_copied, 1)


def s5_glu(prog, inp, u_feat, d_skip):
    nc, ps, W = prog.nc, prog.ps, prog.weights
    with ExitStack() as own:
        y_feat = prog.sbuf("s5_yfeat", [P, KD, STEP, NJ], own)
        hid = prog.sbuf("s5_hid", [P, KD, S], own)
        y = prog.scratch.rearrange("p (i n) -> p i n", i=STEP)
        with Stage(prog, "s5_gelu") as st:
            turned, skipped = st.counter("turned"), st.counter("skipped")
            activated, hi_done = st.counter("activated"), st.counter("hi_done")
            jobs = [(qb, ih) for qb in range(KD // 2) for ih in range(2)]
            features = [gp * KD // 2 + qb for qb in range(KD // 2) for gp in range(2)]

            @st.tensor
            def _(pe):
                for n, (qb, ih) in enumerate(jobs):
                    for i in range(4):
                        m = nc.tensor.transpose(ps[:, n, i * P:(i + 1) * P], y[:, 4 * ih + i, qb * P:(qb + 1) * P], prog.ident)
                    m.then_inc(turned, 1)

            @st.vector
            def _(dve):
                def split_lo(n):
                    f = features[n]
                    dve.wait_ge(hi_done, n + 1)
                    nc.vector.tensor_tensor(prog.x_lo[:, f, :], hid[:, f, :], prog.x_hi[:, f, :].bitcast(F32), ALU.subtract)
                for n, (qb, ih) in enumerate(jobs):
                    dve.wait_ge(turned, n + 1)
                    bank = ps[:, n, :].rearrange("p (i g j) -> p g i j", g=2, j=NJ)
                    for gp in range(2):
                        f, steps = gp * KD // 2 + qb, slice(4 * ih, 4 * ih + 4)
                        nc.vector.scalar_tensor_tensor(out=y_feat[:, f, steps, :], in0=u_feat[:, f, steps, :],
                                                       scalar=d_skip[:, f:f + 1], in1=bank[:, gp],
                                                       op0=ALU.mult, op1=ALU.add).then_inc(skipped, 1)
                    if qb and ih:
                        split_lo(2 * qb - 2)
                        split_lo(2 * qb - 1)
                split_lo(KD - 2)
                split_lo(KD - 1)

            @st.scalar
            def _(act):
                for n, f in enumerate(features):
                    act.wait_ge(skipped, 4 * (n // 2 + 1))
                    nc.scalar.activation(hid[:, f, :].rearrange("p (j i) -> p i j", i=STEP), y_feat[:, f], ACT.Gelu
                                         ).then_inc(activated, 1)
                    act.wait_ge(activated, n + 1)
                    nc.scalar.activation(prog.x_hi[:, f, :], hid[:, f, :], ACT.Copy).then_inc(hi_done, 1)

        sig = prog.sbuf("s5_sig", [P, 2, UP_COLS], own)
        hi = hi_slots(prog, own, "s5_glu_hi")
        with Stage(prog, "s5_glu") as st:
            product, gated = st.counter("product"), st.counter("gated")
            multiplied, summed = st.counter("multiplied"), st.counter("summed")
            tiles = SplitTiles(prog, st, "s5_glu", hi)
            NG = D // UP_COLS

            def half(c, r, t):
                return ps[:, 4 * (c % 2) + 2 * r + t // 2, (t % 2) * UP_COLS:(t % 2 + 1) * UP_COLS]

            @st.tensor
            def _(pe):
                for j in range(2 * NG):
                    c, r = divmod(j, 2)
                    w = tiles.take(pe, j)
                    if c >= 2 and r == 0:
                        pe.wait_ge(multiplied, NT * (c - 1))
                    for t in range(NT):
                        for k in range(KD):
                            tiles.quarter(pe, j, k // 2)
                            m = three_pass(nc, half(c, r, t), [x[:, k, t * P:(t + 1) * P] for x in (prog.x_hi, prog.x_lo)],
                                           [x[:, k, :] for x in w], k == 0, k == KD - 1,
                                           (lambda m: W.leave(m, "s5_glu", j - 1)) if j and k == 0 and t == 0 else None)
                        m.then_inc(product, 1)

            @st.scalar
            def _(act):
                tiles.split_hi(act, 0)
                tiles.split_hi(act, 1)
                for c in range(NG):
                    tiles.split_hi(act, 2 * c + 2)
                    for t in range(NT):
                        n = c * NT + t
                        act.wait_ge(product, (2 * c + 1) * NT + 2 * (t // 2) + 2)
                        if n >= 2:
                            act.wait_ge(summed, n - 1)
                        nc.scalar.activation(sig[:, n % 2, :], half(c, 1, t), ACT.Sigmoid).then_inc(gated, 1)
                    tiles.split_hi(act, 2 * c + 3)

            @st.vector
            def _(dve):
                tiles.split_lo(dve, 0)
                tiles.split_lo(dve, 1)
                for c in range(NG):
                    tiles.split_lo(dve, 2 * c + 2)
                    for t in range(NT):
                        n = c * NT + t
                        cs = slice(c * UP_COLS, (c + 1) * UP_COLS)
                        dve.wait_ge(gated, n + 1)
                        nc.vector.tensor_tensor(sig[:, n % 2, :], sig[:, n % 2, :], half(c, 0, t), ALU.mult
                                                ).then_inc(multiplied, 1)
                        dve.wait_ge(multiplied, n + 1)
                        nc.vector.scalar_tensor_tensor(out=prog.acc[:, t, cs], in0=prog.x_tok[:, t, cs], scalar=ALPHA,
                                                       in1=sig[:, n % 2, :], op0=ALU.mult, op1=ALU.add).then_inc(summed, 1)
                    tiles.split_lo(dve, 2 * c + 3)



I32 = mybir.dt.int32
CHUNKS = [(c, min(c + UP_COLS, FF_PART)) for c in range(0, FF_PART, UP_COLS)]
N_UP = 2 * len(CHUNKS)
N_DOWN = (FT + 1) // 2
N_TILES = N_UP + N_DOWN
RAW = 3
SPLITS = 2
SLOTS = 192
SLOT_PAD = 256
assert N_TILES % RAW == 0 and N_TILES % SPLITS == 0


def tile_rows(j):
    if j < N_UP:
        return KD, CHUNKS[j // 2][1] - CHUNKS[j // 2][0]
    return min(2, FT - 2 * (j - N_UP)), D


def tiles_of_chunk(c):
    return range(2 * c, min(2 * c + 2, FT))


class PartStream:

    def __init__(self, prog, st, parts, w1, w3, w2, hi, lo):
        self.prog, self.parts, self.w = prog, parts, (w1, w3, w2)
        self.hi, self.lo = hi, lo
        self.landed = [st.counter(f"landed_{i}") for i in range(RAW)]
        self.hi_done, self.lo_done = st.counter("hi_done"), st.counter("lo_done")
        self.slot_free = st.counter("slot_free")
        self.tile_used = st.counter("tile_used")

    def view(self, buf, slot, j):
        k, n = tile_rows(j)
        return buf[:, slot, 0:k * n].rearrange("p (k n) -> p k n", n=n)

    def flat(self, buf, slot, j):
        k, n = tile_rows(j)
        return buf[:, slot, 0:k * n]

    def raw(self, j):
        return self.flat(self.prog.weights.ring, j % RAW, j)

    def load(self, sp, e, j):
        w1, w3, w2 = self.w
        if j < N_UP:
            c0, c1 = CHUNKS[j // 2]
            src = (w1, w3)[j % 2][bass.ds(e, 1), :, c0:c1]
        else:
            r = 2 * (j - N_UP)
            src = w2[bass.ds(e, 1), r * P:min(r + 2, FT) * P, :]
        sp.dma_start(self.view(self.prog.weights.ring, j % RAW, j), src.rearrange("a (k p) n -> p (a k) n", p=P)
                     ).then_inc(self.landed[j % RAW], 16)

    def loads(self, sp):
        for j in range(RAW):
            self.load(sp, 0, j)

        def part(here, after, values, count):
            for j in range(count):
                sp.wait_ge(self.lo_done, values[j])
                sp.sem_inc(self.slot_free, 1)
                ahead = j + RAW
                self.load(sp, *((here, ahead) if ahead < N_TILES else (after, ahead - N_TILES)))
        with sp.Fori(0, self.parts - 1) as e:
            values = [sp.snap(e * N_TILES + (j + 1)) for j in range(N_TILES)]
            part(e, sp.snap(e + 1), values, N_TILES)
        part(self.parts - 1, None, [(self.parts - 1) * N_TILES + j + 1 for j in range(N_TILES)], N_TILES - RAW)

    def split_hi(self, act, e, j):
        act.wait_ge(self.landed[j % RAW], e * (16 * N_TILES // RAW) + 16 * (j // RAW + 1))
        act.wait_ge(self.tile_used, e * N_TILES + (j + 1))
        self.prog.nc.scalar.activation(self.flat(self.hi, j % SPLITS, j), self.raw(j),
                                       ACT.Copy).then_inc(self.hi_done, 1)

    def split_lo(self, dve, e, j):
        dve.wait_ge(self.hi_done, e * N_TILES + (j + 1))
        self.prog.nc.vector.tensor_tensor(self.flat(self.lo, j % SPLITS, j), self.raw(j),
                                          self.flat(self.hi, j % SPLITS, j).bitcast(F32), ALU.subtract
                                          ).then_inc(self.lo_done, 1)

    def leave(self, m):
        m.then_inc(self.tile_used, 1)

    def take(self, pe, e, j):
        pe.wait_ge(self.lo_done, e * N_TILES + (j + 1))
        return self.view(self.hi, j % SPLITS, j), self.view(self.lo, j % SPLITS, j)


def dense_parts(prog, st, buf, parts, w1, w3, w2, gates):
    nc, ps = prog.nc, prog.ps
    x_hi, x_lo = prog.x_hi, prog.x_lo
    hid_hi, hid_lo, sig, prod, hi, lo = buf
    S_ = PartStream(prog, st, parts, w1, w3, w2, hi, lo)
    acc_ready = st.counter("acc_ready")
    up_ready, silu_done = st.counter("up_ready"), st.counter("silu_done")
    mult_done = st.counter("mult_done")
    hid_ready = st.counter("hid_ready")
    hi_ready = st.counter("hid_hi_ready")
    down_ready, added = st.counter("down_ready"), st.counter("added")

    def bank(m, which):
        return 4 * ((m // 2) % 2) + 2 * which + m % 2

    def tensor(pe):
        with pe.Fori(0, parts) as e:
            for j in range(N_UP):
                c, which = divmod(j, 2)
                wh, wl = S_.take(pe, e, j)
                if which == 0:
                    if c < 2:
                        pe.wait_ge(added, e * 8 + (4, 8)[c])
                    else:
                        pe.wait_ge(mult_done, e * FT + (2 * c + 2))
                for m in tiles_of_chunk(c):
                    cs = slice((m % 2) * P, (m % 2 + 1) * P)
                    for k in range(KD):
                        mm = three_pass(nc, ps[:, bank(m, which), :], (wh[:, k, cs], wl[:, k, cs]),
                                        (x_hi[:, k, :], x_lo[:, k, :]), k == 0, k == KD - 1,
                                        S_.leave if j and k == 0 and m % 2 == 0 else None)
                    mm.then_inc(up_ready, 1)
            pe.wait_ge(mult_done, e * FT + (FT + 4))
            for j in range(N_UP, N_TILES):
                wh, wl = S_.take(pe, e, j)
                for r in range(tile_rows(j)[0]):
                    m = 2 * (j - N_UP) + r
                    pe.wait_ge(hid_ready, e * FT + (m + 3))
                    for i in range(2 * NT):
                        t, cs = slice((i // 2) * P, (i // 2 + 1) * P), slice((i % 2) * BANK, (i % 2 + 1) * BANK)
                        mm = three_pass(nc, ps[:, i, :], (hid_hi[:, m, t], hid_lo[:, m, t]), (wh[:, r, cs], wl[:, r, cs]),
                                        m == 0, m == FT - 1, S_.leave if r == 0 and i == 0 else None)
                        if m == FT - 1 and i < 2 * NT - 1:
                            mm.then_inc(down_ready, 1)
            mm.then_inc(down_ready, 1)
            pe.wait_ge(added, e * 8 + 9)
            nc.tensor.matmul(ps[:, 0, 0:2], x_hi[:, 0, 0:P], x_hi[:, 0, 0:2], start=True, stop=True).then_inc(S_.tile_used, 1)

    def scalar(act):
        with act.Fori(0, parts) as e:
            S_.split_hi(act, e, 0)
            S_.split_hi(act, e, 1)
            for c in range(len(CHUNKS)):
                S_.split_hi(act, e, 2 * c + 2)
                for m in tiles_of_chunk(c):
                    act.wait_ge(up_ready, up_count(e, m, 0))
                    act.wait_ge(mult_done, e * FT + (4 if m == 0 else m + 3))
                    nc.scalar.activation(sig[:, m % 2, :], ps[:, bank(m, 0), :], ACT.Silu).then_inc(silu_done, 1)
                S_.split_hi(act, e, 2 * c + 3)
            for j in range(N_UP + 2, N_TILES):
                S_.split_hi(act, e, j)

    def up_count(e, m, which):
        n = len(tiles_of_chunk(m // 2))
        return e * (2 * FT) + (4 * (m // 2) + which * n + m % 2 + 1)

    def vector(dve):
        dve.sem_inc(S_.tile_used, SPLITS)
        dve.sem_inc(mult_done, 4)
        dve.sem_inc(hid_ready, 2)
        dve.sem_inc(added, 8)
        with dve.Fori(0, parts) as e:
            S_.split_lo(dve, e, 0)
            S_.split_lo(dve, e, 1)
            for c in range(len(CHUNKS)):
                S_.split_lo(dve, e, 2 * c + 2)
                for m in tiles_of_chunk(c):
                    dve.wait_ge(up_ready, up_count(e, m, 1))
                    dve.wait_ge(silu_done, e * FT + (m + 1))
                    dve.wait_ge(hid_ready, e * FT + (2 if m == 0 else m + 1))
                    nc.vector.tensor_tensor(prod[:, m % 2, :], sig[:, m % 2, :], ps[:, bank(m, 1), :], ALU.mult
                                            ).then_inc(mult_done, 1)
                S_.split_lo(dve, e, 2 * c + 3)
            for j in range(N_UP + 2, N_TILES):
                S_.split_lo(dve, e, j)
            dve.wait_ge(acc_ready, 1)
            dve.wait_ge(added, e * 8 + 8)
            for i in range(2 * NT):
                t, cs = i // 2, slice((i % 2) * BANK, (i % 2 + 1) * BANK)
                dve.wait_ge(down_ready, e * 8 + (i + 1))
                if gates is None:
                    ins = nc.vector.tensor_tensor(prog.acc[:, t, cs], ps[:, i, :], prog.acc[:, t, cs], ALU.add)
                else:
                    ins = nc.vector.scalar_tensor_tensor(out=prog.acc[:, t, cs], in0=ps[:, i, :],
                                                         scalar=gates[:, t, bass.ds(e, 1)], in1=prog.acc[:, t, cs],
                                                         op0=ALU.mult, op1=ALU.add)
                ins.then_inc(added, 1)

    def gpsimd(pool):
        for t in range(NT):
            ins = nc.gpsimd.tensor_scalar(prog.acc[:, t, :], prog.x_tok[:, t, :], ALPHA, None, ALU.mult)
        ins.then_inc(acc_ready, 1)
        with pool.Fori(0, parts) as e:
            for m in range(FT):
                pool.wait_ge(mult_done, e * FT + (m + 5))
                nc.gpsimd.tensor_tensor(hid_hi[:, m, :], prod[:, m % 2, :],
                                        prog.ones[:, 0:1].to_broadcast([P, S]), ALU.mult).then_inc(hi_ready, 1)
                pool.wait_ge(hi_ready, e * FT + (m + 1))
                nc.gpsimd.tensor_tensor(hid_lo[:, m, :], prod[:, m % 2, :], hid_hi[:, m, :].bitcast(F32), ALU.subtract
                                        ).then_inc(hid_ready, 1)
    return S_.loads, tensor, scalar, vector, gpsimd


def sparse_parts(prog, st, buf, w1, w3, w2, gates, place, iota, iota_landed):
    nc, ps = prog.nc, prog.ps
    xy_hi, xy_lo, hid_hi, hid_lo, sig, prod, hi, lo, pick, put, ident_r = buf
    xt_hi, xt_lo = (x.rearrange("p k n -> p (k n)").rearrange("p (t n) -> p t n", n=D) for x in (prog.x_hi, prog.x_lo))
    S_ = PartStream(prog, st, EXPERTS, w1, w3, w2, hi, lo)
    names = ("prepared", "pick_ready", "gathered", "g_hi", "g_lo", "put_ready", "put_act", "put_dve", "up_ready",
             "silu_done", "mult_done", "hi_ready", "hid_ready", "down_ready", "y_hi", "y_lo", "back_ready", "back_done")
    (prepared, pick_ready, gathered, g_hi, g_lo, put_ready, put_act, put_dve, up_ready, silu_done, mult_done,
     hi_ready, hid_ready, down_ready, y_hi, y_lo, back_ready, back_done) = (st.counter(n) for n in names)
    acc_ready = st.counter("acc_ready")
    NC = len(CHUNKS)
    xg = [b[:, 0:KD * SLOTS].rearrange("p (k n) -> p k n", n=SLOTS) for b in (xy_hi, xy_lo)]
    y = [b[:, :].rearrange("p (s n) -> p s n", n=D) for b in (xy_hi, xy_lo)]

    def pair(c):
        return len(tiles_of_chunk(c)) * SLOTS

    def gather_view(r, part):
        return ps[:, 2 * part:2 * part + 2, 0:2 * SLOTS].rearrange("p b (k n) -> p b k n", n=SLOTS)

    def gather_dst(r, part):
        return xg[part][:, 4 * r:4 * r + 4, :].rearrange("p (b k) n -> p b k n", b=2)

    def tensor(pe):
        pe.wait_ge(prepared, 2)
        with pe.Fori(0, EXPERTS) as e:
            pe.wait_ge(pick_ready, e + 1)
            for r in range(2):
                if r == 0:
                    pe.wait_ge(mult_done, e * NC + 2)
                else:
                    pe.wait_ge(g_hi, e * 2 + 1)
                    pe.wait_ge(g_lo, e * 2 + 1)
                for part, x in enumerate((xt_hi, xt_lo)):
                    for k in range(4 * r, 4 * r + 4):
                        out = ps[:, 2 * part + (k % 4) // 2, (k % 2) * SLOTS:(k % 2 + 1) * SLOTS]
                        for t in range(NT):
                            mm = nc.tensor.matmul(out, x[:, t, k * P:(k + 1) * P], pick[:, t, 0:SLOTS],
                                                  start=(t == 0), stop=(t == NT - 1))
                mm.then_inc(gathered, 1)
            pe.wait_ge(back_done, e * 8 + 4)
            for s in range(2):
                for t in range(NT):
                    mm = nc.tensor.matmul(ps[:, 4 + s, t * P:(t + 1) * P], pick[:, t, s * P:(s + 1) * P], ident_r,
                                          start=True, stop=True)
            mm.then_inc(put_ready, 1)
            pe.wait_ge(g_hi, e * 2 + 2)
            pe.wait_ge(g_lo, e * 2 + 2)
            for j in range(N_UP):
                c, which = divmod(j, 2)
                wh, wl = S_.take(pe, e, j)
                if which == 0 and c >= 2:
                    pe.wait_ge(mult_done, e * NC + (c + 1))
                for m in tiles_of_chunk(c):
                    cs = slice((m % 2) * P, (m % 2 + 1) * P)
                    out = ps[:, 2 * (c % 2) + which, (m % 2) * SLOTS:(m % 2 + 1) * SLOTS]
                    for k in range(KD):
                        mm = three_pass(nc, out, (wh[:, k, cs], wl[:, k, cs]), (xg[0][:, k, :], xg[1][:, k, :]),
                                        k == 0, k == KD - 1, S_.leave if j and k == 0 and m % 2 == 0 else None)
                mm.then_inc(up_ready, 1)
            pe.wait_ge(put_act, e + 1)
            pe.wait_ge(put_dve, e + 1)
            for j in range(N_UP, N_TILES):
                wh, wl = S_.take(pe, e, j)
                pe.wait_ge(hid_ready, e * NC + (j - N_UP + 3))
                for r in range(tile_rows(j)[0]):
                    m = 2 * (j - N_UP) + r
                    for i in range(4):
                        s, cs = slice((i // 2) * P, (i // 2 + 1) * P), slice((i % 2) * BANK, (i % 2 + 1) * BANK)
                        mm = three_pass(nc, ps[:, 4 + i, :], (hid_hi[:, m, s], hid_lo[:, m, s]), (wh[:, r, cs], wl[:, r, cs]),
                                        m == 0, m == FT - 1, S_.leave if r == 0 and i == 0 else None)
                        if m == FT - 1:
                            mm.then_inc(down_ready, 1)
            pe.wait_ge(y_hi, e * 4 + 4)
            pe.wait_ge(y_lo, e * 4 + 4)
            for i in range(2 * NT):
                t, cs = slice((i // 2) * P, (i // 2 + 1) * P), slice((i % 2) * BANK, (i % 2 + 1) * BANK)
                if i >= 4:
                    pe.wait_ge(back_done, e * 8 + (i + 1))
                for n, (s, part) in enumerate((s, part) for s in range(2) for part in range(2)):
                    mm = nc.tensor.matmul(ps[:, 4 + i % 4, :], put[:, s, t], y[part][:, s, cs], start=(n == 0), stop=(n == 3))
                    if i == 0 and n == 0:
                        mm.then_inc(S_.tile_used, 1)
                mm.then_inc(back_ready, 1)

    def scalar(act):
        with act.Fori(0, EXPERTS) as e:
            S_.split_hi(act, e, 0)
            for r in range(2):
                act.wait_ge(gathered, e * 2 + (r + 1))
                nc.scalar.activation(gather_dst(r, 0), gather_view(r, 0), ACT.Copy).then_inc(g_hi, 1)
            S_.split_hi(act, e, 1)
            act.wait_ge(put_ready, e + 1)
            nc.scalar.activation(put[:, 0, :], ps[:, 4, :], ACT.Copy).then_inc(put_act, 1)
            for c in range(NC):
                S_.split_hi(act, e, 2 * c + 2)
                act.wait_ge(up_ready, e * N_UP + (2 * c + 1))
                act.wait_ge(mult_done, e * NC + (c + 1))
                nc.scalar.activation(sig[:, c % 2, 0:pair(c)], ps[:, 2 * (c % 2), 0:pair(c)], ACT.Silu).then_inc(silu_done, 1)
                S_.split_hi(act, e, 2 * c + 3)
            for j in range(N_UP + 2, N_TILES):
                S_.split_hi(act, e, j)
            for i in range(4):
                act.wait_ge(down_ready, e * 4 + (i + 1))
                nc.scalar.activation(y[0][:, i // 2, (i % 2) * BANK:(i % 2 + 1) * BANK], ps[:, 4 + i, :], ACT.Copy
                                     ).then_inc(y_hi, 1)

    def vector(dve):
        def make_pick(e):
            for t in range(NT):
                ins = nc.vector.tensor_scalar(pick[:, t, :], iota, place[:, t, bass.ds(e, 1)], None, ALU.is_equal)
            ins.then_inc(pick_ready, 1)
        dve.sem_inc(S_.tile_used, SPLITS)
        dve.sem_inc(mult_done, 2)
        dve.sem_inc(hid_ready, 2)
        dve.sem_inc(back_done, 4)
        nc.vector.tensor_copy(ident_r, prog.ident)
        for t in range(NT):
            ins = nc.vector.tensor_copy(xt_hi[:, t, :], prog.x_tok[:, t, :])
        ins.then_inc(prepared, 1)
        dve.wait_ge(prepared, 1)
        for t in range(NT):
            ins = nc.vector.tensor_tensor(xt_lo[:, t, :], prog.x_tok[:, t, :], xt_hi[:, t, :].bitcast(F32), ALU.subtract)
        ins.then_inc(prepared, 1)
        dve.wait_ge(iota_landed, 16)
        make_pick(0)
        dve.wait_ge(pick_ready, 1)
        with dve.Fori(0, EXPERTS) as e:
            S_.split_lo(dve, e, 0)
            for r in range(2):
                dve.wait_ge(gathered, e * 2 + (r + 1))
                nc.vector.tensor_copy(gather_dst(r, 1), gather_view(r, 1)).then_inc(g_lo, 1)
            S_.split_lo(dve, e, 1)
            dve.wait_ge(put_ready, e + 1)
            nc.vector.tensor_copy(put[:, 1, :], ps[:, 5, :]).then_inc(put_dve, 1)
            for c in range(NC):
                S_.split_lo(dve, e, 2 * c + 2)
                dve.wait_ge(up_ready, e * N_UP + (2 * c + 2))
                dve.wait_ge(silu_done, e * NC + (c + 1))
                dve.wait_ge(hid_ready, e * NC + (c + 1))
                nc.vector.tensor_tensor(prod[:, c % 2, 0:pair(c)], sig[:, c % 2, 0:pair(c)],
                                        ps[:, 2 * (c % 2) + 1, 0:pair(c)], ALU.mult).then_inc(mult_done, 1)
                S_.split_lo(dve, e, 2 * c + 3)
            for j in range(N_UP + 2, N_TILES):
                S_.split_lo(dve, e, j)
            for i in range(4):
                cs = slice((i % 2) * BANK, (i % 2 + 1) * BANK)
                dve.wait_ge(y_hi, e * 4 + (i + 1))
                nc.vector.tensor_tensor(y[1][:, i // 2, cs], ps[:, 4 + i, :], y[0][:, i // 2, cs].bitcast(F32),
                                        ALU.subtract).then_inc(y_lo, 1)
            make_pick(e + 1)
            dve.wait_ge(acc_ready, 1)
            dve.wait_ge(back_done, e * 8 + 4)
            for i in range(2 * NT):
                t, cs = i // 2, slice((i % 2) * BANK, (i % 2 + 1) * BANK)
                dve.wait_ge(back_ready, e * 8 + (i + 1))
                nc.vector.scalar_tensor_tensor(out=prog.acc[:, t, cs], in0=ps[:, 4 + i % 4, :],
                                               scalar=gates[:, t, bass.ds(e, 1)], in1=prog.acc[:, t, cs],
                                               op0=ALU.mult, op1=ALU.add).then_inc(back_done, 1)

    def gpsimd(pool):
        for b in (hid_hi, hid_lo):
            nc.gpsimd.memset(b[:, :, SLOTS:].bitcast(F32), 0.0)
        for t in range(NT):
            ins = nc.gpsimd.tensor_scalar(prog.acc[:, t, :], prog.x_tok[:, t, :], ALPHA, None, ALU.mult)
        ins.then_inc(acc_ready, 1)
        with pool.Fori(0, EXPERTS) as e:
            for c in range(NC):
                ms = tiles_of_chunk(c)
                dst = [b[:, ms[0]:ms[-1] + 1, 0:SLOTS] for b in (hid_hi, hid_lo)]
                src = prod[:, c % 2, 0:pair(c)].rearrange("p (m n) -> p m n", n=SLOTS)
                pool.wait_ge(mult_done, e * NC + (c + 3))
                nc.gpsimd.tensor_tensor(dst[0], src, prog.ones[:, 0:1].unsqueeze(2).to_broadcast([P, len(ms), SLOTS]), ALU.mult
                                        ).then_inc(hi_ready, 1)
                pool.wait_ge(hi_ready, e * NC + (c + 1))
                nc.gpsimd.tensor_tensor(dst[1], src, dst[0].bitcast(F32), ALU.subtract).then_inc(hid_ready, 1)
    return S_.loads, tensor, scalar, vector, gpsimd


def dense_buffers(prog, own, name):
    def new(n, shape, dt=F32R):
        return own.enter_context(prog.nc.sbuf_tensor(f"{name}_{n}", shape, dt))
    return (new("hid_hi", [P, FT, S]), new("hid_lo", [P, FT, S]),
            new("sig", [P, 2, S], F32), new("prod", [P, 2, S], F32),
            new("w_hi", [P, SPLITS, RING_COLS]), new("w_lo", [P, SPLITS, RING_COLS]))


def dense_ffn(prog, name, w1, w3, w2, parts):
    with ExitStack() as own:
        buf = dense_buffers(prog, own, name)
        with Stage(prog, name) as st:
            loads, tensor, scalar, vector, gpsimd = dense_parts(prog, st, buf, parts, w1, w3, w2, None)
            st.sync(loads)
            st.tensor(tensor)
            st.scalar(scalar)
            st.vector(vector)
            st.gpsimd(gpsimd)


def moe_experts(prog, name, w, gates, place, flag):
    with ExitStack() as own:
        dense_buf = dense_buffers(prog, own, name + "_dense")
    with ExitStack() as own:
        def new(n, shape, dt=F32R):
            return own.enter_context(prog.nc.sbuf_tensor(f"{name}_{n}", shape, dt))
        iota = new("iota", [P, SLOT_PAD], F32)
        buf = (new("xy_hi", [P, 2 * D]), new("xy_lo", [P, 2 * D]),
               new("hid_hi", [P, FT, SLOT_PAD]), new("hid_lo", [P, FT, SLOT_PAD]),
               new("sig", [P, 2, 2 * SLOTS], F32), new("prod", [P, 2, 2 * SLOTS], F32),
               new("w_hi", [P, SPLITS, RING_COLS]), new("w_lo", [P, SPLITS, RING_COLS]),
               new("pick", [P, NT, SLOT_PAD]), new("put", [P, 2, S]), new("ident_r", [P, P])[:, :])
        with Stage(prog, name) as st:
            iota_landed = st.counter("iota_landed")
            sparse = sparse_parts(prog, st, buf, *w, gates, place, iota[:, :], iota_landed)
            dense = dense_parts(prog, st, dense_buf, EXPERTS, *w, gates)

            def either(i):
                def program(eng):
                    fits = eng.value_load(flag[0:1, 0:1], min_val=0, max_val=1)
                    with eng.If(fits > 0):
                        sparse[i](eng)
                    with eng.Else():
                        dense[i](eng)
                return program

            def loads(sp):
                sp.dma_start(iota[:, :], prog.iota_in).then_inc(iota_landed, 16)
                either(0)(sp)
                sp.wait_ge(iota_landed, 16)
            st.sync(loads)
            st.tensor(either(1))
            st.scalar(either(2))
            st.vector(either(3))
            st.gpsimd(either(4))



def router(prog, inp, gates, place, flag):
    nc, ps = prog.nc, prog.ps
    PAD = 2 * EXPERTS
    FILL, TAKEN = -3.0e38, -2.0e38
    with ExitStack() as own:
        w = prog.sbuf("moe_wr", [P, KD, EXPERTS], own)
        w_parts = [own.enter_context(nc.sbuf_tensor(n, [P, KD, EXPERTS], F32R)) for n in ("moe_wr_hi", "moe_wr_lo")]
        bias = prog.sbuf("moe_br", [P, EXPERTS], own)
        logit = prog.sbuf("moe_logit", [P, NT, PAD], own)
        left = prog.sbuf("moe_left", [P, NT, PAD], own)
        top = prog.sbuf("moe_top", [P, NT, 8], own)
        neg = prog.sbuf("moe_neg", [P, NT], own)
        den = prog.sbuf("moe_den", [P, NT], own)
        e = prog.sbuf("moe_e", [P, NT, EXPERTS], own)
        layer_norm(prog, "s5_ln", inp["ln_gb"][2], meanwhile=[(w[:, :, :], inp["moe_wr"]), (bias[:, :], inp["moe_br"])])
        with Stage(prog, "moe_router") as st:
            w_split = st.counter("w_split")
            product, link_sem, neg_ready, exped, chosen, ranked = (
                st.counter(n) for n in ("product", "dve_link", "neg_ready", "exped", "chosen", "ranked"))

            @st.tensor
            def _(pe):
                pe.wait_ge(w_split, 2)
                for t in range(NT):
                    for k in range(KD):
                        m = three_pass(nc, ps[:, t, 0:EXPERTS], [x[:, k, t * P:(t + 1) * P] for x in (prog.x_hi, prog.x_lo)],
                                       (w_parts[0][:, k, :], w_parts[1][:, k, :]), k == 0, k == KD - 1)
                    m.then_inc(product, 1)
                pe.wait_ge(chosen, 1)
                for t in range(NT):
                    for b in range(t + 1):
                        m = nc.tensor.matmul(ps[:, 4, t * EXPERTS:(t + 1) * EXPERTS], prog.tri if b == t else prog.ones,
                                             left[:, b, 0:EXPERTS], start=(b == 0), stop=(b == t))
                m.then_inc(ranked, 1)
                for t in range(NT):
                    m = nc.tensor.matmul(ps[:, 5, 0:EXPERTS], prog.ones, left[:, t, 0:EXPERTS], start=(t == 0), stop=(t == NT - 1))
                m.then_inc(ranked, 1)

            @st.vector
            def _(dve):
                link = linker(dve, link_sem)
                nc.vector.tensor_copy(w_parts[0][:, :, :], w[:, :, :]).then_inc(w_split, 1)
                dve.wait_ge(w_split, 1)
                nc.vector.tensor_tensor(w_parts[1][:, :, :], w[:, :, :], w_parts[0][:, :, :].bitcast(F32), ALU.subtract
                                        ).then_inc(w_split, 1)
                nc.vector.memset(logit[:, :, EXPERTS:], FILL)
                for t in range(NT):
                    dve.wait_ge(product, t + 1)
                    m = nc.vector.tensor_tensor(logit[:, t, 0:EXPERTS], ps[:, t, 0:EXPERTS], bias[:, :], ALU.add)
                link(m)
                for t in range(NT):
                    m = nc.vector.max(top[:, t, :], logit[:, t, 0:EXPERTS])
                link(m)
                nc.vector.tensor_scalar(neg[:, :], top[:, :, 0], -1.0, None, ALU.mult).then_inc(neg_ready, 1)
                link(nc.vector.memset(top[:, :, 2:], FILL))
                for t in range(NT):
                    m = nc.vector.match_replace(left[:, t, :], top[:, t, :], logit[:, t, :], TAKEN)
                link(m)
                nc.vector.tensor_scalar(left[:, :, 0:EXPERTS], left[:, :, 0:EXPERTS], TAKEN, None, ALU.is_equal
                                        ).then_inc(chosen, 1)
                dve.wait_ge(chosen, 1)
                dve.wait_ge(exped, NT)
                link(nc.vector.tensor_tensor(e[:, :, :], e[:, :, :], left[:, :, 0:EXPERTS], ALU.mult))
                link(nc.vector.tensor_reduce(den[:, :], e[:, :, :], AX_X, ALU.add))
                link(nc.vector.reciprocal(den[:, :], den[:, :]))
                nc.vector.tensor_tensor(gates, e[:, :, :], den[:, :].unsqueeze(2).to_broadcast([P, NT, EXPERTS]),
                                        ALU.mult)
                dve.wait_ge(ranked, 2)
                link(nc.vector.memset(place[:, :, EXPERTS:], -1.0))
                pl = place[:, :, 0:EXPERTS]
                link(nc.vector.tensor_tensor(pl, ps[:, 4, 0:NT * EXPERTS].rearrange("p (t n) -> p t n", n=EXPERTS),
                                             left[:, :, 0:EXPERTS], ALU.mult))
                link(nc.vector.tensor_scalar(pl, pl, 1.0, None, ALU.subtract))
                link(nc.vector.tensor_reduce(den[:, 0:1], ps[:, 5, 0:EXPERTS], AX_X, ALU.max))
                nc.vector.tensor_scalar(flag[:, :], den[:, 0:1], SLOTS + 0.5, None, ALU.is_lt)

            @st.scalar
            def _(act):
                act.wait_ge(neg_ready, 1)
                for t in range(NT):
                    nc.scalar.activation(e[:, t, :], logit[:, t, 0:EXPERTS], ACT.Exp, bias=neg[:, t:t + 1]).then_inc(exped, 1)


def moe_layer(prog, inp):
    with ExitStack() as own:
        gates, place = (prog.sbuf(n, [P, NT, EXPERTS + 1], own) for n in ("moe_gates", "moe_place"))
        flag = own.enter_context(prog.nc.sbuf_tensor("moe_fits", [P, 1], I32))
        router(prog, inp, gates[:, :, 0:EXPERTS], place, flag)
        moe_experts(prog, "moe", (inp["moe_w1"][0], inp["moe_w3"][0], inp["moe_w2"][0]), gates, place, flag)



NEG = -1.0e30
A_HEADS, A_NOPE, A_ROPE, A_V = 6, 64, 32, 64
Q_LORA, KV_LORA = 768, 256
B_HEADS, C_HEADS, HD = 6, 4, 64
IDX_HEADS, IDX_DIM = 8, 64
TOPK = min(256, S // 4)
ROPE_THETA = 10000.0
DILATED = ((128, 1), (512, 4), (2048, 16))
A_SCALE, BC_SCALE = (A_NOPE + A_ROPE) ** -0.5, HD ** -0.5
SPLIT = (Q_LORA, KV_LORA, A_ROPE, B_HEADS * HD, B_HEADS * HD, B_HEADS * HD, C_HEADS * HD, C_HEADS * HD, C_HEADS * HD,
         IDX_HEADS * IDX_DIM, IDX_DIM, IDX_HEADS, D)
AT = [sum(SPLIT[:i]) for i in range(len(SPLIT) + 1)]
N_BIAS = 1 + B_HEADS + C_HEADS


def attention_constants():
    dist = np.arange(P)[:, None] + (S - P) - np.arange(S)[None, :]
    causal = np.where(dist >= 0, 0.0, NEG)
    slopes = 2.0 ** (-8.0 * np.arange(1, B_HEADS + C_HEADS + 1) / (B_HEADS + C_HEADS))
    count = sum(((dist >= 0) & (dist <= w) & (dist % d == 0)).astype(np.float64) for w, d in DILATED)
    windows = np.where(count > 0, np.log(np.maximum(count, 1)), NEG)
    tables = [causal / A_SCALE]
    tables += [(windows - s * dist * (count > 0)) / BC_SCALE for s in slopes[:B_HEADS]]
    tables += [(causal - s * dist * (dist >= 0)) / BC_SCALE for s in slopes[B_HEADS:]]
    half = A_ROPE // 2
    freqs = ROPE_THETA ** (-np.arange(0, A_ROPE, 2) / A_ROPE)
    angle = (np.arange(S, dtype=np.float32)[None, :] * np.tile(freqs, 2).astype(np.float32)[:, None]).astype(np.float32)
    rot = np.zeros((A_ROPE, A_ROPE))
    for m in range(half):
        rot[m + half, m] = -1.0
        rot[m, m + half] = 1.0
    rope = np.zeros((P, 2 * S + A_ROPE))
    rope[A_NOPE:A_NOPE + A_ROPE] = np.concatenate([np.cos(angle), np.sin(angle), rot], axis=1)
    return np.stack(tables, axis=1).astype(np.float32), rope.astype(np.float32)


def in_columns():
    names = ("cq", "ckv", "kr", "qb", "kb", "vb", "qc", "kc", "vc", "qi", "ki", "wi", "gate")
    order = ("cq", "ckv", "kr", "qb", "kb", "qc", "kc", "qi", "ki", "vb", "vc", "wi", "gate")
    out = []
    for n in order:
        a, b = AT[names.index(n)], AT[names.index(n) + 1]
        if n == "kr":
            out.append((n, 0, a - A_NOPE, a - A_NOPE + P))
        elif n == "ki":
            out.append((n, 0, a - IDX_DIM, a - IDX_DIM + P + IDX_DIM))
        else:
            out += [(n, c - a, c, min(c + UP_COLS, b)) for c in range(a, b, UP_COLS)]
    return out


def plan_attention(W, inp, l):
    w_in = inp["w_in_2"][l]
    W.plan(f"in{l}", [w_in[:, c0:c1].rearrange("(k p) n -> p k n", p=P) for _, _, c0, c1 in in_columns()])
    W.plan(f"uq{l}", col_tiles(inp["w_uq_2"][l], 3 * (A_NOPE + A_ROPE)))
    W.plan(f"ukv{l}", col_tiles(inp["w_uk_2"][l], A_HEADS * A_NOPE) + col_tiles(inp["w_uv_2"][l], A_HEADS * A_V))
    W.plan(f"att_out{l}", row_tiles(inp["w_out_2"][l]))


def modulation(prog, name, l, gate, meanwhile):
    nc, ps, mods = prog.nc, prog.ps, prog.mods
    with Stage(prog, name) as st:
        modulated, hi_done, spread = st.counter("modulated"), st.counter("hi_done"), st.counter("spread")
        load_meanwhile(st, meanwhile)

        @st.scalar
        def _(act):
            for k in range(KD):
                act.wait_ge(modulated, k + 1)
                nc.scalar.activation(prog.x_lo[:, k, :], prog.x_feat[:, k, :], ACT.Copy).then_inc(hi_done, 1)
            for h in range(2):
                act.wait_ge(spread, h + 1)
                nc.scalar.activation(gate[:, h * BANK:(h + 1) * BANK], ps[:, h, :], ACT.Copy)

        @st.tensor
        def _(pe):
            for n in range(KD):
                m = nc.tensor.matmul(ps[:, n // 4, (n % 4) * P:(n % 4 + 1) * P],
                                     bc(mods[:, l, 2 * KD + n:2 * KD + n + 1], [P, P]), prog.ident, start=True, stop=True)
                if n % 4 == 3:
                    m.then_inc(spread, 1)

        @st.vector
        def _(dve):
            for k in range(KD + 1):
                if k < KD:
                    nc.vector.tensor_scalar(prog.x_feat[:, k, :], prog.x_feat[:, k, :], mods[:, l, KD + k:KD + k + 1],
                                            mods[:, l, k:k + 1], ALU.mult, ALU.add).then_inc(modulated, 1)
                if k:
                    dve.wait_ge(hi_done, k)
                    nc.vector.tensor_tensor(prog.x_hi[:, k - 1, :], prog.x_feat[:, k - 1, :],
                                            prog.x_lo[:, k - 1, :].bitcast(F32), ALU.subtract)


def latent_norms(prog, name, c_all, g):
    nc, ps = prog.nc, prog.ps
    nq = Q_LORA // P
    sq, rs = (prog.scratch[:, i * 2 * S:(i + 1) * 2 * S].rearrange("p (a n) -> p a n", a=2) for i in range(2))
    with Stage(prog, name) as st:
        squared = [st.counter(f"squared_{i}") for i in range(2)]
        summed = st.counter("summed")
        rooted, link_sem = st.counter("rooted"), st.counter("dve_link")

        @st.gpsimd
        def _(pool):
            for k in range(1, KD, 2):
                if k >= 2:
                    pool.wait_ge(summed, k - 1)
                nc.gpsimd.tensor_tensor(sq[:, 1, :], c_all[:, k, :], c_all[:, k, :], ALU.mult).then_inc(squared[1], 1)

        @st.tensor
        def _(pe):
            for k in range(KD):
                pe.wait_ge(squared[k % 2], k // 2 + 1)
                nc.tensor.matmul(ps[:, int(k >= nq), :], prog.ones, sq[:, k % 2, :], start=k in (0, nq),
                                 stop=k in (nq - 1, KD - 1)).then_inc(summed, 1)

        @st.scalar
        def _(act):
            for k in range(0, KD, 2):
                if k >= 2:
                    act.wait_ge(summed, k - 1)
                nc.scalar.activation(sq[:, 0, :], c_all[:, k, :], ACT.Square).then_inc(squared[0], 1)
            for i, (k, n) in enumerate(((nq, Q_LORA), (KD, KV_LORA))):
                act.wait_ge(summed, k)
                nc.scalar.activation(rs[:, i, :], ps[:, i, :], ACT.Sqrt, scale=1.0 / n, bias=prog.eps_norm
                                     ).then_inc(rooted, 1)

        @st.vector
        def _(dve):
            link = linker(dve, link_sem)
            for i, ks in enumerate((range(nq), range(nq, KD))):
                dve.wait_ge(rooted, i + 1)
                link(nc.vector.reciprocal(rs[:, i, :], rs[:, i, :]))
                dve.wait_ge(summed, ks[-1] + 1)
                for k in ks:
                    nc.vector.scalar_tensor_tensor(out=c_all[:, k, :], in0=c_all[:, k, :], scalar=g[:, k:k + 1],
                                                   in1=rs[:, i, :], op0=ALU.mult, op1=ALU.mult)


class Selection:
    TAKEN = -3.0e38
    TILES = range(1, NT)
    ROUNDS = TOPK // 8

    def __init__(self, prog, mem, top):
        self.nc, self.top = prog.nc, top
        self.sel = mem[:, 0:NT * S].rearrange("p (t n) -> p t n", n=S)
        at, self.scores = NT * S, {}
        for t in self.TILES:
            self.scores[t] = mem[:, at:at + (t + 1) * P]
            at += (t + 1) * P
        self.spare = mem[:, at:at + S]

    def round(self, link, n):
        if n >= len(self.TILES) * self.ROUNDS:
            return
        nc, t, r = self.nc, self.TILES[n // self.ROUNDS], n % self.ROUNDS
        x, y = self.scores[t], self.spare[:, 0:(t + 1) * P]
        if r % 2:
            x, y = y, x
        link(nc.vector.max(self.top, x))
        link(nc.vector.match_replace(y, self.top, x, self.TAKEN))
        if r == self.ROUNDS - 1:
            link(nc.vector.tensor_scalar(self.sel[:, t, 0:(t + 1) * P], y, self.TAKEN / 2, NEG, ALU.is_gt, ALU.mult))


def index_scores(prog, name, qi, ki, wi, causal, scores, rope, qa, ka):
    nc, ps = prog.nc, prog.ps
    tmp, relu = (prog.scratch[:, i * 2 * S:(i + 1) * 2 * S].rearrange("p (a n) -> p a n", a=2) for i in range(2))
    rows = slice(A_NOPE, A_NOPE + A_ROPE)
    cos, sin, rot = rope[rows, 0:S], rope[rows, S:2 * S], rope[rows, 2 * S:]
    xs = [ka[rows, 0, :]] + [qa[rows, h, :] for h in range(A_HEADS)]
    units = [(t, i) for t in Selection.TILES for i in range(IDX_HEADS)]
    SCORE_BANKS = 6
    PER = len(units) // len(xs)
    with Stage(prog, name) as st:
        product, relued, summed = st.counter("product"), st.counter("relued"), st.counter("summed")
        turned, cosined, sined, rotated = (st.counter(n) for n in ("turned", "cosined", "sined", "rotated"))
        link_sem = st.counter("dve_link")

        @st.tensor
        def _(pe):
            for n, (t, i) in enumerate(units):
                r, at = divmod(n, PER)
                if at == 0 and r < len(xs):
                    if r >= 2:
                        pe.wait_ge(sined, r - 1)
                    nc.tensor.matmul(ps[rows, SCORE_BANKS + r % 2, :], rot, xs[r], start=True, stop=True).then_inc(turned, 1)
                half = slice((i % 2) * IDX_DIM, (i % 2 + 1) * IDX_DIM)
                if n >= SCORE_BANKS:
                    pe.wait_ge(relued, n - SCORE_BANKS + 1)
                nc.tensor.matmul(ps[:, n % SCORE_BANKS, 0:(t + 1) * P], qi[half, i // 2, t * P:(t + 1) * P],
                                 ki[half, 0:(t + 1) * P], start=True, stop=True).then_inc(product, 1)

        @st.scalar
        def _(act):
            for n, (t, i) in enumerate(units):
                act.wait_ge(product, n + 1)
                if n >= 2:
                    act.wait_ge(summed, n - 1)
                nc.scalar.activation(relu[:, n % 2, 0:(t + 1) * P], ps[:, n % SCORE_BANKS, 0:(t + 1) * P], ACT.Relu,
                                     scale=IDX_DIM ** -0.5).then_inc(relued, 1)
            act.wait_ge(rotated, 1)
            for h in range(1, A_HEADS):
                nc.scalar.activation(ka[rows, h, :], ka[rows, 0, :], ACT.Copy)

        @st.gpsimd
        def _(pool):
            for r, x in enumerate(xs):
                pool.wait_ge(turned, r + 1)
                nc.gpsimd.tensor_tensor(x, x, cos, ALU.mult).then_inc(cosined, 1)

        @st.vector
        def _(dve):
            def rotate(r):
                dve.wait_ge(turned, r + 1)
                if r >= 2:
                    dve.wait_ge(rotated, r - 1)
                nc.vector.tensor_tensor(tmp[rows, r % 2, :], ps[rows, SCORE_BANKS + r % 2, :], sin, ALU.mult).then_inc(sined, 1)
                dve.wait_ge(sined, r + 1)
                dve.wait_ge(cosined, r + 1)
                nc.vector.tensor_tensor(xs[r], xs[r], tmp[rows, r % 2, :], ALU.add).then_inc(rotated, 1)
            linker(dve, link_sem)(nc.vector.tensor_scalar(wi[:, :, :], wi[:, :, :], IDX_HEADS ** -0.5, None, ALU.mult))
            for n, (t, i) in enumerate(units):
                w = (t + 1) * P
                x = scores[t]
                dve.wait_ge(relued, n + 1)
                if n:
                    dve.wait_ge(summed, n)
                nc.vector.scalar_tensor_tensor(out=x, in0=relu[:, n % 2, 0:w], scalar=wi[:, t, i:i + 1],
                                               in1=causal[:, S - w:S] if i == 0 else x, op0=ALU.mult, op1=ALU.add
                                               ).then_inc(summed, 1)
                r, at = divmod(n, PER)
                if at == PER - 1 and r < len(xs):
                    rotate(r)


BIAS_PARTS = ((0, 1), (1, 4), (4, 1 + B_HEADS), (1 + B_HEADS, N_BIAS))


def attend(prog, name, heads, bias, bias_src, choice, gate, y):
    nc, ps = prog.nc, prog.ps
    units = [(h, t) for h in range(len(heads)) for t in range(NT)]
    U = len(units)
    sel = choice.sel
    free_units = sum(not heads[h][5] for h, _ in units)
    rounds = -(-len(Selection.TILES) * Selection.ROUNDS // free_units)
    with ExitStack() as own:
        s_sb = prog.x_feat[:, 0:3, :]
        p_t = prog.x_feat[:, 3:5, :]
        small = prog.sbuf(name + "_small", [P, 4, 4], own)
        with Stage(prog, name) as st:
            s_ready, s_read, neg_ready, p_ready, pt_ready, pt_copied, o_ready, o_read, link_sem, p_read = (
                st.counter(n) for n in ("s_ready", "s_read", "neg_ready", "p_ready", "pt_ready", "pt_copied",
                                       "o_ready", "o_read", "dve_link", "p_read"))

            bias_landed = [st.counter(f"bias_landed_{i}") for i in range(len(BIAS_PARTS))]

            @st.sync
            def _(sp):
                for landed, (a, b) in zip(bias_landed, BIAS_PARTS):
                    sp.dma_start(bias[:, a:b, :], bias_src[:, a:b, :]).then_inc(landed, 16)

            def keys(u):
                return (units[u][1] + 1) * P

            @st.tensor
            def _(pe):
                def scores(u):
                    h, t = units[u]
                    q, k = heads[h][0], heads[h][1]
                    if u >= 3:
                        pe.wait_ge(s_read, u - 2)
                    nc.tensor.matmul(ps[:, u % 3, 0:keys(u)], q(t * P, (t + 1) * P), k(0, keys(u)), start=True, stop=True
                                     ).then_inc(s_ready, 1)

                def turn(u):
                    pe.wait_ge(p_ready, u + 1)
                    if u >= 2:
                        pe.wait_ge(pt_copied, u - 1)
                    for b in range(keys(u) // P):
                        m = nc.tensor.transpose(ps[:, 3 + u % 2, b * P:(b + 1) * P], s_sb[:, u % 3, b * P:(b + 1) * P],
                                                prog.ident)
                    m.then_inc(pt_ready, 1)

                def values(u):
                    pe.wait_ge(pt_copied, u + 1)
                    if u >= 2:
                        pe.wait_ge(o_read, u - 1)
                    v = heads[units[u][0]][2]
                    nb = keys(u) // P
                    for b in range(nb):
                        m = nc.tensor.matmul(ps[:, 5 + u % 2, 0:HD], p_t[:, u % 2, b * P:(b + 1) * P], v(b),
                                             start=(b == 0), stop=(b == nb - 1))
                    m.then_inc(o_ready, 1)
                for step in range(U + 2):
                    if step < U:
                        scores(step)
                    if 1 <= step <= U:
                        turn(step - 1)
                    if step >= 2:
                        values(step - 2)

            @st.vector
            def _(dve):
                link = linker(dve, link_sem)

                def read_scores(u):
                    h, t = units[u]
                    w, scale, selected = keys(u), heads[h][3], heads[h][5]
                    x, mx, neg = s_sb[:, u % 3, 0:w], small[:, u % 4, 0:1], small[:, u % 4, 1:2]
                    table = bias[:, heads[h][4], S - w:S]
                    for landed, (a, _) in zip(bias_landed, BIAS_PARTS):
                        if a == heads[h][4] and t == 0:
                            dve.wait_ge(landed, 16)
                    dve.wait_ge(s_ready, u + 1)
                    if u >= 3:
                        dve.wait_ge(pt_ready, u - 2)
                    if u >= 4:
                        dve.wait_ge(o_read, u - 3)
                    if selected and t > 0:
                        nc.vector.tensor_tensor(x, ps[:, u % 3, 0:w], table, ALU.add).then_inc(s_read, 1)
                        dve.wait_ge(s_read, u + 1)
                        link(nc.vector.tensor_tensor_reduce(out=x, in0=x, in1=sel[:, t, 0:w], scale=1.0, scalar=-3.0e38,
                                                            op0=ALU.add, op1=ALU.max, accum_out=mx))
                    else:
                        nc.vector.tensor_tensor_reduce(out=x, in0=ps[:, u % 3, 0:w], in1=table, scale=1.0, scalar=-3.0e38,
                                                       op0=ALU.add, op1=ALU.max, accum_out=mx).then_inc(s_read, 1)
                        dve.wait_ge(s_read, u + 1)
                    nc.vector.tensor_scalar(neg, mx, -scale, None, ALU.mult).then_inc(neg_ready, 1)

                def output(u):
                    h, t = units[u]
                    den, inv = small[:, u % 4, 2:3], small[:, u % 4, 3:4]
                    cs = slice(h * HD, (h + 1) * HD)
                    dve.wait_ge(p_ready, u + 1)
                    link(nc.vector.reciprocal(inv, den))
                    dve.wait_ge(o_ready, u + 1)
                    nc.vector.scalar_tensor_tensor(out=y[:, t, cs], in0=ps[:, 5 + u % 2, 0:HD], scalar=inv,
                                                   in1=gate[:, t, cs], op0=ALU.mult, op1=ALU.mult).then_inc(o_read, 1)
                for step in range(U + 2):
                    if step < U:
                        read_scores(step)
                    for r in range(rounds // 2):
                        choice.round(link, step * rounds + r)
                    if step >= 2:
                        output(step - 2)
                    for r in range(rounds // 2, rounds):
                        choice.round(link, step * rounds + r)

            @st.scalar
            def _(act):
                for step in range(U + 1):
                    if step < U:
                        u = step
                        x = s_sb[:, u % 3, 0:keys(u)]
                        act.wait_ge(neg_ready, u + 1)
                        nc.scalar.activation(x, x, ACT.Exp, bias=small[:, u % 4, 1:2], scale=heads[units[u][0]][3],
                                             accum_out=small[:, u % 4, 2:3]).then_inc(p_ready, 1)
                    if step >= 1:
                        u = step - 1
                        act.wait_ge(pt_ready, u + 1)
                        if u >= 2:
                            act.wait_ge(o_ready, u - 1)
                        nc.scalar.activation(p_t[:, u % 2, 0:keys(u)], ps[:, 3 + u % 2, 0:keys(u)], ACT.Copy
                                             ).then_inc(pt_copied, 1)


def attention_layer(prog, inp, l, last):
    def new(name, shape, c):
        return prog.sbuf(f"{name}_{l}", shape, c)
    with ExitStack() as own:
        mod_gate = new("mod_gate", [P, D], own)
        with ExitStack() as heads_ctx:
            qa, ka = new("qa", [P, A_HEADS, S], heads_ctx), new("ka", [P, A_HEADS, S], heads_ctx)
            va, vb = new("va", [P, NT, A_HEADS * A_V], heads_ctx), new("vb", [P, NT, B_HEADS * HD], heads_ctx)
            vc = new("vc", [P, NT, C_HEADS * HD], heads_ctx)
            qb, kb = (new(n, [P, B_HEADS // 2, S], heads_ctx) for n in ("qb", "kb"))
            qc, kc = (new(n, [P, C_HEADS // 2, S], heads_ctx) for n in ("qc", "kc"))
            gate = new("gate", [P, NT, D], heads_ctx)
            choice = Selection(prog, prog.x_free.rearrange("p k n -> p (k n)"), new("top", [P, 8], heads_ctx)[:, :])
            with ExitStack() as early:
                c_all = new("c_all", [P, KD, S], early)
                qi, ki = new("qi", [P, IDX_HEADS // 2, S], early), new("ki", [P, S], early)
                wi, g = new("wi", [P, NT, IDX_HEADS], early), new("lat_g", [P, KD], early)
                modulation(prog, f"mod{l}", l, mod_gate, [(g[:, :], inp["lat_g"][l])])
                feat = {"cq": c_all, "ckv": c_all[:, Q_LORA // P:, :], "qb": qb, "kb": kb, "qc": qc, "kc": kc, "qi": qi}
                groups = []
                for i, (part, at, c0, c1) in enumerate(in_columns()):
                    n = c1 - c0
                    if part in feat:
                        groups += [(i, c, P, None, slice(0, P), feat[part][:, (at + c) // P, :], None) for c in range(0, n, P)]
                    elif part == "kr":
                        rows = slice(A_NOPE, A_NOPE + A_ROPE)
                        groups.append((i, 0, P, None, rows, ka[rows, 0, :], None))
                    elif part == "ki":
                        for c, r in ((0, IDX_DIM), (IDX_DIM, 0)):
                            rows = slice(r, r + IDX_DIM)
                            groups.append((i, c, P, None, rows, ki[rows, :], None))
                    else:
                        dst, func = {"vb": (vb, None), "vc": (vc, None), "wi": (wi, None), "gate": (gate, ACT.Silu)}[part]
                        groups += [(i, 0, n, t, None, dst[:, t, at:at + n], func) for t in range(NT)]
                project(prog, f"in{l}", [prog.x_lo, prog.x_hi], groups, prog.split_scratch)
                latent_norms(prog, f"lat{l}", c_all, g)
                project(prog, f"uq{l}", [c_all[:, 0:Q_LORA // P, :]],
                        [(h // 3, (h % 3) * (A_NOPE + A_ROPE), A_NOPE + A_ROPE, None, slice(0, A_NOPE + A_ROPE), qa[0:A_NOPE + A_ROPE, h, :], None)
                         for h in range(A_HEADS)])
                rope, causal = prog.scratch[:, 4 * S:6 * S + A_ROPE], prog.scratch[:, 7 * S:8 * S]
                project(prog, f"ukv{l}", [c_all[:, Q_LORA // P:, :]],
                        [(0, h * A_NOPE, A_NOPE, None, slice(0, A_NOPE), ka[0:A_NOPE, h, :], None) for h in range(A_HEADS)]
                        + [(1, 0, A_HEADS * A_V, t, None, va[:, t, :], None) for t in range(NT)],
                        meanwhile=[(rope, inp["rope"]), (causal, inp["bias"][:, 0, :])])
                index_scores(prog, f"index{l}", qi, ki, wi, causal, choice.scores, rope, qa, ka)
            with ExitStack() as late:
                bias = new("bias", [P, N_BIAS, S], late)
                def cols(x, rows, h):
                    return lambda a, b: x[rows, h, a:b]

                def vals(x, h):
                    return lambda b: x[:, b, h * HD:(h + 1) * HD]
                full = slice(0, A_NOPE + A_ROPE)
                heads = [(cols(qa, full, h), cols(ka, full, h), vals(va, h), A_SCALE, 0, False) for h in range(A_HEADS)]
                for q, k, v, n, b0, s in ((qb, kb, vb, B_HEADS, 1, False), (qc, kc, vc, C_HEADS, 1 + B_HEADS, True)):
                    for h in range(n):
                        rows = slice((h % 2) * HD, (h % 2 + 1) * HD)
                        heads.append((cols(q, rows, h // 2), cols(k, rows, h // 2), vals(v, h), BC_SCALE, b0 + h, s))
                attend(prog, f"attend{l}", heads, bias, inp["bias"], choice, gate, prog.acc)
        turn_split(prog, f"att_turn{l}", [([prog.acc[:, t, k * P:(k + 1) * P] for t in range(NT)],
                                           prog.x_hi[:, k, :], prog.x_lo[:, k, :]) for k in range(KD)])
        down_project(prog, f"att_out{l}", (prog.x_hi, prog.x_lo), mod_gate)
        layer_norm(prog, f"att_ln{l}", inp["ln_gb"][4 + l], last, split=False)


BIG = ["x", "gdn_w_in", "gdn_w_out", "ffn_w1", "ffn_w3", "ffn_w2", "s5_w_in", "s5_w_glu", "moe_w1", "moe_w3", "moe_w2",
       "w_ada_2", "w_in_2", "w_uq_2", "w_uk_2", "w_uv_2", "w_out_2"]


def plan_rest(prog, W, inp):
    W.plan("s5_u", col_tiles(inp["s5_w_in"][0], UP_COLS))
    W.plan("s5_scan", [t for l in range(DEPTH) for t in col_tiles(inp["w_ada_2"][l], UP_COLS)])
    prog.mods = prog.sbuf("mods", [P, DEPTH, 3 * KD])[:, :, :]
    prog.ada_par = prog.sbuf("ada_par", [P, DEPTH, 4 * KD])[:, :, :]
    prog.ada_junk = prog.sbuf("ada_junk", [P, P])[:, :]
    glu = col_tiles(inp["s5_w_glu"][0], UP_COLS)
    W.plan("s5_glu", [t for pair in zip(glu[:D // UP_COLS], glu[D // UP_COLS:]) for t in pair])
    W.hold("moe")
    prog.iota_in = inp["iota"]
    for l in range(DEPTH):
        plan_attention(W, inp, l)
    prog.u_dram = prog.nc.dram_tensor("u_turn", (KD, P, S), F32).ap()


def rest_steps(prog, inp):
    return [lambda: s5_layer(prog, inp),
            lambda: moe_layer(prog, inp),
            lambda: layer_norm(prog, "moe_ln", inp["ln_gb"][3], split=False),
            lambda: attention_layer(prog, inp, 0, False),
            lambda: attention_layer(prog, inp, 1, True)]


def lay_out_rest(f, arr, rep):
    def lanes(a):
        a = a.reshape((2, PAIRS, GP) + a.shape[2:])
        return np.moveaxis(a, 1, 2).reshape((P, PAIRS) + a.shape[3:])
    vec = [lanes(f["s5_lam_re"][0]), lanes(f["s5_lam_im"][0]),
           lanes(np.broadcast_to(f["s5_log_dt"][0][:, None], (GROUPS, GP)))]
    arr["s5_par"] = np.concatenate([f["s5_d"][0].reshape(KD, P).T] + vec + [rep(np.arange(STEP + 1, dtype=np.float32))], axis=1)
    arr["s5_bc"] = np.stack([lanes(f["s5_b_re"][0]), lanes(f["s5_b_im"][0]),
                             lanes(f["s5_c_re"][0].transpose(0, 2, 1)), lanes(f["s5_c_im"][0].transpose(0, 2, 1))], axis=1)
    arr["moe_wr"] = f["moe_w_router"][0].reshape(KD, P, EXPERTS).transpose(1, 0, 2)
    arr["iota"] = rep(np.arange(SLOT_PAD, dtype=np.float32))
    arr["moe_br"] = rep(f["moe_b_router"][0])

    def feat(a):
        return a.reshape(-1, P).T
    arr["ada_par"] = np.stack([np.concatenate([feat(f["c_2"][0]), feat(f["b_ada_2"][l])], axis=1)
                               for l in range(DEPTH)], axis=1)
    arr["lat_g"] = np.stack([np.concatenate([feat(f["q_norm_g_2"][l]), feat(f["kv_norm_g_2"][l])], axis=1)
                             for l in range(DEPTH)])
    arr["bias"], arr["rope"] = attention_constants()



def constants():
    i = np.arange(P)
    ident = np.eye(P)
    ones = np.ones((P, P))
    tri = (i[:, None] <= i[None, :]) * 1.0
    levels = []
    for level in range(LEVELS):
        b = 1 << level
        s, c = i[:, None], i[None, :]
        levels.append((s // (2 * b) == c // (2 * b)) & (s % (2 * b) < b) & (c % (2 * b) >= b))
    pick_row = np.zeros((P, PICK_ROW))
    pick_row[:, PICK_ROW // 2] = 1.0
    return np.concatenate([ident, ones, tri] + [m * 1.0 for m in levels] + [pick_row], axis=1).astype(np.float32)


def build(nc, inp, out):
    with ExitStack() as ctx:
        prog = Program(nc, ctx)
        prog.out = out
        prog.ps = ctx.enter_context(nc.psum_tensor("ps", [P, 8, BANK], F32))
        def twins(name, shape):
            with ExitStack() as first:
                plain = prog.sbuf(name, shape, first)
            return plain, ctx.enter_context(nc.sbuf_tensor(name + "_r", shape, F32R))
        ring, ring_r = twins("ring", [P, RING, RING_COLS])
        loaded = [ctx.enter_context(nc.semaphore(f"weights_loaded_{i}")) for i in range(RING)]
        used = ctx.enter_context(nc.semaphore("weights_used"))
        W = prog.weights = Weights(ring, ring_r, loaded, used)
        prog.x_tok = prog.sbuf("x_tok", [P, NT, D])
        (prog.x_feat, prog.x_hi), (prog.x_free, prog.x_lo) = (
            (a[:, :, :], b[:, :, :]) for a, b in (twins(n, [P, KD, S]) for n in ("x_feat", "x_free")))
        prog.acc, acc_r = twins("acc", [P, NT, D])
        prog.split_scratch = acc_r[:, :, :].rearrange("p t n -> p (t n)").rearrange("p (a n) -> p a n", a=2)
        prog.scratch = prog.acc[:, :, :].rearrange("p t n -> p (t n)")
        cst = prog.sbuf("cst", [P, 3 * P])
        prog.ident, prog.ones, prog.tri = (cst[:, i * P:(i + 1) * P] for i in range(3))
        eps = prog.sbuf("eps", [P, 2])
        prog.eps_norm, prog.eps_qk = eps[:, 0:1], eps[:, 1:2]

        w_in = inp["gdn_w_in"][0]
        QKV = 3 * HEADS * P
        W.plan("gdn_conv", col_tiles(w_in[:, 0:QKV], UP_COLS))
        W.plan("gdn_ba", col_tiles(w_in[:, QKV + D:QKV + D + 2 * HEADS], UP_COLS))
        W.plan("gdn_z", col_tiles(w_in[:, QKV:QKV + D], UP_COLS))
        W.plan("gdn_out", row_tiles(inp["gdn_w_out"][0]))

        ffn1, ffn3 = (inp[n][0].rearrange("k (e n) -> e k n", n=FF_PART) for n in ("ffn_w1", "ffn_w3"))
        ffn2 = inp["ffn_w2"][0].rearrange("(e k) n -> e k n", k=FF_PART)
        W.hold("ffn")
        plan_rest(prog, W, inp)

        with Stage(prog, "setup") as st:
            landed, eps_set = st.counter("landed"), st.counter("eps_set")

            @st.sync
            def _(sp):
                sp.dma_start(prog.x_tok[:, :, :], inp["x"][0].rearrange("(t p) n -> p t n", p=P)).then_inc(landed, 16)
                sp.dma_start(cst[:, :], inp["cst"][:, 0:3 * P]).then_inc(landed, 16)
                sp.wait_ge(landed, 32)

            @st.gpsimd
            def _(pool):
                nc.gpsimd.memset(eps[:, 0:1], NORM_EPS)
                nc.gpsimd.memset(eps[:, 1:2], NORM_EPS * P)

        steps = [
            lambda: gdn_layer(prog, inp),
            lambda: layer_norm(prog, "gdn_ln", inp["ln_gb"][0]),
            lambda: dense_ffn(prog, "ffn", ffn1, ffn3, ffn2, 2),
        ] + rest_steps(prog, inp)
        for step in steps:
            step()



def lay_out(inputs):
    f = {n: np.ascontiguousarray(np.asarray(a)) for n, a in inputs.items()}
    arr = {n: f[n] for n in BIG}

    def rep(a):
        return np.broadcast_to(a, (P,) + a.shape)
    taps = f["gdn_conv_w"][0].T.reshape(3 * HEADS, P, 4).transpose(1, 0, 2).reshape(P, -1)
    arr["gdn_taps"] = taps
    arr["gdn_par"] = rep(np.concatenate([f["gdn_dt_bias"][0], f["gdn_a_log"][0], f["gdn_norm_g"][0]]))
    gb = np.stack([f["ln_g"].reshape(4, D), f["ln_b"].reshape(4, D)], axis=1)
    gb2 = np.stack([f["ln_g_2"], f["ln_b_2"]], axis=1)
    arr["ln_gb"] = np.stack([rep(a) for a in np.concatenate([gb, gb2])])
    arr["cst"] = constants()
    lay_out_rest(f, arr, rep)
    return {n: np.ascontiguousarray(a) for n, a in arr.items()}


def kernel(**inputs):
    import concourse.bacc as bacc
    from concourse.bass_utils import run_bass_kernel_spmd

    nc = bacc.Bacc("TRN2", target_bir_lowering=False, num_devices=1)
    arrays = {f"in_{n}": a for n, a in lay_out(inputs).items()}
    inp = {n[3:]: nc.dram_tensor(n, a.shape, F32, kind="ExternalInput").ap() for n, a in arrays.items()}
    out = nc.dram_tensor("out_0", (S, D), F32, kind="ExternalOutput").ap()
    build(nc, inp, out)
    r = run_bass_kernel_spmd(nc, [arrays], core_ids=[0])
    return r.results[0]["out_0"].reshape(1, S, D)
```
